# Optimizing a Trainium2 kernel written in Bass

```python
import numpy as np
import jax
import jax.numpy as jnp
from jax import lax
import jax, jax.numpy as jnp

D_MODEL = 2048
BATCH = 1
SEQ = 256
DEPTH = 2

N_MIXERS = 4
HEAD_DIM = 128
GROUP_WIDTH = D_MODEL // N_MIXERS
MIX_WIDTH = N_MIXERS * GROUP_WIDTH
N_HEADS = GROUP_WIDTH // HEAD_DIM
Q_BLOCK = 128
ROPE_THETA = 10000.0
RMS_EPS = 1e-6
NEG_INF = -1e30

CMP_LEN = 32
CMP_STRIDE = 16
CMP_HIDDEN = HEAD_DIM
SEL_LEN = 64
SEL_TOPN = 16
WINDOW = 512
FORCED_BONUS = 1e6

MLA_Q_RANK = 384
MLA_KV_RANK = 128
MLA_NOPE = 128
MLA_ROPE = 64
MLA_V = 128

IN_SPLITS = (
    ("sb_q", GROUP_WIDTH), ("sb_k", GROUP_WIDTH), ("sb_v", GROUP_WIDTH), ("sb_gate", GROUP_WIDTH),
    ("nsa_q", GROUP_WIDTH), ("nsa_k_cmp", HEAD_DIM), ("nsa_v_cmp", HEAD_DIM),
    ("nsa_k_sel", HEAD_DIM), ("nsa_v_sel", HEAD_DIM), ("nsa_k_win", HEAD_DIM), ("nsa_v_win", HEAD_DIM),
    ("nsa_branch", 3 * N_HEADS), ("nsa_gate", GROUP_WIDTH),
    ("fox_q", GROUP_WIDTH), ("fox_k", GROUP_WIDTH), ("fox_v", GROUP_WIDTH), ("fox_f", N_HEADS),
    ("fox_gate", GROUP_WIDTH),
    ("mla_cq", MLA_Q_RANK), ("mla_ckv", MLA_KV_RANK), ("mla_k_rope", MLA_ROPE), ("mla_gate", GROUP_WIDTH),
)
IN_WIDTH = sum(width for _, width in IN_SPLITS)


def rms_norm(x, g):
    xf = x.astype(jnp.float32)
    y = xf * lax.rsqrt(jnp.mean(xf * xf, axis=-1, keepdims=True) + RMS_EPS)
    return (y * g.astype(jnp.float32)).astype(x.dtype)

def apply_rope(x, pos):
    half = x.shape[-1] // 2
    inv_freq = ROPE_THETA ** (-jnp.arange(half, dtype=jnp.float32) / half)
    ang = pos.astype(jnp.float32)[:, None] * inv_freq[None, :]
    cos = jnp.cos(ang)[:, None, :]
    sin = jnp.sin(ang)[:, None, :]
    xf = x.astype(jnp.float32)
    x1, x2 = xf[..., :half], xf[..., half:]
    return jnp.concatenate([x1 * cos - x2 * sin, x2 * cos + x1 * sin], axis=-1).astype(x.dtype)

def masked_softmax(z, mask):
    p = jax.nn.softmax(jnp.where(mask, z, NEG_INF), axis=-1)
    return jnp.where(mask, p, 0.0)

def sweep_query_blocks(block_fn, seq_len):
    out = lax.map(block_fn, jnp.arange(seq_len // Q_BLOCK))
    n_blocks, b, q, h, d = out.shape
    return jnp.moveaxis(out, 0, 1).reshape(b, n_blocks * q, h, d)

def split_columns(z):
    parts = {}
    offset = 0
    for name, width in IN_SPLITS:
        parts[name] = z[..., offset:offset + width]
        offset += width
    return parts

def stick_breaking_attention(q, k, v):
    B, S, H, d = q.shape
    scale = d ** -0.5
    kpos = jnp.arange(S)

    def block(i):
        s0 = i * Q_BLOCK
        qb = lax.dynamic_slice_in_dim(q, s0, Q_BLOCK, axis=1)
        qpos = s0 + jnp.arange(Q_BLOCK)
        z = jnp.einsum("bqhd,bshd->bhqs", qb, k).astype(jnp.float32) * scale
        earlier = kpos[None, :] < qpos[:, None]
        log_keep = jnp.where(earlier, jax.nn.log_sigmoid(-z), 0.0)
        log_after = lax.cumsum(log_keep, axis=3, reverse=True) - log_keep
        w = jnp.where(earlier, jnp.exp(jax.nn.log_sigmoid(z) + log_after), 0.0)
        return jnp.einsum("bhqs,bshd->bqhd", w.astype(v.dtype), v)

    return sweep_query_blocks(block, S)

def compress_blocks(tok, pos_emb, w1, w2):
    B, S, d = tok.shape
    n_cmp = (S - CMP_LEN) // CMP_STRIDE + 1
    gather = np.arange(n_cmp)[:, None] * CMP_STRIDE + np.arange(CMP_LEN)[None, :]
    blocks = tok[:, gather] + pos_emb
    hidden = jax.nn.silu(blocks.reshape(B, n_cmp, CMP_LEN * d) @ w1)
    return hidden @ w2

def native_sparse_attention(q, kc_tok, vc_tok, ks, vs, kw, vw, branch_gates,
                            pos_k, w1_k, w2_k, pos_v, w1_v, w2_v, pos):
    B, S, H, d = q.shape
    scale = d ** -0.5
    n_cmp = (S - CMP_LEN) // CMP_STRIDE + 1
    n_sel = S // SEL_LEN
    top_n = min(SEL_TOPN, n_sel)
    cmp_start = np.arange(n_cmp) * CMP_STRIDE
    cmp_end = jnp.asarray(cmp_start + CMP_LEN - 1, dtype=jnp.int32)
    sel_start = np.arange(n_sel) * SEL_LEN
    overlap = np.clip(np.minimum(cmp_start[:, None] + CMP_LEN, sel_start[None, :] + SEL_LEN)
                      - np.maximum(cmp_start[:, None], sel_start[None, :]), 0, None)
    cmp_to_sel = jnp.asarray(overlap / CMP_LEN, dtype=jnp.float32)

    q = apply_rope(q, pos)
    kc = compress_blocks(kc_tok, pos_k, w1_k, w2_k)
    kc = apply_rope(kc[:, :, None, :], cmp_end)[:, :, 0, :]
    vc = compress_blocks(vc_tok, pos_v, w1_v, w2_v)
    ks = apply_rope(ks[:, :, None, :], pos)[:, :, 0, :]
    kw = apply_rope(kw[:, :, None, :], pos)[:, :, 0, :]
    ks_blocks = ks.reshape(B, n_sel, SEL_LEN, d)
    vs_blocks = vs.reshape(B, n_sel, SEL_LEN, d)
    kw_pad = jnp.pad(kw, ((0, 0), (WINDOW, 0), (0, 0)))
    vw_pad = jnp.pad(vw, ((0, 0), (WINDOW, 0), (0, 0)))
    sel_ids = jnp.arange(n_sel)
    gather_blocks = jax.vmap(lambda blocks, ids: blocks[ids])

    def block(i):
        s0 = i * Q_BLOCK
        qb = lax.dynamic_slice_in_dim(q, s0, Q_BLOCK, axis=1)
        gb = lax.dynamic_slice_in_dim(branch_gates, s0, Q_BLOCK, axis=1)
        qpos = s0 + jnp.arange(Q_BLOCK)
        zc = jnp.einsum("bqhd,bnd->bhqn", qb, kc).astype(jnp.float32) * scale
        pc = masked_softmax(zc, cmp_end[None, :] <= qpos[:, None])
        o_cmp = jnp.einsum("bhqn,bnd->bqhd", pc.astype(vc.dtype), vc)
        imp = jnp.einsum("bhqn,ns->bqs", pc, cmp_to_sel)
        cur = qpos // SEL_LEN
        valid = sel_ids[None, :] <= cur[:, None]
        forced = ((sel_ids[None, :] == 0) | (sel_ids[None, :] == cur[:, None])
                  | (sel_ids[None, :] == cur[:, None] - 1))
        score = jnp.where(valid, jnp.where(forced, FORCED_BONUS, imp), NEG_INF)
        _, idx = lax.top_k(score, top_n)
        kg = gather_blocks(ks_blocks, idx)
        vg = gather_blocks(vs_blocks, idx).reshape(B, Q_BLOCK, top_n * SEL_LEN, d)
        tok = idx[..., None] * SEL_LEN + jnp.arange(SEL_LEN)
        sel_mask = (tok <= qpos[None, :, None, None]).reshape(B, 1, Q_BLOCK, top_n * SEL_LEN)
        zs = jnp.einsum("bqhd,bqnld->bhqnl", qb, kg).astype(jnp.float32)
        zs = zs.reshape(B, H, Q_BLOCK, top_n * SEL_LEN) * scale
        ps = masked_softmax(zs, sel_mask)
        o_slc = jnp.einsum("bhqm,bqmd->bqhd", ps.astype(vg.dtype), vg)
        kwb = lax.dynamic_slice_in_dim(kw_pad, s0, WINDOW + Q_BLOCK, axis=1)
        vwb = lax.dynamic_slice_in_dim(vw_pad, s0, WINDOW + Q_BLOCK, axis=1)
        kpos = s0 - WINDOW + jnp.arange(WINDOW + Q_BLOCK)
        win_mask = ((kpos[None, :] >= 0) & (kpos[None, :] <= qpos[:, None])
                    & (kpos[None, :] > qpos[:, None] - WINDOW))
        zw = jnp.einsum("bqhd,bkd->bhqk", qb, kwb).astype(jnp.float32) * scale
        pw = masked_softmax(zw, win_mask)
        o_win = jnp.einsum("bhqk,bkd->bqhd", pw.astype(vwb.dtype), vwb)
        return gb[..., 0:1] * o_cmp + gb[..., 1:2] * o_slc + gb[..., 2:3] * o_win

    return sweep_query_blocks(block, S)

def forgetting_attention(q, k, v, log_f):
    B, S, H, d = q.shape
    scale = d ** -0.5
    cum = jnp.cumsum(log_f, axis=1).transpose(0, 2, 1)
    kpos = jnp.arange(S)

    def block(i):
        s0 = i * Q_BLOCK
        qb = lax.dynamic_slice_in_dim(q, s0, Q_BLOCK, axis=1)
        cq = lax.dynamic_slice_in_dim(cum, s0, Q_BLOCK, axis=2)
        qpos = s0 + jnp.arange(Q_BLOCK)
        z = (jnp.einsum("bqhd,bshd->bhqs", qb, k).astype(jnp.float32) * scale
             + cq[..., None] - cum[:, :, None, :])
        p = masked_softmax(z, kpos[None, :] <= qpos[:, None])
        return jnp.einsum("bhqs,bshd->bqhd", p.astype(v.dtype), v)

    return sweep_query_blocks(block, S)

def latent_attention(c_q, c_kv, k_rope, q_norm_g, w_uq, kv_norm_g, w_ukv, pos):
    B, S, _ = c_q.shape
    q = (rms_norm(c_q, q_norm_g) @ w_uq).reshape(B, S, N_HEADS, MLA_NOPE + MLA_ROPE)
    q_nope = q[..., :MLA_NOPE]
    q_rot = apply_rope(q[..., MLA_NOPE:], pos)
    kv = (rms_norm(c_kv, kv_norm_g) @ w_ukv).reshape(B, S, N_HEADS, MLA_NOPE + MLA_V)
    k_nope, v = kv[..., :MLA_NOPE], kv[..., MLA_NOPE:]
    k_rot = apply_rope(k_rope[:, :, None, :], pos)[:, :, 0, :]
    scale = (MLA_NOPE + MLA_ROPE) ** -0.5
    kpos = jnp.arange(S)

    def block(i):
        s0 = i * Q_BLOCK
        qn = lax.dynamic_slice_in_dim(q_nope, s0, Q_BLOCK, axis=1)
        qr = lax.dynamic_slice_in_dim(q_rot, s0, Q_BLOCK, axis=1)
        qpos = s0 + jnp.arange(Q_BLOCK)
        z = (jnp.einsum("bqhd,bshd->bhqs", qn, k_nope)
             + jnp.einsum("bqhr,bsr->bhqs", qr, k_rot)).astype(jnp.float32) * scale
        p = masked_softmax(z, kpos[None, :] <= qpos[:, None])
        return jnp.einsum("bhqs,bshd->bqhd", p.astype(v.dtype), v)

    return sweep_query_blocks(block, S)

def hybrid_layer(x, pre_g, post_g, w_in, b_in, w_out, forget_bias,
                 pos_k, w1_k, w2_k, pos_v, w1_v, w2_v,
                 q_norm_g, w_uq, kv_norm_g, w_ukv):
    B, S, _ = x.shape
    pos = jnp.arange(S)
    h = rms_norm(x, pre_g)
    p = split_columns(h @ w_in + b_in)

    def heads(t):
        return t.reshape(B, S, N_HEADS, HEAD_DIM)

    o_sb = stick_breaking_attention(heads(p["sb_q"]), heads(p["sb_k"]), heads(p["sb_v"]))

    branch_gates = jax.nn.sigmoid(p["nsa_branch"].reshape(B, S, N_HEADS, 3))
    o_nsa = native_sparse_attention(heads(p["nsa_q"]), p["nsa_k_cmp"], p["nsa_v_cmp"],
                                    p["nsa_k_sel"], p["nsa_v_sel"], p["nsa_k_win"], p["nsa_v_win"],
                                    branch_gates, pos_k, w1_k, w2_k, pos_v, w1_v, w2_v, pos)

    log_f = jax.nn.log_sigmoid((p["fox_f"] + forget_bias).astype(jnp.float32))
    o_fox = forgetting_attention(heads(p["fox_q"]), heads(p["fox_k"]), heads(p["fox_v"]), log_f)

    o_mla = latent_attention(p["mla_cq"], p["mla_ckv"], p["mla_k_rope"],
                             q_norm_g, w_uq, kv_norm_g, w_ukv, pos)

    mix = jnp.concatenate([
        o_sb.reshape(B, S, GROUP_WIDTH) * jax.nn.silu(p["sb_gate"]),
        o_nsa.reshape(B, S, GROUP_WIDTH) * jax.nn.silu(p["nsa_gate"]),
        o_fox.reshape(B, S, GROUP_WIDTH) * jax.nn.silu(p["fox_gate"]),
        o_mla.reshape(B, S, GROUP_WIDTH) * jax.nn.silu(p["mla_gate"]),
    ], axis=-1)
    return x + rms_norm(mix @ w_out, post_g)

def first_inputs(seed: int = 0) -> dict:
    key = jax.random.key(seed)
    ks = jax.random.split(key, 17)
    f32 = jnp.float32

    def normal(k, shape, scale):
        return jax.random.normal(k, shape, f32) * scale

    def gain(k, shape):
        return 1.0 + 0.02 * jax.random.normal(k, shape, f32)

    flat = CMP_LEN * HEAD_DIM
    return {
        "x": normal(ks[0], (BATCH, SEQ, D_MODEL), 1.0),
        "pre_norm_g": gain(ks[1], (DEPTH, D_MODEL)),
        "post_norm_g": gain(ks[2], (DEPTH, D_MODEL)),
        "w_in": normal(ks[3], (DEPTH, D_MODEL, IN_WIDTH), D_MODEL ** -0.5),
        "b_in": normal(ks[4], (DEPTH, IN_WIDTH), 0.02),
        "w_out": normal(ks[5], (DEPTH, MIX_WIDTH, D_MODEL), MIX_WIDTH ** -0.5),
        "fox_forget_bias": jax.random.uniform(ks[6], (DEPTH, N_HEADS), f32, 1.0, 4.0),
        "nsa_cmp_pos_k": normal(ks[7], (DEPTH, CMP_LEN, HEAD_DIM), 0.02),
        "nsa_cmp_w1_k": normal(ks[8], (DEPTH, flat, CMP_HIDDEN), flat ** -0.5),
        "nsa_cmp_w2_k": normal(ks[9], (DEPTH, CMP_HIDDEN, HEAD_DIM), CMP_HIDDEN ** -0.5),
        "nsa_cmp_pos_v": normal(ks[10], (DEPTH, CMP_LEN, HEAD_DIM), 0.02),
        "nsa_cmp_w1_v": normal(ks[11], (DEPTH, flat, CMP_HIDDEN), flat ** -0.5),
        "nsa_cmp_w2_v": normal(ks[12], (DEPTH, CMP_HIDDEN, HEAD_DIM), CMP_HIDDEN ** -0.5),
        "mla_q_norm_g": gain(ks[13], (DEPTH, MLA_Q_RANK)),
        "mla_w_uq": normal(ks[14], (DEPTH, MLA_Q_RANK, N_HEADS * (MLA_NOPE + MLA_ROPE)), MLA_Q_RANK ** -0.5),
        "mla_kv_norm_g": gain(ks[15], (DEPTH, MLA_KV_RANK)),
        "mla_w_ukv": normal(ks[16], (DEPTH, MLA_KV_RANK, N_HEADS * (MLA_NOPE + MLA_V)), MLA_KV_RANK ** -0.5),
    }

def first_block(x, pre_norm_g, post_norm_g, w_in, b_in, w_out, fox_forget_bias,
              nsa_cmp_pos_k, nsa_cmp_w1_k, nsa_cmp_w2_k,
              nsa_cmp_pos_v, nsa_cmp_w1_v, nsa_cmp_w2_v,
              mla_q_norm_g, mla_w_uq, mla_kv_norm_g, mla_w_ukv):
    for l in range(DEPTH):
        x = hybrid_layer(x, pre_norm_g[l], post_norm_g[l], w_in[l], b_in[l], w_out[l],
                         fox_forget_bias[l],
                         nsa_cmp_pos_k[l], nsa_cmp_w1_k[l], nsa_cmp_w2_k[l],
                         nsa_cmp_pos_v[l], nsa_cmp_w1_v[l], nsa_cmp_w2_v[l],
                         mla_q_norm_g[l], mla_w_uq[l], mla_kv_norm_g[l], mla_w_ukv[l])
    return x


DEPTH_2 = 1

HEAD_DIM_2 = 64
A_HEADS = 8
A_WIDTH = A_HEADS * HEAD_DIM_2
DILATED_PAIRS = ((128, 1), (512, 4), (2048, 16))
B_WIDTH = 512
CONV_WIDTH = 31
C_Q_HEADS = 16
C_KV_HEADS = 2
C_WIDTH = C_Q_HEADS * HEAD_DIM_2
C_WINDOW = 128
MIX_WIDTH_2 = A_WIDTH + B_WIDTH + C_WIDTH
IN_WIDTHS = (A_WIDTH, A_WIDTH, A_WIDTH,
             B_WIDTH, B_WIDTH,
             C_WIDTH, C_KV_HEADS * HEAD_DIM_2, C_KV_HEADS * HEAD_DIM_2)
IN_WIDTH_2 = sum(IN_WIDTHS)
D_FF = -(-(8 * D_MODEL) // (3 * 256)) * 256
BLOCK = 128
EPS = 1e-6


def _rms_norm(x, g):
    xf = x.astype(jnp.float32)
    y = xf * lax.rsqrt(jnp.mean(xf * xf, axis=-1, keepdims=True) + EPS)
    return (y * g.astype(jnp.float32)).astype(x.dtype)

def _layer_norm(x, g, b):
    xf = x.astype(jnp.float32)
    mu = jnp.mean(xf, axis=-1, keepdims=True)
    var = jnp.mean(jnp.square(xf - mu), axis=-1, keepdims=True)
    y = (xf - mu) * lax.rsqrt(var + EPS)
    return (y * g.astype(jnp.float32) + b.astype(jnp.float32)).astype(x.dtype)

def _band_attention(q, k, v, max_dist, sinks=None):
    N, L, Hq, hd = q.shape
    Hk = k.shape[2]
    G = Hq // Hk
    blk = min(BLOCK, L)
    nb = -(-L // blk)
    Lp = nb * blk
    C = blk + max_dist
    qb = jnp.pad(q, ((0, 0), (0, Lp - L), (0, 0), (0, 0))).reshape(N, nb, blk, Hk, G, hd)
    kp = jnp.pad(k, ((0, 0), (max_dist, Lp - L), (0, 0), (0, 0)))
    vp = jnp.pad(v, ((0, 0), (max_dist, Lp - L), (0, 0), (0, 0)))
    idx = jnp.arange(nb)[:, None] * blk + jnp.arange(C)[None, :]
    kb = kp[:, idx]
    vb = vp[:, idx]
    s = jnp.einsum('nbqhgd,nbkhd->nbhgqk', qb, kb,
                   preferred_element_type=jnp.float32) * (hd ** -0.5)
    qpos = jnp.arange(nb)[:, None] * blk + jnp.arange(blk)[None, :]
    kpos = idx - max_dist
    dist = qpos[:, :, None] - kpos[:, None, :]
    valid = (dist >= 0) & (dist <= max_dist) & (kpos[:, None, :] >= 0)
    s = jnp.where(valid[None, :, None, None], s, -jnp.inf)
    m = jnp.max(s, axis=-1)
    if sinks is not None:
        sk = sinks.astype(jnp.float32).reshape(Hk, G)[None, None, :, :, None]
        m = jnp.maximum(m, sk)
    p = jnp.exp(s - m[..., None])
    denom = jnp.sum(p, axis=-1)
    if sinks is not None:
        denom = denom + jnp.exp(sk - m)
    o = jnp.einsum('nbhgqk,nbkhd->nbqhgd', p, vb.astype(jnp.float32))
    denom_t = jnp.transpose(denom, (0, 1, 4, 2, 3))
    o = o / denom_t[..., None]
    lse = jnp.transpose(m, (0, 1, 4, 2, 3)) + jnp.log(denom_t)
    o = o.reshape(N, Lp, Hq, hd)[:, :L]
    lse = lse.reshape(N, Lp, Hq)[:, :L]
    return o, lse

def _dilated_mixture(q, k, v):
    B, S, H, hd = q.shape
    outs, lses = [], []
    for (w, d) in DILATED_PAIRS:
        def to_res(t):
            return t.reshape(B, S // d, d, H, hd).transpose(0, 2, 1, 3, 4).reshape(B * d, S // d, H, hd)
        o, lse = _band_attention(to_res(q), to_res(k), to_res(v), w // d)
        outs.append(o.reshape(B, d, S // d, H, hd).transpose(0, 2, 1, 3, 4).reshape(B, S, H, hd))
        lses.append(lse.reshape(B, d, S // d, H).transpose(0, 2, 1, 3).reshape(B, S, H))
    wts = jax.nn.softmax(jnp.stack(lses, axis=0), axis=0)
    return jnp.einsum('cbsh,cbshd->bshd', wts, jnp.stack(outs, axis=0))

def _conformer_conv(u, gate, conv_w, conv_b, ln_g, ln_b):
    h = u * jax.nn.sigmoid(gate)
    C = h.shape[-1]
    y = lax.conv_general_dilated(h, conv_w[:, None, :].astype(h.dtype), window_strides=(1,),
                                 padding=[(CONV_WIDTH - 1, 0)],
                                 dimension_numbers=('NWC', 'WIO', 'NWC'),
                                 feature_group_count=C)
    y = y + conv_b
    return jax.nn.silu(_layer_norm(y, ln_g, ln_b))

def second_inputs(seed: int = 0) -> dict:
    key = jax.random.key(seed)
    ks = jax.random.split(key, 17)
    f32 = jnp.float32
    nrm = lambda k, shp: jax.random.normal(k, shp, dtype=f32)
    return {
        "x": nrm(ks[0], (BATCH, SEQ, D_MODEL)),
        "norm1_g": 1.0 + 0.02 * nrm(ks[1], (DEPTH_2, D_MODEL)),
        "w_in": nrm(ks[2], (DEPTH_2, D_MODEL, IN_WIDTH_2)) * D_MODEL ** -0.5,
        "a_q_g": 1.0 + 0.02 * nrm(ks[3], (DEPTH_2, HEAD_DIM_2)),
        "a_k_g": 1.0 + 0.02 * nrm(ks[4], (DEPTH_2, HEAD_DIM_2)),
        "conv_w": nrm(ks[5], (DEPTH_2, CONV_WIDTH, B_WIDTH)) * CONV_WIDTH ** -0.5,
        "conv_b": 0.02 * nrm(ks[6], (DEPTH_2, B_WIDTH)),
        "conv_ln_g": 1.0 + 0.02 * nrm(ks[7], (DEPTH_2, B_WIDTH)),
        "conv_ln_b": 0.02 * nrm(ks[8], (DEPTH_2, B_WIDTH)),
        "c_q_g": 1.0 + 0.02 * nrm(ks[9], (DEPTH_2, HEAD_DIM_2)),
        "c_k_g": 1.0 + 0.02 * nrm(ks[10], (DEPTH_2, HEAD_DIM_2)),
        "c_sinks": 0.5 * nrm(ks[11], (DEPTH_2, C_Q_HEADS)),
        "w_out": nrm(ks[12], (DEPTH_2, MIX_WIDTH_2, D_MODEL)) * MIX_WIDTH_2 ** -0.5,
        "norm2_g": 1.0 + 0.02 * nrm(ks[13], (DEPTH_2, D_MODEL)),
        "w_gate": nrm(ks[14], (DEPTH_2, D_MODEL, D_FF)) * D_MODEL ** -0.5,
        "w_up": nrm(ks[15], (DEPTH_2, D_MODEL, D_FF)) * D_MODEL ** -0.5,
        "w_down": nrm(ks[16], (DEPTH_2, D_FF, D_MODEL)) * D_FF ** -0.5,
    }

def second_block(x, norm1_g, w_in, a_q_g, a_k_g, conv_w, conv_b, conv_ln_g, conv_ln_b,
              c_q_g, c_k_g, c_sinks, w_out, norm2_g, w_gate, w_up, w_down):
    B, S, _ = x.shape
    splits = [int(s) for s in np.cumsum(IN_WIDTHS)[:-1]]
    for l in range(DEPTH_2):
        h = _rms_norm(x, norm1_g[l])
        proj = h @ w_in[l]
        aq, ak, av, bu, bg, cq, ck, cv = jnp.split(proj, splits, axis=-1)
        aq = _rms_norm(aq.reshape(B, S, A_HEADS, HEAD_DIM_2), a_q_g[l])
        ak = _rms_norm(ak.reshape(B, S, A_HEADS, HEAD_DIM_2), a_k_g[l])
        av = av.reshape(B, S, A_HEADS, HEAD_DIM_2)
        out_a = _dilated_mixture(aq, ak, av).reshape(B, S, A_WIDTH)
        out_b = _conformer_conv(bu, bg, conv_w[l], conv_b[l], conv_ln_g[l], conv_ln_b[l])
        cq = _rms_norm(cq.reshape(B, S, C_Q_HEADS, HEAD_DIM_2), c_q_g[l])
        ck = _rms_norm(ck.reshape(B, S, C_KV_HEADS, HEAD_DIM_2), c_k_g[l])
        cv = cv.reshape(B, S, C_KV_HEADS, HEAD_DIM_2)
        out_c, _ = _band_attention(cq, ck, cv, C_WINDOW - 1, sinks=c_sinks[l])
        out_c = out_c.reshape(B, S, C_WIDTH)
        mix = jnp.concatenate([out_a.astype(x.dtype), out_b.astype(x.dtype),
                               out_c.astype(x.dtype)], axis=-1)
        x = x + mix @ w_out[l]
        h2 = _rms_norm(x, norm2_g[l])
        x = x + (jax.nn.silu(h2 @ w_gate[l]) * (h2 @ w_up[l])) @ w_down[l]
    return x


def setup_inputs(seed=0):
    out = dict(first_inputs(seed))
    for name, value in second_inputs(seed + 1).items():
        if name != "x":
            out[name + "_2"] = value
    return out


def reference(
    x, pre_norm_g, post_norm_g, w_in, b_in, w_out, fox_forget_bias, nsa_cmp_pos_k, nsa_cmp_w1_k,
    nsa_cmp_w2_k, nsa_cmp_pos_v, nsa_cmp_w1_v, nsa_cmp_w2_v, mla_q_norm_g, mla_w_uq,
    mla_kv_norm_g, mla_w_ukv, norm1_g_2, w_in_2, a_q_g_2, a_k_g_2, conv_w_2, conv_b_2,
    conv_ln_g_2, conv_ln_b_2, c_q_g_2, c_k_g_2, c_sinks_2, w_out_2, norm2_g_2, w_gate_2, w_up_2,
    w_down_2,
):
    x = first_block(
        x, pre_norm_g, post_norm_g, w_in, b_in, w_out, fox_forget_bias, nsa_cmp_pos_k,
        nsa_cmp_w1_k, nsa_cmp_w2_k, nsa_cmp_pos_v, nsa_cmp_w1_v, nsa_cmp_w2_v, mla_q_norm_g,
        mla_w_uq, mla_kv_norm_g, mla_w_ukv,
    )
    return second_block(
        x, norm1_g_2, w_in_2, a_q_g_2, a_k_g_2, conv_w_2, conv_b_2, conv_ln_g_2, conv_ln_b_2,
        c_q_g_2, c_k_g_2, c_sinks_2, w_out_2, norm2_g_2, w_gate_2, w_up_2, w_down_2,
    )


_drawn_inputs = setup_inputs


def setup_inputs(seed=0):
    import zlib

    import numpy as np

    out = dict(_drawn_inputs(seed))
    spreads = {}
    factors = {'nsa_cmp_pos_k': 22.356,
     'nsa_cmp_pos_v': 6.719,
     'mla_q_norm_g': 8.0,
     'mla_kv_norm_g': 7.518,
     'norm1_g_2': 8.0,
     'a_q_g_2': 8.0,
     'a_k_g_2': 8.0,
     'conv_b_2': 25.149,
     'conv_ln_g_2': 45.393,
     'conv_ln_b_2': 43.131,
     'c_q_g_2': 8.0,
     'c_k_g_2': 8.0,
     'c_sinks_2': 149.316,
     'norm2_g_2': 6.082}
    for name, (base, spread) in spreads.items():
        noise = np.random.default_rng([zlib.crc32(name.encode()), seed]).standard_normal(out[name].shape)
        drawn = base * np.exp(spread * noise) if base else spread * noise
        out[name] = jnp.asarray(drawn.astype(out[name].dtype))
    for name, factor in factors.items():
        out[name] = (out[name] * factor).astype(out[name].dtype)
    return out
```

```python
from contextlib import ExitStack

import numpy as np

import concourse.bass as bass
from concourse import mybir

P = 128
F32 = mybir.dt.float32
F32R = mybir.dt.float32r
BF16 = mybir.dt.bfloat16
ALU = mybir.AluOpType
ACT = mybir.ActivationFunctionType
AX = mybir.AxisListType.X

LAYERS = 2
DM = 2048
T = 256
TB = T // P
KT = DM // P
EPS = 1e-6
NEG = -1e30
H = 4
HD = 128
SCALE = HD ** -0.5
MLA_SCALE = (128 + 64) ** -0.5
CMP_LEN, CMP_STRIDE = 32, 16
NCMP = (T - CMP_LEN) // CMP_STRIDE + 1
SCALE2 = 64 ** -0.5
TAPS = 31
PAD = TAPS - 1
DFF = 5632

GN = 512
RAW_SLOTS = 4
SPLIT_SLOTS = 4
SLOT_UNITS = 4

GROUPS = (
    ("mla_c", ((5904, 512),), "t"),
    ("nsa_cmp_sel", ((2560, 512),), "t"),
    ("nsa_q", ((2048, 512),), "t"),
    ("nsa_win_small", ((3072, 268), (5388, 4), (6416, 64)), "t"),
    ("sb_q", ((0, 512),), "f"),
    ("sb_k", ((512, 512),), "f"),
    ("sb_v", ((1024, 512),), "t"),
    ("fox_q", ((3852, 512),), "f"),
    ("fox_k", ((4364, 512),), "f"),
    ("fox_v", ((4876, 512),), "t"),
    ("nsa_gate", ((3340, 512),), "t"),
    ("sb_gate", ((1536, 512),), "t"),
    ("fox_gate", ((5392, 512),), "t"),
    ("mla_gate", ((6480, 512),), "t"),
)
NG = len(GROUPS)
GROUPS_2 = (
    ("c_kv", ((3584, 256),), "t"),
    ("c_q0", ((2560, 512),), "t"),
    ("b_u", ((1536, 512),), "t"),
    ("b_gate", ((2048, 512),), "t"),
    ("c_q1", ((3072, 512),), "t"),
    ("a_q", ((0, 512),), "t"),
    ("a_k", ((512, 512),), "t"),
    ("a_v", ((1024, 512),), "t"),
)
NSA_KT, SB_KT, FOX_KT, MLA_KT = 4, 0, 8, 12


class Unit:

    def __init__(self, weight, pieces, kts, layout, pair, operand, ktiles, first, last):
        self.weight, self.pieces, self.kts, self.layout = weight, pieces, kts, layout
        self.pair, self.operand, self.ktiles, self.first, self.last = pair, operand, ktiles, first, last
        self.n = sum(w for _, w in pieces)
        self.after_mid = None


def slots_of(units):
    return [units[i:i + SLOT_UNITS] for i in range(0, len(units), SLOT_UNITS)]


def input_units(weight, groups):
    return [Unit(weight, pieces, (2 * j, 2 * j + 1), layout, g % 2, "x", KT, j == 0, j == KT // 2 - 1)
            for g, (_, pieces, layout) in enumerate(groups) for j in range(KT // 2)]


def output_unit(weight, g, pair, last_pair, first_pair=0):
    return Unit(weight, ((g * GN, GN),), (2 * pair, 2 * pair + 1), "t", g % 2, "mix", KT,
                pair == first_pair, pair == last_pair)


def output_slots():
    units = [output_unit("w_out", g, pair, 7) for g in range(DM // GN) for pair in range(8)]
    units[6].after_mid = NG * 2
    return slots_of(units)


def output_slots_2():
    def both(pairs):
        return [output_unit("w_out_2", g, pair, 1, 4) for g in (0, 1) for pair in pairs]
    slots = [both((4, 5)), both((6, 7)), [], [], both((2, 3)), [], [], both((0, 1))]
    slots[0][2].after_mid = 15
    slots[1][0].after_mid = 16
    slots[7][0].after_mid = 22
    rest = [output_unit("w_out_2", g, pair, 7) for g in (2, 3) for pair in range(8)]
    rest[0].after_mid = 23
    return slots + slots_of(rest)


LAYER_SLOTS = slots_of(input_units("w_in", GROUPS)) + output_slots()
WIN_SLOTS = NG * 2
NSLOT = len(LAYER_SLOTS)
LAYER_UNITS = sum(len(s) for s in LAYER_SLOTS)
SLOTS_2 = slots_of(input_units("w_in_2", GROUPS_2)) + output_slots_2()
WIN_SLOTS_2 = len(GROUPS_2) * 2
NSLOT_2 = len(SLOTS_2)
UNITS_2 = sum(len(s) for s in SLOTS_2)
FFN_STEPS = DFF // GN
FFN_KT = DFF // P
DOWN_KTS = [(2 * j, 2 * j + 1) for j in range(20)] + [(40 + j,) for j in range(4)]
DOWN_SLOTS = len(DOWN_KTS) // SLOT_UNITS


def pages(base):
    kb = 1024
    at, off = {}, base

    def page(size, *names):
        nonlocal off
        for n in names:
            at[n] = off
        off += size
    page(16 * kb, "raw")
    page(16 * kb, "wh")
    page(16 * kb, "wl")
    page(16 * kb, "x")
    page(16 * kb, "xh")
    page(16 * kb, "xl")
    page(1024, "small")
    page(512, "ident")
    page(256, "ident_b")
    page(512, "tri_up")
    page(512, "neg_tri")
    page(256, "causal_b", )
    page(256, "strict_t_b")
    page(256, "keep_t_b")
    page(64, "cmp_mask_b")
    common_end = off
    page(16 * kb, "w1k", "mh")
    page(16 * kb, "w1v", "ml")
    at["xn"] = at["y"] = off
    at["rope_in_m"] = off
    at["rope_out_m"] = off + 2560
    at["qrT"] = off + 5120
    at["pcT"] = off
    at["pT_sel"] = off + 4 * kb
    at["pT_win"] = off + 10 * kb
    off += 16 * kb
    page(9 * kb, "w_uq", "post_g")
    page(6 * kb, "rope_in", "prob")
    page(6 * kb, "w_ukv", "rope_out", "probT")
    at["w2"] = off
    page(6 * kb, "rope_tmp", "qkT", "gate_z")
    page(4 * kb, "cT", "sb_qT", "fox_qT", "o_fox")
    page(4 * kb, "c", "cmp_tok", "sb_kT", "fox_kT", "gate_e")
    page(4 * kb, "qnT", "sb_v", "fox_v")
    page(4 * kb, "knT", "o_sb")
    page(4 * kb, "v_mla", "o_nsa")
    page(4 * kb, "cmp_blk", "o_mla")
    page(2 * kb, "bias")
    page(1 * kb, "v_sel")
    page(1 * kb, "v_win")
    page(512, "cos")
    page(1024, "sin")
    page(256, "cos_m")
    page(512, "sin_m")
    page(480, "prob_c")
    page(64, "kcT")
    page(512, "v_cmp")
    page(256, "cos_c")
    page(512, "sin_c")
    layers_end = off
    off = common_end
    page(16 * kb, "mh2")
    page(16 * kb, "ml2")
    page(16 * kb, "xn2")
    page(6 * kb, "prob2")
    page(6 * kb, "probT2")
    page(4 * kb, "tmp2")
    page(4 * kb, "cqn")
    page(4 * kb, "aqn")
    page(4 * kb, "akn")
    page(4 * kb, "cqT")
    page(2 * kb, "ckT")
    page(1 * kb, "cv")
    page(2 * kb, "ckn")
    page(4 * kb, "av")
    page(4 * kb, "u")
    page(4 * kb, "conv_y")
    page(4 * (T + PAD) * 4, "conv_h")
    page(512, "conv_wT")
    page(768, "mask_c")
    page(1536, "log_count")
    page(4 * kb, "o_c0", "o_c1", "o_a")
    block2_end = off
    at["aqT"] = at["xn2"]
    at["akT"] = at["xn2"] + 4 * kb
    at["conv_sq"] = at["xn2"] + 8 * kb
    at["conv_stat"] = at["xn2"] + 12 * kb
    at["conv_raw"] = at["xn2"] + 8 * kb
    off = common_end
    page(44 * kb, "ah")
    page(44 * kb, "al")
    at["xn3"] = at["al"]
    page(4 * kb, "silu")
    page(4 * kb, "act")
    ffn_end = off
    return at, max(layers_end, block2_end, ffn_end)


def build(nc, d, out):
    with ExitStack() as ctx:
        at, end = pages(-(-nc.sbuf_base // 64) * 64)
        assert end <= nc.sbuf_usable_end, (end, nc.sbuf_usable_end)

        def sb(name, shape, dt=F32, where=None):
            return nc.alloc_sbuf_tensor_at(name, shape, dt, offset=at[where or name])

        def sem(name):
            return ctx.enter_context(nc.semaphore(name))

        raw = sb("raw", [P, RAW_SLOTS, 2, GN])
        wh = sb("wh", [P, SPLIT_SLOTS, 2, GN], F32R)
        wl = sb("wl", [P, SPLIT_SLOTS, 2, GN], F32R)
        x = sb("x", [P, TB, DM])
        xh = sb("xh", [P, KT, T], F32R)
        xl = sb("xl", [P, KT, T], F32R)
        small = sb("small", [P, 256])
        ident = sb("ident", [P, P])
        ident_b = sb("ident_b", [P, P], BF16)
        tri_up = sb("tri_up", [P, P])
        neg_tri = sb("neg_tri", [P, P])
        causal_b = sb("causal_b", [P, P], BF16)
        strict_t_b = sb("strict_t_b", [P, P], BF16)
        keep_t_b = sb("keep_t_b", [P, P], BF16)

        cursor = [0]

        def cols(n):
            cursor[0] += n
            assert cursor[0] <= 256
            return small[:, cursor[0] - n:cursor[0]]
        one, minus_one, minus_half = cols(1), cols(1), cols(1)
        pow_in, rstd = cols(16), cols(16)
        norm_g = cols(16)
        assert cursor[0] < 64
        cursor[0] = 64
        neg_max, den, factor = cols(8), cols(8), cols(8)
        branch = cols(24)
        row_ok = cols(2)
        fox_u, fox_sp = cols(8), cols(8)
        forget_b = cols(4)
        q_norm, kv_norm = cols(3), cols(1)
        col_bias = cols(16)
        hidT, hid_e = cols(2 * NCMP), cols(2 * NCMP)
        cmp_max, cmp_den, gate_0 = cols(8), cols(8), cols(8)
        block2_cursor = cursor[0]
        cursor[0] = 88
        gq_c, gk_c, gq_a, gk_a = cols(1), cols(1), cols(1), cols(1)
        conv_b, ln_g, ln_b = cols(4), cols(4), cols(4)
        sinks, neg_sinks, sink_e = cols(16), cols(16), cols(8)
        cursor[0] = max(cursor[0], block2_cursor)

        mh, ml = sb("mh", [P, KT, T], F32R), sb("ml", [P, KT, T], F32R)
        w1 = [sb("w1k", [P, CMP_LEN, HD]), sb("w1v", [P, CMP_LEN, HD])]
        xn, y = sb("xn", [P, TB, DM]), sb("y", [P, TB, DM])
        rope_in_m, rope_out_m = sb("rope_in_m", [P, TB, 5, 64]), sb("rope_out_m", [P, TB, 5, 64])
        qrT = sb("qrT", [P, 5, T])
        pcT = sb("pcT", [P, TB, 512])
        pT_sel, pT_win = sb("pT_sel", [P, 1536]), sb("pT_win", [P, 1536])
        w_uq, post_g = sb("w_uq", [P, 3, 768]), sb("post_g", [P, DM])
        w_ukv = sb("w_ukv", [P, 1024])
        rope_in, prob = sb("rope_in", [P, TB, 6, HD]), sb("prob", [P, 1536])
        rope_out, probT = sb("rope_out", [P, TB, 6, HD]), sb("probT", [P, 1536])
        w2 = sb("w2", [P, 2, HD])
        rope_tmp, qkT, gate_z = sb("rope_tmp", [P, 6, HD]), sb("qkT", [P, 6, T]), sb("gate_z", [P, TB, 512])
        cT, sb_qT, fox_qT = sb("cT", [P, 4, T]), sb("sb_qT", [P, H, T]), sb("fox_qT", [P, H, T])
        c = sb("c", [P, TB, 512])
        cmp_tok, sb_kT, fox_kT = sb("cmp_tok", [P, TB, 2, HD]), sb("sb_kT", [P, H, T]), sb("fox_kT", [P, H, T])
        gate_e = sb("gate_e", [P, TB, 512])
        qnT, sb_v, fox_v = sb("qnT", [P, H, T]), sb("sb_v", [P, TB, 512]), sb("fox_v", [P, TB, 512])
        knT, v_mla = sb("knT", [P, H, T]), sb("v_mla", [P, TB, 512])
        cmp_blk = sb("cmp_blk", [P, 2, CMP_LEN, NCMP])
        o_mix = {"sb": sb("o_sb", [P, TB, 512]), "nsa": sb("o_nsa", [P, TB, 512]),
                 "fox": sb("o_fox", [P, TB, 512]), "mla": sb("o_mla", [P, TB, 512])}
        bias = sb("bias", [P, 512])
        v_sel, v_win = sb("v_sel", [P, TB, HD]), sb("v_win", [P, TB, HD])
        cos_t, sin_t = sb("cos", [P, TB, 64]), sb("sin", [P, TB, 2, 64])
        cos_m, sin_m = sb("cos_m", [P, TB, 32]), sb("sin_m", [P, TB, 2, 32])
        prob_c = sb("prob_c", [P, TB, H, NCMP])
        kc = nc.alloc_sbuf_tensor_at("kc", [P, 3, HD], F32, offset=at["y"] + 14 * 1024 + 512)
        kcT, v_cmp = sb("kcT", [P, NCMP]), sb("v_cmp", [P, HD])
        cos_c, sin_c = sb("cos_c", [P, 64]), sb("sin_c", [P, 2, 64])
        cmp_mask_b = sb("cmp_mask_b", [P, TB * NCMP], BF16)
        pos_in = nc.alloc_sbuf_tensor_at("pos_in", [P, 2, HD], F32, offset=at["y"] + 14 * 1024 + 512)
        posT = nc.alloc_sbuf_tensor_at("posT", [P, 2, CMP_LEN], F32, offset=at["y"] + 15 * 1024 + 512)

        mh2, ml2 = sb("mh2", [P, KT, T], F32R), sb("ml2", [P, KT, T], F32R)
        xn2 = sb("xn2", [P, TB, DM])
        prob2, probT2 = sb("prob2", [P, 1536]), sb("probT2", [P, 1536])
        tmp2 = sb("tmp2", [P, TB, 512])
        cqn, aqn, akn = sb("cqn", [P, TB, 512]), sb("aqn", [P, TB, 512]), sb("akn", [P, TB, 512])
        cqT, ckT, ckn, cv = sb("cqT", [P, 4, T]), sb("ckT", [P, 2, T]), sb("ckn", [P, TB, 2, P]), sb("cv", [P, TB, 128])
        av, u = sb("av", [P, TB, 512]), sb("u", [P, TB, 512])
        conv_y, conv_h = sb("conv_y", [P, 4, T]), sb("conv_h", [P, 4, PAD + T])
        conv_wT = sb("conv_wT", [P, 4, TAPS])
        mask_c = sb("mask_c", [P, 384], BF16)
        log_count = sb("log_count", [P, 384])
        o_c = [sb("o_c0", [P, TB, 512]), sb("o_c1", [P, TB, 512])]
        o_a = sb("o_a", [P, TB, 512])
        aqT, akT = sb("aqT", [P, 4, T]), sb("akT", [P, 4, T])
        conv_sq, conv_stat = sb("conv_sq", [P, 4, T]), sb("conv_stat", [P, 3, T])
        conv_raw = sb("conv_raw", [P, 512])
        ah, al = sb("ah", [P, FFN_KT, T], F32R), sb("al", [P, FFN_KT, T], F32R)
        xn3 = sb("xn3", [P, TB, DM])
        silu, act_a = sb("silu", [P, TB, 512]), sb("act", [P, TB, 512])

        psum = ctx.enter_context(nc.psum_tensor("psum", [P, 8, 512], F32))
        acc = [psum[:, 0:2, :], psum[:, 2:4, :]]
        accf = [a.rearrange("p b c -> p (b c)") for a in acc]
        st = psum[:, 4:8, :].rearrange("p b c -> p (b c)")
        all_banks = psum[:, :, :].rearrange("p b c -> p (b c)")

        raw_loaded = [sem(f"raw_loaded{i}") for i in range(RAW_SLOTS)]
        hi_done = sem("hi_done")
        lo_done = sem("lo_done")
        unit_used = sem("unit_used")
        stage_done = sem("stage_done")
        act_mid_done = sem("act_mid_done")
        dve_mid_done = sem("dve_mid_done")
        named = {}

        def s(name):
            if name not in named:
                named[name] = sem(name)
            return named[name]

        consts_loaded = sem("consts_loaded")
        x_loaded = sem("x_loaded")
        layer_loads = sem("layer_loads")
        w1_loaded = sem("w1_loaded")
        bias_loaded = sem("bias_loaded")
        post_g_loaded = sem("post_g_loaded")
        block2_loads = sem("block2_loads")
        out_stored = sem("out_stored")
        norm_g_loaded = sem("norm_g_loaded")
        ffn_high = sem("ffn_high")
        ffn_exp = sem("ffn_exp")
        N_CONSTS = 15
        LAYER_LOADS = 3 + 4 + 2 + 2
        BLOCK2_LOADS = 8 + 3 + 3 + 1
        BIAS_GROUPS = [g for g, (_, _, layout) in enumerate(GROUPS) if layout == "t"]
        BIAS_DMAS = [len(GROUPS[g][1]) for g in BIAS_GROUPS]
        BIAS_TOTAL = sum(BIAS_DMAS)

        def rows(weight, l):
            if weight in ("w_in", "w_out"):
                return d[weight][bass.ds(l, 1), :, :].rearrange("a k n -> (a k) n")
            return d[weight][0, :, :]

        def weight_src(unit, l, c0, w):
            m = rows(unit.weight, l)
            if unit.operand == "x":
                v = m.rearrange("(p t) n -> p t n", t=KT)
            else:
                v = m.rearrange("(t p) n -> p t n", p=P)
            return v[:, unit.kts[0]:unit.kts[-1] + 1, c0:c0 + w]

        operands = {"x": (xh, xl), "mix": (mh, ml), "mix2": (mh2, ml2), "act": (ah, al)}

        class Place:

            def __init__(self, units, slots, loads, once, single):
                self.units, self.slots, self.loads, self.once, self.single = units, slots, loads, once, single

        loads_before = [[0] * RAW_SLOTS]
        n_units = 0
        for slot in LAYER_SLOTS:
            for unit in slot:
                row = list(loads_before[-1])
                row[n_units % RAW_SLOTS] += len(unit.pieces)
                loads_before.append(row)
                n_units += 1
        LAYER_PIECES = loads_before[-1]

        def in_layer(l):
            return Place(l * LAYER_UNITS, l * NSLOT, [l * q for q in LAYER_PIECES], l + 1, False)

        def after(units, slots):
            return Place(LAYERS * LAYER_UNITS + units, LAYERS * NSLOT + slots,
                         [LAYERS * q + units // RAW_SLOTS for q in LAYER_PIECES], 1, True)

        def pieces_loaded(place, n):
            within = n // RAW_SLOTS + 1 if place.single else loads_before[n + 1][n % RAW_SLOTS]
            return 16 * (place.loads[n % RAW_SLOTS] + within)

        wait_passed = {name: sem(f"{name}_wait_passed") for name in ("sp", "pe", "act", "dve")}

        def stand_alone(eng, name):
            eng.sem_inc(wait_passed[name], 1)

        def load_unit(sp, place, n, unit, src):
            sp.wait_ge(lo_done, place.units + n + 1)
            stand_alone(sp, "sp")
            off = 0
            for piece, (c0, w) in enumerate(unit.pieces):
                sp.dma_start(raw[:, n % RAW_SLOTS, 0:len(unit.kts), off:off + w], src(unit, c0, w))\
                    .then_inc(raw_loaded[n % RAW_SLOTS], 16)
                off += w

        def split_high(place, n, unit):
            act = nc.scalar
            act.wait_ge(raw_loaded[n % RAW_SLOTS], pieces_loaded(place, n))
            act.wait_ge(unit_used, place.units + n + 1)
            k = len(unit.kts)
            act.activation(wh[:, n % SPLIT_SLOTS, 0:k, 0:unit.n], raw[:, n % RAW_SLOTS, 0:k, 0:unit.n],
                           ACT.Copy).then_inc(hi_done, 1)

        def split_low(place, n, unit):
            dve = nc.vector
            dve.wait_ge(hi_done, place.units + n + 1)
            k = len(unit.kts)
            dve.tensor_tensor(out=wl[:, n % SPLIT_SLOTS, 0:k, 0:unit.n], in0=raw[:, n % RAW_SLOTS, 0:k, 0:unit.n],
                              in1=wh[:, n % SPLIT_SLOTS, 0:k, 0:unit.n].bitcast(F32),
                              op=ALU.subtract).then_inc(lo_done, 1)

        def multiply(place, n, unit, operand=None):
            pe = nc.tensor
            if unit.after_mid is not None:
                pe.wait_ge(act_mid_done, place.slots + unit.after_mid + 2)
                pe.wait_ge(dve_mid_done, place.slots + unit.after_mid + 2)
            pe.wait_ge(lo_done, RAW_SLOTS + place.units + n + 1)
            ah_, al_ = operands[operand or unit.operand]
            slot, out_ = n % SPLIT_SLOTS, acc[unit.pair]
            for kk, kt in enumerate(unit.kts):
                first = unit.first and kk == 0
                last = unit.last and kk == len(unit.kts) - 1
                hi_w, lo_w = wh[:, slot, kk, 0:unit.n], wl[:, slot, kk, 0:unit.n]
                if unit.layout == "t":
                    for tb in range(TB):
                        tok = slice(tb * P, (tb + 1) * P)
                        o = out_[:, tb, 0:unit.n]
                        pe.matmul(o, ah_[:, kt, tok], hi_w, start=first, stop=False)
                        pe.matmul(o, ah_[:, kt, tok], lo_w, start=False, stop=False)
                        ins = pe.matmul(o, al_[:, kt, tok], hi_w, start=False, stop=last)
                else:
                    for j in range(H):
                        o = accf[unit.pair][:, j * T:(j + 1) * T]
                        f = slice(j * P, (j + 1) * P)
                        pe.matmul(o, hi_w[:, f], ah_[:, kt, :], start=first and j % 2 == 0, stop=False,
                                  skip_group_check=True)
                        pe.matmul(o, lo_w[:, f], ah_[:, kt, :], start=False, stop=False, skip_group_check=True)
                        ins = pe.matmul(o, hi_w[:, f], al_[:, kt, :], start=False, stop=last,
                                        skip_group_check=True)
            ins.then_inc(unit_used, 1)

        def pe_stage(place, h, stage):
            pe = nc.tensor
            pe.wait_ge(act_mid_done, place.slots + h + 1)
            pe.wait_ge(dve_mid_done, place.slots + h + 1)
            stand_alone(pe, "pe")
            stage()
            pe.drain().then_inc(stage_done, 1)

        def act_mid(place, h, mid):
            act = nc.scalar
            act.wait_ge(stage_done, place.slots + h + 2)
            stand_alone(act, "act")
            mid()
            act.drain().then_inc(act_mid_done, 1)

        def dve_mid(place, h, mid):
            dve = nc.vector
            dve.wait_ge(stage_done, place.slots + h + 2)
            stand_alone(dve, "dve")
            mid()
            dve.drain().then_inc(dve_mid_done, 1)

        def nothing():
            pass

        def pe_scores(q, k, extra=None):
            pe = nc.tensor
            for h in range(4):
                for blk, o, n in ((1, st[:, h * 256:(h + 1) * 256], 256),
                                  (0, st[:, 1024 + h * P:1024 + (h + 1) * P], P)):
                    parts = [(q(h, blk), k(h)[:, 0:n])] + (extra(h, blk, n) if extra else [])
                    for i, (lhsT, rhs) in enumerate(parts):
                        pe.matmul(o, lhsT, rhs, start=i == 0, stop=False, skip_group_check=True)
                    pe.matmul(o[:, n - P:n], ident_b[:, :], causal_b[:, :], start=False, stop=True,
                              skip_group_check=True)

        def pe_transpose_probs(p):
            pe = nc.tensor
            for h in range(4):
                for src, dst in ((1024 + h * P, h * 256), (h * 256, h * 256 + P), (h * 256 + P, 1024 + h * P)):
                    pe.transpose(st[:, dst:dst + P], p[:, src:src + P], ident[:, :])

        def pe_values(terms, o, width=HD):
            pe = nc.tensor
            for h in range(4):
                for blk in range(TB):
                    prods = []
                    for pT, v in terms:
                        prods.append((pT[:, h * 256 + blk * P:h * 256 + (blk + 1) * P], v(0, h)))
                        if blk == 1:
                            prods.append((pT[:, 1024 + h * P:1024 + (h + 1) * P], v(1, h)))
                    for i, (a, b) in enumerate(prods):
                        pe.matmul(o(h, blk), a, b, start=i == 0, stop=i == len(prods) - 1, skip_group_check=True)

        scores_1 = st[:, 0:1024].rearrange("p (h k) -> p h k", h=4)
        scores_0 = st[:, 1024:1536].rearrange("p (h k) -> p h k", h=4)

        def act_softmax(place, name, p):
            act = nc.scalar
            act.wait_ge(s(name + "_max"), place.once)
            for blk, base, n in ((0, 1024, P), (1, 0, 256)):
                for h in range(4):
                    ins = act.activation(p[:, base + h * n:base + (h + 1) * n], st[:, base + h * n:base + (h + 1) * n],
                                         ACT.Exp, bias=neg_max[:, blk * 4 + h:blk * 4 + h + 1],
                                         accum_out=den[:, blk * 4 + h:blk * 4 + h + 1])
            act.drain().then_inc(s(name + "_exp"), 1)

        def dve_softmax(place, name):
            dve = nc.vector
            dve.tensor_reduce(out=neg_max[:, 4:8], in_=scores_1, axis=AX, op=ALU.max, negate=True)
            dve.tensor_reduce(out=neg_max[:, 0:4], in_=scores_0, axis=AX, op=ALU.max, negate=True)
            dve.drain().then_inc(s(name + "_max"), 1)
            dve.wait_ge(s(name + "_exp"), place.once)
            dve.reciprocal(factor, den)
            dve.drain()

        def act_copy_half(dst):
            nc.scalar.activation(dst[:, 0:1024], st[:, 0:1024], ACT.Copy)

        def dve_copy_half(dst):
            nc.vector.tensor_copy(dst[:, 1024:1536], st[:, 1024:1536])

        def bc(ap, n):
            return ap.unsqueeze(2).to_broadcast([ap.shape[0], ap.shape[1], n])

        def over(ap, m):
            return ap.unsqueeze(1).to_broadcast([ap.shape[0], m, ap.shape[1]])

        def heads(ap, n):
            return ap.rearrange("p b (h c) -> p (b h) c", c=n)

        def dve_scaled_out(dst, src):
            nc.vector.tensor_tensor(out=heads(dst[:, :, :], HD), in0=src.rearrange("p (n c) -> p n c", c=HD),
                                    in1=bc(factor, HD), op=ALU.mult)

        def dve_evacuate_biased(pair, parts):
            for c0, w, dst in parts:
                nc.vector.tensor_tensor(out=dst, in0=acc[pair][:, :, c0:c0 + w], in1=over(bias[:, c0:c0 + w], TB),
                                        op=ALU.add)

        def dve_rope(src, dst, tmp, cos, sin, m, half, parts=P):
            dve = nc.vector
            s4 = src.rearrange("p m (a c) -> p m a c", a=2)
            t4 = tmp.rearrange("p m (a c) -> p m a c", a=2)
            dve.tensor_tensor(out=dst.rearrange("p m (a c) -> p (m a) c", a=2),
                              in0=src.rearrange("p m (a c) -> p (m a) c", a=2), in1=over(cos, 2 * m), op=ALU.mult)
            dve.tensor_tensor(out=t4[:, :, 0, :], in0=s4[:, :, 1, :], in1=over(sin[:, 0, :], m), op=ALU.mult)
            dve.tensor_tensor(out=t4[:, :, 1, :], in0=s4[:, :, 0, :], in1=over(sin[:, 1, :], m), op=ALU.mult)
            dve.drain()
            dve.tensor_tensor(out=dst, in0=dst, in1=tmp, op=ALU.add)
            dve.drain()

        def pool_power(place, name, n):
            pool = nc.gpsimd
            pool.wait_ge(s(name + "_ms"), place.once)
            pool.tensor_tensor(out=rstd[:, 0:n], in0=pow_in[:, 0:n], in1=minus_half.to_broadcast([P, n]),
                               op=ALU.pow).then_inc(s(name + "_rstd"), 1)

        def act_norm(place, name, buf, update_wait):
            act = nc.scalar
            act.wait_ge(*update_wait)
            for tb in range(TB):
                act.activation(buf[:, tb, :], x[:, tb, :], ACT.Square, accum_out=pow_in[:, tb:tb + 1])
            act.drain().then_inc(s(name + "_sumsq"), 1)

        def dve_norm(place, name, buf):
            dve = nc.vector
            dve.wait_ge(s(name + "_sumsq"), place.once)
            dve.tensor_scalar(out=pow_in[:, 0:2], in0=pow_in[:, 0:2], scalar1=1.0 / DM, scalar2=EPS,
                              op0=ALU.mult, op1=ALU.add).then_inc(s(name + "_ms"), 1)
            dve.wait_ge(s(name + "_rstd"), place.once)
            for tb in range(TB):
                ins = dve.tensor_scalar(out=buf[:, tb, :], in0=x[:, tb, :], scalar1=rstd[:, tb:tb + 1],
                                        scalar2=None, op0=ALU.mult)
            ins.then_inc(s(name + "_scaled"), 1)

        def pe_norm(place, name, buf):
            pe = nc.tensor
            pe.wait_ge(s(name + "_scaled"), place.once)
            for kt in range(KT):
                for tb in range(TB):
                    pe.transpose(all_banks[:, kt * T + tb * P:kt * T + (tb + 1) * P],
                                 buf[:, tb, :].rearrange("p (c t) -> p t c", t=KT)[:, kt, :], ident[:, :])
            pe.drain().then_inc(s(name + "_turned"), 1)

        def act_operand(place, name, gains):
            act = nc.scalar
            act.wait_ge(norm_g_loaded, 16 * gains)
            act.wait_ge(s(name + "_turned"), place.once)
            for kt in range(KT):
                ins = act.activation(xh[:, kt, :], all_banks[:, kt * T:(kt + 1) * T], ACT.Copy,
                                     scale=norm_g[:, kt:kt + 1])
                if kt == KT // 2 - 1:
                    ins.then_inc(s(name + "_high_half"), 1)
            ins.then_inc(s(name + "_high"), 1)

        def dve_operand(place, name, gains):
            dve = nc.vector
            dve.wait_ge(norm_g_loaded, 16 * gains)
            dve.wait_ge(s(name + "_high_half"), place.once)
            for kt in range(KT):
                if kt == KT // 2:
                    dve.wait_ge(s(name + "_high"), place.once)
                ins = dve.scalar_tensor_tensor(out=xl[:, kt, :], in0=all_banks[:, kt * T:(kt + 1) * T],
                                               scalar=norm_g[:, kt:kt + 1], in1=xh[:, kt, :].bitcast(F32),
                                               op0=ALU.mult, op1=ALU.subtract)
            ins.then_inc(s(name + "_operand"), 1)

        def pe_turn_mix(o, bank):
            pe = nc.tensor
            for j in range(4):
                for tb in range(TB):
                    pe.transpose(st[:, bank * 512 + j * T + tb * P:bank * 512 + j * T + (tb + 1) * P],
                                 o[:, tb, j * P:(j + 1) * P], ident[:, :])

        def act_mix_high(place, name, hi, kt0, bank):
            nc.scalar.activation(hi[:, kt0:kt0 + 4, :].rearrange("p k t -> p (k t)"),
                                 st[:, bank * 512:bank * 512 + 1024], ACT.Copy).then_inc(s(name + "_mix_high"), 1)

        def dve_mix_low(place, name, hi, lo, kt0, bank):
            nc.vector.wait_ge(s(name + "_mix_high"), place.once)
            nc.vector.tensor_tensor(out=lo[:, kt0:kt0 + 4, :].rearrange("p k t -> p (k t)"),
                                    in0=st[:, bank * 512:bank * 512 + 1024],
                                    in1=hi[:, kt0:kt0 + 4, :].rearrange("p k t -> p (k t)").bitcast(F32),
                                    op=ALU.subtract)

        FFN_UNITS, FFN_SLOTS = 16, 4

        def ffn_place(i):
            a = after(UNITS_2, NSLOT_2)
            return Place(a.units + i * FFN_UNITS, a.slots + i * FFN_SLOTS,
                         [q + i * (FFN_UNITS // RAW_SLOTS) for q in a.loads], 1, True)

        def down_place(i):
            a = after(UNITS_2 + FFN_STEPS * FFN_UNITS, NSLOT_2 + FFN_STEPS * FFN_SLOTS + 1)
            return Place(a.units + i * 48, a.slots + i * 2 * DOWN_SLOTS,
                         [q + i * (48 // RAW_SLOTS) for q in a.loads], 1, True)

        def gate_up_units():
            return [Unit(w, ((0, GN),), (2 * j, 2 * j + 1), "t", i, "x", KT, j == 0, j == KT // 2 - 1)
                    for i, w in enumerate(("w_gate_2", "w_up_2")) for j in range(KT // 2)]

        def down_units(g):
            return [Unit("w_down_2", ((0, GN),), kts, "t", g, "act", FFN_KT, j == 0, j == 23)
                    for j, kts in enumerate(DOWN_KTS)]

        block = ctx.enter_context(nc.Block())

        @block.sync
        def _(sp):
            def layer_src(l):
                return lambda unit, c0, w: weight_src(unit, l, c0, w)
            with sp.Fori(0, LAYERS) as l:
                place, n = in_layer(l), 0
                for slot in LAYER_SLOTS:
                    for unit in slot:
                        load_unit(sp, place, n, unit, layer_src(l))
                        n += 1
            place, n = after(0, 0), 0
            for slot in SLOTS_2:
                for unit in slot:
                    load_unit(sp, place, n, unit, layer_src(0))
                    n += 1
            with sp.Fori(0, FFN_STEPS) as i:
                place = ffn_place(i)
                for n, unit in enumerate(gate_up_units()):
                    load_unit(sp, place, n, unit, lambda unit, c0, w: rows(unit.weight, 0).rearrange(
                        "(p t) n -> p t n", t=KT)[:, unit.kts[0]:unit.kts[-1] + 1, bass.ds(i * GN, GN)])
            with sp.Fori(0, 2) as i:
                place = down_place(i)
                for g in range(2):
                    for j, unit in enumerate(down_units(g)):
                        load_unit(sp, place, g * 24 + j, unit, lambda unit, c0, w: rows(unit.weight, 0).rearrange(
                            "(t p) n -> p t n", p=P)[:, unit.kts[0]:unit.kts[-1] + 1,
                                                     bass.ds(i * (2 * GN) + g * GN, GN)])
            sp.wait_ge(out_stored, 16 * 4)

        @block.gpsimd
        def _(pool):
            def load(dst, src, signal):
                pool.dma_start(dst, src, allow_slow_non_contiguous=True).then_inc(signal, 16)
            load(x[:, :, :], d["x"][0, :, :].rearrange("(b p) n -> p b n", p=P), x_loaded)
            consts = [(ident[:, :], "c_ident"), (ident_b[:, :], "c_ident_b"), (tri_up[:, :], "c_tri_up"),
                      (neg_tri[:, :], "c_neg_tri"), (causal_b[:, :], "c_causal_b"),
                      (strict_t_b[:, :], "c_strict_t_b"), (keep_t_b[:, :], "c_keep_t_b"), (cos_t[:, :, :], "c_cos"),
                      (sin_t[:, :, :, :], "c_sin"), (cos_m[:, :, :], "c_cos_m"), (sin_m[:, :, :, :], "c_sin_m"),
                      (row_ok, "c_row_ok"),
                      (cmp_mask_b[:, :], "c_cmp_mask_b"), (cos_c[0:NCMP, :], "c_cos_c"),
                      (sin_c[0:NCMP, :, :], "c_sin_c")]
            assert len(consts) == N_CONSTS
            for dst, name in consts:
                load(dst, d[name], consts_loaded)

            with pool.Fori(0, LAYERS) as l:
                place = in_layer(l)

                def row(name):
                    return d[name][bass.ds(l, 1), :]

                def mat(name):
                    return d[name][bass.ds(l, 1), :, :].rearrange("a k n -> (a k) n")
                pool.wait_ge(act_mid_done, place.slots + 1)
                pool.wait_ge(dve_mid_done, place.slots + 1)
                pool.wait_ge(stage_done, place.slots + 1)
                load(norm_g, row("pre_norm_g").rearrange("a (p t) -> (a p) t", t=KT), norm_g_loaded)
                pool_power(place, "pre", 2)
                load(q_norm, row("mla_q_norm_g").rearrange("a (t p) -> p (a t)", p=P), layer_loads)
                load(kv_norm, row("mla_kv_norm_g").rearrange("a (t p) -> p (a t)", p=P), layer_loads)
                load(forget_b, row("fox_forget_bias").to_broadcast([P, 4]), layer_loads)
                for i, c0 in enumerate((0, 512, 3852, 4364)):
                    load(col_bias[:, 4 * i:4 * i + 4],
                         row("b_in")[:, c0:c0 + 512].rearrange("a (t p) -> p (a t)", p=P), layer_loads)
                load(w_uq[:, :, :], mat("mla_w_uq").rearrange("(t p) n -> p t n", p=P), layer_loads)
                load(w_ukv[:, :], mat("mla_w_ukv"), layer_loads)

                def load_bias(i):
                    off = 0
                    for c0, w in GROUPS[BIAS_GROUPS[i]][1]:
                        load(bias[:, off:off + w], row("b_in")[:, c0:c0 + w].to_broadcast([P, w]), bias_loaded)
                        off += w
                load_bias(0)
                pool.wait_ge(s("pre_turned"), place.once)
                load(pos_in[0:CMP_LEN, 0, :], mat("nsa_cmp_pos_k"), layer_loads)
                load(pos_in[0:CMP_LEN, 1, :], mat("nsa_cmp_pos_v"), layer_loads)
                load(w1[0][:, :, :], mat("nsa_cmp_w1_k").rearrange("(j p) n -> p j n", p=P), w1_loaded)
                load(w1[1][:, :, :], mat("nsa_cmp_w1_v").rearrange("(j p) n -> p j n", p=P), w1_loaded)
                load(w2[:, 0, :], mat("nsa_cmp_w2_k"), w1_loaded)
                load(w2[:, 1, :], mat("nsa_cmp_w2_v"), w1_loaded)
                pool_power(place, "mla", 4)
                for i in range(1, len(BIAS_GROUPS)):
                    pool.wait_ge(dve_mid_done, place.slots + 2 * BIAS_GROUPS[i - 1] + 3)
                    load_bias(i)
                    if BIAS_GROUPS[i] == 6:
                        load(post_g[:, :], row("post_norm_g").to_broadcast([P, DM]), post_g_loaded)
                pool_power(place, "post", 2)

            place = after(0, 0)
            pool.wait_ge(act_mid_done, place.slots + 1)
            pool.wait_ge(dve_mid_done, place.slots + 1)
            pool.wait_ge(stage_done, place.slots + 1)
            load(norm_g, d["norm1_g_2"][0:1, :].rearrange("a (p t) -> (a p) t", t=KT), norm_g_loaded)
            for half in (0, 64):
                for dst, name in ((gq_c, "c_q_g_2"), (gk_c, "c_k_g_2"), (gq_a, "a_q_g_2"), (gk_a, "a_k_g_2")):
                    load(dst[half:half + 64, :], d[name][0:1, :].rearrange("a n -> n a"), block2_loads)
            for dst, name in ((conv_b, "conv_b_2"), (ln_g, "conv_ln_g_2"), (ln_b, "conv_ln_b_2")):
                load(dst, d[name][0:1, :].rearrange("a (t p) -> p (a t)", p=P), block2_loads)
            load(sinks, d["c_sinks_2"][0:1, :].to_broadcast([P, 16]), block2_loads)
            load(mask_c[:, :], d["c_mask_c"], block2_loads)
            load(log_count[:, :], d["c_log_count"], block2_loads)
            pool_power(place, "first2", 2)
            pool.wait_ge(s("first2_turned"), place.once)
            load(conv_raw[0:TAPS, :], d["conv_w_2"][0, :, :], block2_loads)
            pool.wait_ge(s("first2_operand"), 1)
            load(norm_g, d["norm2_g_2"][0:1, :].rearrange("a (p t) -> (a p) t", t=KT), norm_g_loaded)
            for name, n in (("ck2", 4), ("cq02", 16), ("cq12", 16), ("aq2", 16), ("ak2", 16)):
                pool_power(place, name, n)
            pool.wait_ge(s("conv_var2"), 1)
            pool.tensor_tensor(out=conv_stat[:, 2, :], in0=conv_stat[:, 1, :],
                               in1=minus_half.to_broadcast([P, T]), op=ALU.pow).then_inc(s("conv_rstd2"), 1)
            pool_power(place, "second3", 2)
            with pool.Fori(0, 2) as i:
                for g in range(2):
                    pool.wait_ge(dve_mid_done, down_place(i).slots + (g + 1) * DOWN_SLOTS + 1)
                    pool.dma_start(out[:, bass.ds(i * (2 * GN) + g * GN, GN)].rearrange("(b p) n -> p b n", p=P),
                                   x[:, :, bass.ds(i * (2 * GN) + g * GN, GN)]).then_inc(out_stored, 16)

        @block.tensor
        def _(pe):
            pe.sem_inc(unit_used, SPLIT_SLOTS)
            pe.sem_inc(stage_done, 1)
            pe.wait_ge(consts_loaded, 16 * N_CONSTS)

            with pe.Fori(0, LAYERS) as l:
                place = in_layer(l)
                pe_norm(place, "pre", xn)
                pe.wait_ge(s("pre_operand"), place.once)

                def mla_turn_latents():
                    for j in range(4):
                        for tb in range(TB):
                            pe.transpose(st[:, j * T + tb * P:j * T + (tb + 1) * P], c[:, tb, j * P:(j + 1) * P],
                                         ident[:, :])
                    pe.wait_ge(layer_loads, 16 * LAYER_LOADS * place.once)
                    stand_alone(pe, "pe")
                    for i in range(2):
                        pe.transpose(st[:, 1024 + 32 * i:1024 + 32 * (i + 1)], pos_in[0:CMP_LEN, i, :],
                                     ident[0:CMP_LEN, 0:CMP_LEN])

                def mla_queries_and_keys():
                    for h in range(H):
                        for t in range(3):
                            pe.matmul(st[:, h * T:(h + 1) * T], w_uq[:, t, h * 192:h * 192 + 128], cT[:, t, :],
                                      start=t == 0, stop=t == 2, skip_group_check=True)
                        pe.matmul(st[:, 1024 + h * T:1024 + (h + 1) * T], w_ukv[:, h * 256:h * 256 + 128],
                                  cT[:, 3, :], start=True, stop=True, skip_group_check=True)

                def mla_values_and_ropes():
                    v_cols = w_ukv[:, :].rearrange("p (h c) -> p h c", h=H)[:, :, 128:256]
                    for tb in range(TB):
                        tok = slice(tb * P, (tb + 1) * P)
                        pe.matmul(st[:, tb * 512:(tb + 1) * 512], cT[:, 3, tok], v_cols, start=True, stop=True)
                        for t in range(3):
                            rope_cols = w_uq[:, t, :].rearrange("p (h c) -> p h c", h=H)[:, :, 128:192]
                            pe.matmul(st[:, 1024 + tb * 256:1024 + (tb + 1) * 256], cT[:, t, tok], rope_cols,
                                      start=t == 0, stop=t == 2, skip_group_check=True)
                    for i in range(2):
                        for tb in range(TB):
                            pe.transpose(st[:, 1536 + i * T + tb * P:1536 + i * T + (tb + 1) * P],
                                         cmp_tok[:, tb, i, :], ident[:, :])

                def nsa_compress_hidden():
                    pe.wait_ge(w1_loaded, 64 * place.once)
                    for i in range(2):
                        for j in range(CMP_LEN):
                            pe.matmul(st[:, 1536 + i * NCMP:1536 + (i + 1) * NCMP], w1[i][:, j, :], cmp_blk[:, i, j, :],
                                      start=j == 0, stop=j == CMP_LEN - 1, skip_group_check=True)

                def nsa_compress_out():
                    for i in range(2):
                        pe.matmul(st[0:NCMP, 1536 + i * HD:1536 + (i + 1) * HD], hidT[:, i * NCMP:(i + 1) * NCMP],
                                  w2[:, i, :], start=True, stop=True, skip_group_check=True)

                def nsa_turn_compressed_keys():
                    pe.transpose(st[:, 1536:1536 + NCMP], kc[0:NCMP, 1, :], ident[0:NCMP, 0:NCMP])

                def mla_turn_ropes():
                    for j in range(5):
                        for tb in range(TB):
                            pe.transpose(st[0:64, j * T + tb * P:j * T + (tb + 1) * P], rope_out_m[:, tb, j, :],
                                         ident[:, :])

                def nsa_turn():
                    for j in range(6):
                        for tb in range(TB):
                            pe.transpose(st[:, j * T + tb * P:j * T + (tb + 1) * P], rope_out[:, tb, j, :], ident[:, :])

                def mla_scores():
                    def rope_part(h, blk, n):
                        return [(qrT[0:64, h, blk * P:(blk + 1) * P], qrT[0:64, 4, 0:n])]
                    pe_scores(lambda h, blk: qnT[:, h, blk * P:(blk + 1) * P], lambda h: knT[:, h, :], rope_part)
                    for blk in range(TB):
                        for h in range(H):
                            o = st[:, 1536 + (blk * H + h) * NCMP:1536 + (blk * H + h + 1) * NCMP]
                            pe.matmul(o, qkT[:, h, blk * P:(blk + 1) * P], kcT[:, :],
                                      start=True, stop=False, skip_group_check=True)
                            pe.matmul(o, ident_b[:, :], cmp_mask_b[:, blk * NCMP:(blk + 1) * NCMP], start=False,
                                      stop=True, skip_group_check=True)

                def turn_probs_and_compressed(p, blk):
                    if p is not None:
                        pe_transpose_probs(p)
                    for h in range(H):
                        pe.transpose(st[0:NCMP, 1536 + h * P:1536 + (h + 1) * P], prob_c[:, blk, h, :], ident[:, :])

                def sb_scores():
                    for h in range(H):
                        pe.matmul(st[:, h * T:(h + 1) * T], sb_kT[:, h, 0:P], sb_qT[:, h, :],
                                  start=h % 2 == 0, stop=True, skip_group_check=True)
                        pe.matmul(st[:, 1024 + h * P:1024 + (h + 1) * P], sb_kT[:, h, P:T], sb_qT[:, h, P:T],
                                  start=h == 0, stop=True, skip_group_check=True)

                def sb_decays():
                    for h in range(H):
                        k0, k1 = st[:, h * T:(h + 1) * T], st[:, 1024 + h * P:1024 + (h + 1) * P]
                        sp1 = prob[:, 1024 + h * P:1024 + (h + 1) * P]
                        for o, lhsT, rhs in ((k0, neg_tri[:, :], prob[:, h * T:(h + 1) * T]),
                                             (k0[:, P:T], minus_one.to_broadcast([P, P]), sp1),
                                             (k1, neg_tri[:, :], sp1),
                                             (k0[:, 0:P], ident_b[:, :], strict_t_b[:, :]),
                                             (k1, ident_b[:, :], strict_t_b[:, :])):
                            pe.matmul(o, lhsT, rhs, start=False, stop=True, skip_group_check=True)

                def bank_pair(first):
                    return lambda h, blk: st[:, first * 512 + blk * 512 + h * HD:first * 512 + blk * 512 + (h + 1) * HD]

                def sb_and_mla_values():
                    pe_values([(prob, lambda kb, h: sb_v[:, kb, h * HD:(h + 1) * HD])], bank_pair(0))
                    pe_values([(probT, lambda kb, h: v_mla[:, kb, h * HD:(h + 1) * HD])], bank_pair(2))

                def nsa_scores(kv):
                    pe_scores(lambda h, blk: qkT[:, h, blk * P:(blk + 1) * P], lambda h: qkT[:, kv, :])

                def nsa_values():
                    for h in range(H):
                        for blk in range(TB):
                            o = bank_pair(0)(h, blk)
                            prods = [(pcT[0:NCMP, blk, h * P:(h + 1) * P], v_cmp[0:NCMP, :])]
                            for pT, v in ((pT_sel, v_sel), (pT_win, v_win)):
                                prods.append((pT[:, h * T + blk * P:h * T + (blk + 1) * P], v[:, 0, :]))
                                if blk == 1:
                                    prods.append((pT[:, 1024 + h * P:1024 + (h + 1) * P], v[:, 1, :]))
                            for i, (a, b) in enumerate(prods):
                                pe.matmul(o, a, b, start=i == 0, stop=i == len(prods) - 1, skip_group_check=True)

                def fox_all_scores():
                    for h in range(H):
                        o1, o0 = st[:, h * T:(h + 1) * T], st[:, 1024 + h * P:1024 + (h + 1) * P]
                        sp0 = fox_sp[:, h:h + 1].to_broadcast([P, P])
                        sp1 = fox_sp[:, 4 + h:5 + h].to_broadcast([P, P])
                        for o, lhsT, rhs, start in (
                                (o1, fox_qT[:, h, P:T], fox_kT[:, h, :], True),
                                (o1[:, 0:P], sp0, tri_up[:, :], False),
                                (o1[:, P:T], sp0, one.to_broadcast([P, P]), False),
                                (o1[:, P:T], sp1, tri_up[:, :], False),
                                (o1[:, P:T], ident_b[:, :], causal_b[:, :], False),
                                (o0, fox_qT[:, h, 0:P], fox_kT[:, h, 0:P], True),
                                (o0, sp0, tri_up[:, :], False),
                                (o0, ident_b[:, :], causal_b[:, :], False)):
                            pe.matmul(o, lhsT, rhs, start=start, stop=True, skip_group_check=True)
                stages = {
                    2: mla_turn_latents, 3: mla_queries_and_keys, 4: mla_values_and_ropes, 5: nsa_compress_hidden,
                    6: nsa_compress_out, 7: nsa_turn_compressed_keys, 8: mla_turn_ropes, 9: nsa_turn,
                    10: mla_scores, 11: lambda: turn_probs_and_compressed(prob, 0),
                    12: lambda: (sb_scores(), turn_probs_and_compressed(None, 1)), 13: sb_decays,
                    14: sb_and_mla_values, 15: lambda: nsa_scores(4), 16: lambda: pe_transpose_probs(prob),
                    17: lambda: nsa_scores(5), 18: lambda: pe_transpose_probs(prob), 19: nsa_values,
                    21: fox_all_scores, 22: lambda: pe_transpose_probs(prob),
                    23: lambda: pe_values([(probT, lambda kb, h: fox_v[:, kb, h * HD:(h + 1) * HD])], bank_pair(0)),
                    24: lambda: pe_turn_mix(o_mix["nsa"], 0), 25: lambda: pe_turn_mix(o_mix["sb"], 0),
                    26: lambda: pe_turn_mix(o_mix["fox"], 0), 28: lambda: pe_turn_mix(o_mix["mla"], 0),
                }
                n = 0
                for h, slot in enumerate(LAYER_SLOTS):
                    for unit in slot:
                        multiply(place, n, unit)
                        n += 1
                    pe_stage(place, h, stages.get(h, nothing))

            place = after(0, 0)
            pe_norm(place, "first2", xn2)
            pe.wait_ge(s("first2_operand"), 1)

            def turn_conv_weights():
                pe.wait_ge(block2_loads, 16 * BLOCK2_LOADS)
                for j in range(4):
                    pe.transpose(st[:, 1536 + j * TAPS:1536 + (j + 1) * TAPS], conv_raw[0:TAPS, j * P:(j + 1) * P],
                                 ident[0:TAPS, 0:TAPS])

            def turn_c_keys():
                for kv in range(2):
                    for tb in range(TB):
                        pe.transpose(st[:, kv * T + tb * P:kv * T + (tb + 1) * P], ckn[:, tb, kv, :], ident[:, :])

            def turn_pairs(src, bank):
                for j in range(4):
                    for tb in range(TB):
                        pe.transpose(st[:, bank * 512 + j * T + tb * P:bank * 512 + j * T + (tb + 1) * P],
                                     src[:, tb, j * P:(j + 1) * P], ident[:, :])

            def small_scores(qT, kT, first, mask):
                banks_begun = set()
                for parity in (0, 1):
                    for h in (parity, parity + 2):
                        j = first + h
                        half = slice(64 * parity, 64 * parity + 64)
                        for blk, c0, n in ((1, h * T, T), (0, 1024 + h * P, P)):
                            pe.matmul(st[:, c0:c0 + n], qT[half, j // 2, blk * P:(blk + 1) * P], kT(j)[half, 0:n],
                                      start=c0 // 512 not in banks_begun, stop=False, skip_group_check=True)
                            banks_begun.add(c0 // 512)
                    pe.drain()
                for h in range(4):
                    for blk, c0, n in ((1, h * T, T), (0, 1024 + h * P, P)):
                        lhsT, rhs = mask(blk)
                        pe.matmul(st[:, c0:c0 + n], lhsT, rhs, start=False, stop=True, skip_group_check=True)

            def c_mask(blk):
                return ident_b[:, :], (mask_c[:, 0:T] if blk else mask_c[:, T:T + P])

            def a_mask(blk):
                return ident[:, :], (log_count[:, 0:T] if blk else log_count[:, T:T + P])

            def small_values(first, v):
                for h in range(4):
                    j = first + h
                    for blk in range(TB):
                        o = st[:, 1536 + blk * 256 + h * 64:1536 + blk * 256 + (h + 1) * 64]
                        pe.matmul(o, probT2[:, h * T + blk * P:h * T + (blk + 1) * P], v(0, j), start=True,
                                  stop=blk == 0, skip_group_check=True)
                        if blk:
                            pe.matmul(o, probT2[:, 1024 + h * P:1024 + (h + 1) * P], v(1, j), start=False, stop=True,
                                      skip_group_check=True)

            def c_scores(group, first):
                small_scores(cqT, lambda j: ckT[:, group, :], first, c_mask)

            def c_values(group, first):
                small_values(first, lambda kb, j: cv[:, kb, 64 * group:64 * group + 64])

            def a_scores(first):
                small_scores(aqT, lambda j: akT[:, j // 2, :], first, a_mask)

            def a_values(first):
                small_values(first, lambda kb, j: av[:, kb, 64 * j:64 * j + 64])

            def sum_channels(src):
                for j in range(4):
                    pe.matmul(st[:, 1536:1536 + T], one.to_broadcast([P, P]), src[:, j, :], start=j == 0, stop=j == 3)

            def turn_probs2():
                pe_transpose_probs(prob2)
            stages2 = {
                1: turn_conv_weights, 2: turn_c_keys, 4: lambda: turn_pairs(cqn, 0), 5: lambda: c_scores(0, 0),
                6: turn_probs2, 7: lambda: (c_scores(0, 4), c_values(0, 0)), 8: turn_probs2,
                9: lambda: (turn_pairs(u, 0), c_values(0, 4)), 10: lambda: (turn_pairs(cqn, 0), turn_pairs(o_c[0], 2)),
                11: lambda: c_scores(1, 0), 12: turn_probs2, 13: lambda: (c_scores(1, 4), c_values(1, 0)),
                14: turn_probs2, 15: lambda: (turn_pairs(aqn, 0), c_values(1, 4)),
                16: lambda: (turn_pairs(akn, 0), turn_pairs(o_c[1], 2)),
                17: lambda: (a_scores(0), sum_channels(conv_y)), 18: lambda: (turn_probs2(), sum_channels(conv_sq)),
                19: lambda: (a_scores(4), a_values(0)), 20: turn_probs2, 21: lambda: a_values(4),
                22: lambda: turn_pairs(o_a, 0),
            }
            n = 0
            for h, slot in enumerate(SLOTS_2):
                for unit in slot:
                    multiply(place, n, unit, "mix2" if unit.operand == "mix" else None)
                    n += 1
                pe_stage(place, h, stages2.get(h, nothing))

            pe_norm(place, "second3", xn3)
            pe.wait_ge(s("second3_operand"), 1)

            def turn_act():
                pe_turn_mix(act_a, 0)

            def ffn_step(i, first):
                pl = ffn_place(i)
                for n, unit in enumerate(gate_up_units()):
                    multiply(pl, n, unit)
                    if n % SLOT_UNITS == SLOT_UNITS - 1:
                        h = n // SLOT_UNITS
                        pe_stage(pl, h, turn_act if h == 0 and not first else nothing)
            ffn_step(0, True)
            with pe.Fori(1, FFN_STEPS) as i:
                ffn_step(i, False)
            pe_stage(ffn_place(FFN_STEPS), 0, turn_act)
            pe.wait_ge(act_mid_done, down_place(0).slots + 1)
            pe.wait_ge(dve_mid_done, down_place(0).slots + 1)
            with pe.Fori(0, 2) as i:
                pl = down_place(i)
                for g in range(2):
                    for j, unit in enumerate(down_units(g)):
                        multiply(pl, g * 24 + j, unit)
                        if j % SLOT_UNITS == SLOT_UNITS - 1:
                            pe_stage(pl, g * DOWN_SLOTS + j // SLOT_UNITS, nothing)


        @block.scalar
        def _(act):
            act.sem_inc(act_mid_done, 1)
            act.wait_ge(x_loaded, 16)
            act.wait_ge(consts_loaded, 16 * N_CONSTS)

            def slots_with_mids(place, slots, mids):
                n = len(slots[0])
                for h in range(1, len(slots)):
                    for unit in slots[h]:
                        split_high(place, n, unit)
                        n += 1
                    act_mid(place, h - 1, mids.get(h - 1, nothing))
                act_mid(place, len(slots) - 1, mids.get(len(slots) - 1, nothing))

            with act.Fori(0, LAYERS) as l:
                place = in_layer(l)
                act_norm(place, "pre", xn, (dve_mid_done, place.slots + 1))
                for n, unit in enumerate(LAYER_SLOTS[0]):
                    split_high(place, n, unit)
                act_operand(place, "pre", place.once)

                def latent_squares():
                    act.wait_ge(s("latents"), place.once)
                    for tb in range(TB):
                        for i, (a, b) in enumerate(((0, 384), (384, 512))):
                            act.activation(st[:, tb * 512 + a:tb * 512 + b], c[:, tb, a:b], ACT.Square,
                                           accum_out=pow_in[:, 2 * tb + i:2 * tb + i + 1])
                    act.drain().then_inc(s("latent_sumsq"), 1)

                def latents_turned():
                    act.wait_ge(layer_loads, 16 * LAYER_LOADS * place.once)
                    for j in range(4):
                        act.activation(cT[:, j, :], st[:, j * T:(j + 1) * T], ACT.Copy,
                                       scale=q_norm[:, j:j + 1] if j < 3 else kv_norm)

                def scaled(dst, src, scale):
                    act.activation(dst, src, ACT.Copy, scale=scale)

                def hidden_exp():
                    act.activation(hid_e, st[:, 1536:1536 + 2 * NCMP], ACT.Exp, scale=-1.0)\
                        .then_inc(s("hidden_exp"), 1)

                def small_nonlinear():
                    act.wait_ge(s("small_group"), place.once)
                    act.activation(branch, branch, ACT.Exp, scale=-1.0)
                    act.activation(fox_sp, fox_u, ACT.Abs)
                    act.drain()
                    act.activation(fox_sp, fox_sp, ACT.Exp, scale=-1.0)
                    act.drain()
                    act.activation(fox_sp, fox_sp, ACT.Ln, bias=1.0)
                    act.drain().then_inc(s("small_nonlinear"), 1)

                def compressed_and_mla_softmax():
                    act.wait_ge(s("cmp_shifted"), place.once)
                    p = prob_c[:, :, :, :].rearrange("p b h n -> p (b h n)")
                    act.activation(p, p, ACT.Exp).then_inc(s("cmp_exp"), 1)
                    act_softmax(place, "mla", prob)

                def sb_softplus():
                    act.activation(prob[:, :], st[:, 0:1536], ACT.Abs)
                    act.drain()
                    act.activation(prob[:, :], prob[:, :], ACT.Exp, scale=-1.0)
                    act.drain()
                    act.activation(prob[:, :], prob[:, :], ACT.Ln, bias=1.0)
                    act.drain().then_inc(s("sb_softplus"), 1)
                    scaled(pcT[0:NCMP, 1, :], st[0:NCMP, 1536:2048], 1.0)

                def biased_features(pair, dst, b0):
                    for h in range(H):
                        act.activation(dst[:, h, :], accf[pair][:, h * T:(h + 1) * T], ACT.Identity,
                                       bias=col_bias[:, b0 + h:b0 + h + 1])

                def gate_exp(name):
                    act.wait_ge(s(name + "_gate"), place.once)
                    act.activation(gate_e[:, :, :], gate_z[:, :, :], ACT.Exp, scale=-1.0)\
                        .then_inc(s(name + "_gate_exp"), 1)

                def output_squares(g):
                    for tb in range(TB):
                        act.activation(st[:, tb * GN:(tb + 1) * GN], acc[g % 2][:, tb, :], ACT.Square,
                                       accum_out=den[:, 2 * g + tb:2 * g + tb + 1])
                    act.drain().then_inc(s("y_squares"), 1)

                def high(name, kt0):
                    return lambda: act_mix_high(place, name, mh, kt0, 0)
                slots_with_mids(place, LAYER_SLOTS, {
                    1: latent_squares, 2: latents_turned,
                    3: lambda: scaled(qnT[:, :, :].rearrange("p h t -> p (h t)"), st[:, 0:1024], MLA_SCALE),
                    4: lambda: scaled(v_mla[:, :, :].rearrange("p b n -> p (b n)"), st[:, 0:1024], 1.0),
                    5: hidden_exp,
                    7: small_nonlinear,
                    8: lambda: scaled(qrT[0:64, 0:4, :].rearrange("p h t -> p (h t)"), st[0:64, 0:1024], MLA_SCALE),
                    9: lambda: scaled(qkT[:, 0:4, :].rearrange("p h t -> p (h t)"), st[:, 0:1024], SCALE),
                    10: compressed_and_mla_softmax,
                    11: lambda: (act_copy_half(probT), scaled(pcT[0:NCMP, 0, :], st[0:NCMP, 1536:2048], 1.0),
                                 biased_features(1, sb_kT, 4)),
                    12: sb_softplus,
                    13: lambda: act.activation(prob[:, :], st[:, 0:1536], ACT.Exp),
                    15: lambda: act_softmax(place, "sel", prob),
                    16: lambda: act_copy_half(pT_sel),
                    17: lambda: (act_softmax(place, "win", prob), biased_features(0, fox_kT, 12)),
                    18: lambda: act_copy_half(pT_win),
                    21: lambda: (act_softmax(place, "fox", prob), gate_exp("nsa")),
                    22: lambda: act_copy_half(probT),
                    23: lambda: gate_exp("sb"), 24: high("nsa", NSA_KT),
                    25: lambda: (high("sb", SB_KT)(), gate_exp("fox")), 26: high("fox", FOX_KT),
                    27: lambda: gate_exp("mla"), 28: high("mla", MLA_KT),
                    29: lambda: output_squares(0), 31: lambda: output_squares(1), 33: lambda: output_squares(2),
                    35: lambda: output_squares(3),
                })

            place = after(0, 0)
            act_norm(place, "first2", xn2, (dve_mid_done, place.slots + 1))
            for n, unit in enumerate(SLOTS_2[0]):
                split_high(place, n, unit)
            act_operand(place, "first2", LAYERS + 1)

            def squares(pair, n):
                act.activation(tmp2[:, :, 0:n], acc[pair][:, :, 0:n], ACT.Square)

            def head_squares(name, pair, n):
                squares(pair, n)
                act.drain().then_inc(s(name + "_squares"), 1)

            def turned_scaled(dst, gain):
                act.activation(dst, st[:, 0:dst.free_size()], ACT.Copy, scale=gain)

            def softmax(name, sink=False):
                act_softmax(place, name, prob2)
                if sink:
                    act.activation(sink_e, sink_e, ACT.Exp).then_inc(s(name + "_sink"), 1)

            def conv_gate_exp():
                act.activation(tmp2[:, :, :], acc[1], ACT.Exp, scale=-1.0).then_inc(s("b_gate_exp2"), 1)

            def conv_input():
                act.activation(conv_h[:, :, PAD:PAD + T], st[:, 0:1024].rearrange("p (c t) -> p c t", c=4), ACT.Copy)\
                    .then_inc(s("conv_h2"), 1)

            def conv_square():
                act.wait_ge(s("conv_centred2"), 1)
                act.activation(conv_sq[:, :, :], conv_y[:, :, :], ACT.Square)

            def conv_silu():
                act.wait_ge(s("conv_normed2"), 1)
                act.activation(conv_sq[:, :, :], conv_sq[:, :, :], ACT.Exp, scale=-1.0).then_inc(s("conv_exp2"), 1)
                act.wait_ge(s("conv_out2"), 1)
                act.activation(mh2[:, 4:8, :], conv_y[:, :, :], ACT.Copy).then_inc(s("conv_high2"), 1)

            def flat(t):
                return t.rearrange("p a b -> p (a b)")
            slots_with_mids(place, SLOTS_2, {
                1: lambda: (head_squares("ck2", 0, 128),
                            act.activation(flat(conv_wT[:, :, :]), st[:, 1536:1536 + 4 * TAPS], ACT.Copy)),
                2: lambda: turned_scaled(flat(ckT[:, :, :]), gk_c),
                3: lambda: head_squares("cq02", 1, 512),
                4: lambda: turned_scaled(flat(cqT[:, :, :]), gq_c),
                5: lambda: softmax("c00", True), 6: lambda: act_copy_half(probT2),
                7: lambda: (conv_gate_exp(), softmax("c04", True)),
                8: lambda: act_copy_half(probT2),
                9: lambda: (conv_input(), head_squares("cq12", 0, 512)),
                10: lambda: (act_mix_high(place, "c0", mh2, 8, 2), turned_scaled(flat(cqT[:, :, :]), gq_c)),
                11: lambda: (head_squares("aq2", 1, 512), softmax("c10", True)),
                12: lambda: act_copy_half(probT2),
                13: lambda: (head_squares("ak2", 0, 512), softmax("c14", True)),
                14: lambda: act_copy_half(probT2),
                15: lambda: turned_scaled(flat(aqT[:, :, :]), gq_a),
                16: lambda: (act_mix_high(place, "c1", mh2, 12, 2), turned_scaled(flat(akT[:, :, :]), gk_a)),
                17: lambda: (softmax("a0"), conv_square()),
                18: lambda: (act_copy_half(probT2), conv_silu()),
                19: lambda: softmax("a4"), 20: lambda: act_copy_half(probT2),
                22: lambda: act_mix_high(place, "a", mh2, 0, 0),
            })

            act_norm(place, "second3", xn3, (dve_mid_done, place.slots + NSLOT_2 + 1))
            units = gate_up_units()
            for n in range(SLOT_UNITS):
                split_high(ffn_place(0), n, units[n])
            act_operand(place, "second3", LAYERS + 2)

            def act_turned(i):
                act.activation(flat(ah[:, :, :])[:, bass.ds((i - 1) * 1024, 1024)], st[:, 0:1024], ACT.Copy)\
                    .then_inc(ffn_high, 1)

            def gate_part(i):
                act.activation(flat(silu[:, :, :]), accf[0], ACT.Exp, scale=-1.0).then_inc(ffn_exp, 1)

            def ffn_step(i, first):
                pl = ffn_place(i)
                for h in range(4):
                    if not (first and h == 0):
                        for n in range(h * SLOT_UNITS, (h + 1) * SLOT_UNITS):
                            split_high(pl, n, units[n])
                    if h == 0 and not first:
                        act_mid(pl, -1, nothing)
                    elif h == 1:
                        act_mid(pl, 0, nothing if first else lambda: act_turned(i))
                    elif h == 2:
                        act_mid(pl, 1, lambda: gate_part(i))
                    elif h == 3:
                        act_mid(pl, 2, nothing)
            ffn_step(0, True)
            with act.Fori(1, FFN_STEPS) as i:
                ffn_step(i, False)
            act_mid(ffn_place(FFN_STEPS), -1, nothing)
            act_mid(ffn_place(FFN_STEPS), 0, lambda: act_turned(FFN_STEPS))
            with act.Fori(0, 2) as i:
                pl = down_place(i)
                for h in range(2 * DOWN_SLOTS):
                    for n in range(h * SLOT_UNITS, (h + 1) * SLOT_UNITS):
                        split_high(pl, n, down_units(n // 24)[n % 24])
                    if h:
                        act_mid(pl, h - 1, nothing)
                act_mid(pl, 2 * DOWN_SLOTS - 1, nothing)

        @block.vector
        def _(dve):
            def tt(out_, in0, in1, op):
                return dve.tensor_tensor(out=out_, in0=in0, in1=in1, op=op)

            def flat(t):
                return t.rearrange("p a b -> p (a b)")

            dve.sem_inc(lo_done, RAW_SLOTS)
            dve.sem_inc(dve_mid_done, 1)
            dve.memset(one, 1.0)
            dve.memset(minus_one, -1.0)
            dve.memset(minus_half, -0.5)
            dve.drain()
            dve.wait_ge(consts_loaded, 16 * N_CONSTS)

            def slots_with_mids(place, slots, mids):
                n = len(slots[0])
                for h in range(1, len(slots)):
                    for unit in slots[h]:
                        split_low(place, n, unit)
                        n += 1
                    dve_mid(place, h - 1, mids.get(h - 1, nothing))
                dve_mid(place, len(slots) - 1, mids.get(len(slots) - 1, nothing))

            def mean_square(dst, src, width):
                dve.tensor_scalar(out=dst, in0=src, scalar1=1.0 / width, scalar2=EPS, op0=ALU.mult, op1=ALU.add)

            def sigmoid_from_exp(e):
                dve.tensor_scalar(out=e, in0=e, scalar1=1.0, scalar2=None, op0=ALU.add)
                dve.drain()
                dve.reciprocal(e, e)
                dve.drain()

            with dve.Fori(0, LAYERS) as l:
                place = in_layer(l)
                dve_norm(place, "pre", xn)
                for n, unit in enumerate(LAYER_SLOTS[0]):
                    split_low(place, n, unit)
                dve_operand(place, "pre", place.once)
                bias_after = {}
                total = 0
                for i, g in enumerate(BIAS_GROUPS):
                    total += BIAS_DMAS[i]
                    bias_after[g] = total

                def biased(g, parts):
                    dve.wait_ge(bias_loaded, 16 * ((place.once - 1) * BIAS_TOTAL + bias_after[g]))
                    dve_evacuate_biased(g % 2, parts)

                def latents():
                    biased(0, [(0, 512, c[:, :, :])])
                    dve.drain().then_inc(s("latents"), 1)
                    dve.wait_ge(s("latent_sumsq"), place.once)
                    sums = pow_in[:, 0:4].rearrange("p (b i) -> p b i", i=2)
                    mean_square(sums[:, :, 0], sums[:, :, 0], 384)
                    mean_square(sums[:, :, 1], sums[:, :, 1], 128)
                    dve.drain().then_inc(s("mla_ms"), 1)
                    dve.wait_ge(s("mla_rstd"), place.once)
                    for tb in range(TB):
                        for i, (a, b) in enumerate(((0, 384), (384, 512))):
                            dve.tensor_scalar(out=c[:, tb, a:b], in0=c[:, tb, a:b],
                                              scalar1=rstd[:, 2 * tb + i:2 * tb + i + 1], scalar2=None, op0=ALU.mult)

                def keys_and_compressed_tokens():
                    dve.tensor_copy(flat(knT[:, :, :]), st[:, 1024:2048])
                    biased(1, [(0, 256, cmp_tok[:, :, :, :].rearrange("p b i c -> p b (i c)")),
                               (256, 128, rope_in[:, :, 4, :]), (384, 128, v_sel[:, :, :])])

                def compressed_blocks():
                    dve.tensor_copy(rope_in_m[:, :, 0:4, :].rearrange("p b h c -> p b (h c)"),
                                    st[:, 1024:1536].rearrange("p (b n) -> p b n", b=TB))
                    for i in range(2):
                        tok = st[:, 1536 + i * T:1536 + (i + 1) * T].rearrange("p (m b) -> p b m", b=CMP_STRIDE)
                        for a in range(2):
                            j = slice(a * CMP_STRIDE, (a + 1) * CMP_STRIDE)
                            tt(cmp_blk[:, i, j, :], tok[:, :, a:a + NCMP], bc(posT[:, i, j], NCMP), ALU.add)

                def hidden_silu():
                    dve.wait_ge(s("hidden_exp"), place.once)
                    sigmoid_from_exp(hid_e)
                    tt(hidT, st[:, 1536:1536 + 2 * NCMP], hid_e, ALU.mult)
                    biased(2, [(0, 512, rope_in[:, :, 0:4, :].rearrange("p b h c -> p b (h c)"))])

                def compressed_keys():
                    dve.tensor_copy(kc[0:NCMP, 0, :], st[0:NCMP, 1536:1536 + HD])
                    dve.tensor_copy(v_cmp[0:NCMP, :], st[0:NCMP, 1536 + HD:1536 + 2 * HD])
                    dve.drain()
                    dve_rope(kc[0:NCMP, 0:1, :], kc[0:NCMP, 1:2, :], kc[0:NCMP, 2:3, :], cos_c[0:NCMP, :],
                             sin_c[0:NCMP, :, :], 1, 64)

                def small_group():
                    dve.tensor_copy(kcT[:, :], st[:, 1536:1536 + NCMP])
                    b2 = branch.rearrange("p (b n) -> p b n", b=TB)
                    u2 = fox_u.rearrange("p (b n) -> p b n", b=TB)
                    biased(3, [(0, 128, rope_in[:, :, 5, :]), (128, 128, v_win[:, :, :]), (256, 12, b2),
                               (268, 4, u2), (272, 64, rope_in_m[:, :, 4, :])])
                    dve.drain()
                    tt(u2, u2, over(forget_b, TB), ALU.add)
                    dve.drain().then_inc(s("small_group"), 1)
                    for tb in range(TB):
                        tmp = qrT[:, 0:2, :].rearrange("p a t -> p (a t)")[:, 0:320].rearrange("p (h c) -> p h c", h=5)
                        dve_rope(rope_in_m[:, tb, :, :], rope_out_m[:, tb, :, :], tmp, cos_m[:, tb, :],
                                 sin_m[:, tb, :, :], 5, 32)
                    dve.wait_ge(s("small_nonlinear"), place.once)
                    dve.tensor_scalar(out=fox_u, in0=fox_u, scalar1=-1.0, scalar2=0.0, op0=ALU.mult, op1=ALU.max)
                    sigmoid_from_exp(branch)
                    tt(fox_sp, fox_sp, fox_u, ALU.add)
                    tt(gate_0.rearrange("p (b h) -> p b h", b=TB),
                       branch.rearrange("p (b h j) -> p b h j", b=TB, j=3)[:, :, :, 0], bc(row_ok, H), ALU.mult)

                def nsa_ropes():
                    dve.tensor_copy(qrT[0:64, 4, :], st[0:64, 1024:1280])
                    for tb in range(TB):
                        dve_rope(rope_in[:, tb, :, :], rope_out[:, tb, :, :], rope_tmp[:, :, :], cos_t[:, tb, :],
                                 sin_t[:, tb, :, :], 6, 64)

                def scaled_features(pair, dst, b0):
                    for h in range(H):
                        dve.tensor_scalar(out=dst[:, h, :], in0=accf[pair][:, h * T:(h + 1) * T],
                                          scalar1=col_bias[:, b0 + h:b0 + h + 1], scalar2=SCALE,
                                          op0=ALU.add, op1=ALU.mult)

                def nsa_turned():
                    dve.tensor_copy(flat(qkT[:, 4:6, :]), st[:, 1024:1536])
                    scaled_features(0, sb_qT, 0)

                def softmaxes_of_mla_and_compressed():
                    z = st[:, 1536:1536 + TB * H * NCMP].rearrange("p (a n) -> p a n", n=NCMP)
                    p = prob_c[:, :, :, :].rearrange("p b h n -> p (b h) n")
                    dve.tensor_reduce(out=cmp_max, in_=z, axis=AX, op=ALU.max)
                    dve.drain()
                    tt(p, z, bc(cmp_max, NCMP), ALU.subtract)
                    dve.drain().then_inc(s("cmp_shifted"), 1)
                    dve_softmax(place, "mla")
                    dve.wait_ge(s("cmp_exp"), place.once)
                    dve.tensor_reduce(out=cmp_den, in_=p, axis=AX, op=ALU.add)
                    dve.drain()
                    dve.reciprocal(cmp_den, cmp_den)
                    dve.drain()
                    tt(cmp_den, cmp_den, gate_0, ALU.mult)
                    dve.drain()
                    tt(p, p, bc(cmp_den, NCMP), ALU.mult)

                def sb_softplus():
                    dve.wait_ge(s("sb_softplus"), place.once)
                    dve.scalar_tensor_tensor(out=prob[:, :], in0=st[:, 0:1536], scalar=0.0, in1=prob[:, :],
                                             op0=ALU.max, op1=ALU.add)
                    dve.drain()
                    for tile in (prob[:, 0:1024].rearrange("p (h q) -> p h q", h=H)[:, :, 0:P],
                                 prob[:, 1024:1536].rearrange("p (h q) -> p h q", h=H)):
                        tt(tile, tile, over(keep_t_b[:, :], H), ALU.mult)

                def gate_probs(which):
                    f = factor.rearrange("p (b h) -> p b h", b=TB)
                    tt(f, f, branch.rearrange("p (b h j) -> p b h j", b=TB, j=3)[:, :, :, which], ALU.mult)
                    dve.drain()
                    p1 = prob[:, 0:1024].rearrange("p (h k) -> p h k", h=H)
                    p0 = prob[:, 1024:1536].rearrange("p (h k) -> p h k", h=H)
                    tt(p1, p1, bc(factor[:, 4:8], T), ALU.mult)
                    tt(p0, p0, bc(factor[:, 0:4], P), ALU.mult)

                def gate(name, g):
                    biased(g, [(0, 512, gate_z[:, :, :])])
                    dve.drain().then_inc(s(name + "_gate"), 1)
                    o = o_mix[name]
                    tt(o[:, :, :], o[:, :, :], gate_z[:, :, :], ALU.mult)
                    dve.wait_ge(s(name + "_gate_exp"), place.once)
                    sigmoid_from_exp(gate_e[:, :, :])
                    tt(o[:, :, :], o[:, :, :], gate_e[:, :, :], ALU.mult)

                def low(name, kt0):
                    dve_mix_low(place, name, mh, ml, kt0, 0)

                def output_group(g):
                    dve.wait_ge(s("y_squares"), 4 * (place.once - 1) + g + 1)
                    dve.wait_ge(post_g_loaded, 16 * place.once)
                    tt(y[:, :, g * GN:(g + 1) * GN], acc[g % 2], over(post_g[:, g * GN:(g + 1) * GN], TB), ALU.mult)

                def close_layer():
                    output_group(3)
                    dve.tensor_reduce(out=pow_in[:, 0:2], in_=den.rearrange("p (g b) -> p b g", b=TB), axis=AX,
                                      op=ALU.add)
                    dve.drain()
                    mean_square(pow_in[:, 0:2], pow_in[:, 0:2], DM)
                    dve.drain().then_inc(s("post_ms"), 1)
                    dve.wait_ge(s("post_rstd"), place.once)
                    for tb in range(TB):
                        dve.scalar_tensor_tensor(out=x[:, tb, :], in0=y[:, tb, :], scalar=rstd[:, tb:tb + 1],
                                                 in1=x[:, tb, :], op0=ALU.mult, op1=ALU.add)

                slots_with_mids(place, LAYER_SLOTS, {
                    1: latents,
                    2: lambda: dve.tensor_copy(flat(posT[:, :, :]), st[:, 1024:1024 + 2 * CMP_LEN]),
                    3: keys_and_compressed_tokens, 4: compressed_blocks, 5: hidden_silu, 6: compressed_keys,
                    7: small_group, 8: nsa_ropes, 9: nsa_turned, 10: softmaxes_of_mla_and_compressed,
                    11: lambda: dve_copy_half(probT), 12: sb_softplus,
                    13: lambda: biased(6, [(0, 512, sb_v[:, :, :])]),
                    14: lambda: (dve.tensor_copy(flat(o_mix["sb"][:, :, :]), st[:, 0:1024]),
                                 dve_scaled_out(o_mix["mla"], st[:, 1024:2048])),
                    15: lambda: (dve_softmax(place, "sel"), gate_probs(1), scaled_features(1, fox_qT, 8)),
                    16: lambda: dve_copy_half(pT_sel),
                    17: lambda: (dve_softmax(place, "win"), gate_probs(2)),
                    18: lambda: dve_copy_half(pT_win),
                    19: lambda: (dve.tensor_copy(flat(o_mix["nsa"][:, :, :]), st[:, 0:1024]),
                                 biased(9, [(0, 512, fox_v[:, :, :])])),
                    21: lambda: (dve_softmax(place, "fox"), gate("nsa", 10)),
                    22: lambda: dve_copy_half(probT),
                    23: lambda: (dve_scaled_out(o_mix["fox"], st[:, 0:1024]), gate("sb", 11)),
                    24: lambda: low("nsa", NSA_KT), 25: lambda: (low("sb", SB_KT), gate("fox", 12)),
                    26: lambda: low("fox", FOX_KT), 27: lambda: gate("mla", 13), 28: lambda: low("mla", MLA_KT),
                    29: lambda: output_group(0), 31: lambda: output_group(1), 33: lambda: output_group(2),
                    35: close_layer,
                })

            place = after(0, 0)
            dve_norm(place, "first2", xn2)
            for n, unit in enumerate(SLOTS_2[0]):
                split_low(place, n, unit)
            dve_operand(place, "first2", LAYERS + 1)
            dve.memset(conv_h[:, :, 0:PAD], 0.0)
            taps_at = {9: 2, 10: 4, 11: 3, 12: 6, 13: 4, 14: 6, 15: 3, 16: 3}
            assert sum(taps_at.values()) == TAPS
            done = [0]

            def head_norm(name, pair, n, dst):
                m = TB * n // 64
                dve.wait_ge(s(name + "_squares"), 1)
                dve.tensor_reduce(out=pow_in[:, 0:m].rearrange("p (b h) -> p b h", b=TB),
                                  in_=tmp2[:, :, 0:n].rearrange("p b (h c) -> p b h c", c=64), axis=AX, op=ALU.add)
                dve.drain()
                mean_square(pow_in[:, 0:m], pow_in[:, 0:m], 64)
                dve.drain().then_inc(s(name + "_ms"), 1)
                dve.wait_ge(s(name + "_rstd"), 1)
                for tb in range(TB):
                    tt(dst(tb), acc[pair][:, tb, 0:n].rearrange("p (h c) -> p h c", c=64),
                       bc(rstd[:, tb * m // 2:(tb + 1) * m // 2], 64), ALU.mult)

            def kv_group():
                dve.wait_ge(block2_loads, 16 * BLOCK2_LOADS)
                dve.tensor_scalar(out=neg_sinks, in0=sinks, scalar1=-1.0, scalar2=None, op0=ALU.mult)
                for g in (gq_c, gq_a):
                    dve.tensor_scalar(out=g, in0=g, scalar1=SCALE2, scalar2=None, op0=ALU.mult)
                head_norm("ck2", 0, 128, lambda tb: ckn[:, tb, :, 0:64])
                dve.tensor_copy(cv[:, :, :], acc[0][:, :, 128:256])
                dve.drain()
                dve.tensor_copy(ckn[:, :, :, 64:128], ckn[:, :, :, 0:64])

            def split_heads(t):
                return lambda tb: t[:, tb, :].rearrange("p (h c) -> p h c", c=64)

            def softmax_sinks(name, first):
                dve.tensor_reduce(out=neg_max[:, 4:8], in_=scores_1, axis=AX, op=ALU.max, negate=True)
                dve.tensor_reduce(out=neg_max[:, 0:4], in_=scores_0, axis=AX, op=ALU.max, negate=True)
                dve.drain()
                m = neg_max.rearrange("p (b h) -> p b h", b=TB)
                tt(m, m, over(neg_sinks[:, first:first + 4], TB), ALU.min)
                dve.drain()
                tt(sink_e.rearrange("p (b h) -> p b h", b=TB), m, over(sinks[:, first:first + 4], TB), ALU.add)
                dve.drain().then_inc(s(name + "_max"), 1)
                dve.wait_ge(s(name + "_exp"), 1)
                dve.wait_ge(s(name + "_sink"), 1)
                tt(den, den, sink_e, ALU.add)
                dve.drain()
                dve.reciprocal(factor, den)

            def small_out(o, first):
                for tb in range(TB):
                    tt(o[:, tb, first * 64:(first + 4) * 64].rearrange("p (h c) -> p h c", c=64),
                       st[:, 1536 + tb * 256:1536 + (tb + 1) * 256].rearrange("p (h c) -> p h c", c=64),
                       bc(factor[:, 4 * tb:4 * tb + 4], 64), ALU.mult)
                dve.drain()

            def conv_taps(h):
                dve.wait_ge(s("conv_h2"), 1)
                for j in range(done[0], done[0] + taps_at[h]):
                    for ct in range(4):
                        src, w = conv_h[:, ct, j:j + T], conv_wT[:, ct, j:j + 1]
                        if j == 0:
                            dve.tensor_scalar(out=conv_y[:, ct, :], in0=src, scalar1=w, scalar2=conv_b[:, ct:ct + 1],
                                              op0=ALU.mult, op1=ALU.add)
                        else:
                            dve.scalar_tensor_tensor(out=conv_y[:, ct, :], in0=src, scalar=w, in1=conv_y[:, ct, :],
                                                     op0=ALU.mult, op1=ALU.add)
                    dve.drain()
                done[0] += taps_at[h]

            def conv_gate():
                dve.wait_ge(s("b_gate_exp2"), 1)
                sigmoid_from_exp(tmp2[:, :, :])
                tt(u[:, :, :], u[:, :, :], tmp2[:, :, :], ALU.mult)
                dve.drain()

            def conv_centre():
                tt(conv_y[:, :, :], conv_y[:, :, :], over(conv_stat[:, 0, :], 4), ALU.subtract)
                dve.drain().then_inc(s("conv_centred2"), 1)

            def conv_finish():
                mean_square(conv_stat[:, 1, :], st[:, 1536:1536 + T], 512)
                dve.drain().then_inc(s("conv_var2"), 1)
                dve.wait_ge(s("conv_rstd2"), 1)
                tt(conv_y[:, :, :], conv_y[:, :, :], over(conv_stat[:, 2, :], 4), ALU.mult)
                dve.drain()
                for ct in range(4):
                    dve.tensor_scalar(out=conv_y[:, ct, :], in0=conv_y[:, ct, :], scalar1=ln_g[:, ct:ct + 1],
                                      scalar2=ln_b[:, ct:ct + 1], op0=ALU.mult, op1=ALU.add)
                dve.drain()
                dve.tensor_scalar(out=conv_sq[:, :, :], in0=conv_y[:, :, :], scalar1=-87.0, scalar2=None, op0=ALU.max)
                dve.drain().then_inc(s("conv_normed2"), 1)
                dve.wait_ge(s("conv_exp2"), 1)
                sigmoid_from_exp(conv_sq[:, :, :])
                tt(conv_y[:, :, :], conv_y[:, :, :], conv_sq[:, :, :], ALU.mult)
                dve.drain().then_inc(s("conv_out2"), 1)
                dve.wait_ge(s("conv_high2"), 1)
                tt(ml2[:, 4:8, :], conv_y[:, :, :], mh2[:, 4:8, :].bitcast(F32), ALU.subtract)

            def add_output(*groups):
                for g in groups:
                    cols_ = slice(g * GN, (g + 1) * GN)
                    tt(x[:, :, cols_], acc[g % 2], x[:, :, cols_], ALU.add)

            slots_with_mids(place, SLOTS_2, {
                1: kv_group,
                3: lambda: head_norm("cq02", 1, 512, split_heads(cqn)),
                5: lambda: (softmax_sinks("c00", 0), dve.tensor_copy(u[:, :, :], acc[0])),
                6: lambda: dve_copy_half(probT2),
                7: lambda: (small_out(o_c[0], 0), conv_gate(), softmax_sinks("c04", 4)),
                8: lambda: dve_copy_half(probT2),
                9: lambda: (small_out(o_c[0], 4), head_norm("cq12", 0, 512, split_heads(cqn)), conv_taps(9)),
                10: lambda: (dve_mix_low(place, "c0", mh2, ml2, 8, 2), conv_taps(10)),
                11: lambda: (head_norm("aq2", 1, 512, split_heads(aqn)), dve.drain(), softmax_sinks("c10", 8),
                             conv_taps(11)),
                12: lambda: (dve_copy_half(probT2), conv_taps(12)),
                13: lambda: (small_out(o_c[1], 0), head_norm("ak2", 0, 512, split_heads(akn)),
                             softmax_sinks("c14", 12), conv_taps(13)),
                14: lambda: (dve_copy_half(probT2), conv_taps(14)),
                15: lambda: (small_out(o_c[1], 4), dve.tensor_copy(av[:, :, :], acc[1]), conv_taps(15)),
                16: lambda: (dve_mix_low(place, "c1", mh2, ml2, 12, 2), conv_taps(16)),
                17: lambda: (dve.tensor_scalar(out=conv_stat[:, 0, :], in0=st[:, 1536:1536 + T], scalar1=1.0 / 512,
                                               scalar2=None, op0=ALU.mult), dve.drain(), conv_centre(),
                             dve_softmax(place, "a0")),
                18: lambda: (dve_copy_half(probT2), conv_finish()),
                19: lambda: (small_out(o_a, 0), dve_softmax(place, "a4")),
                20: lambda: dve_copy_half(probT2), 21: lambda: small_out(o_a, 4),
                22: lambda: dve_mix_low(place, "a", mh2, ml2, 0, 0),
                23: lambda: add_output(0, 1), 25: lambda: add_output(2), 27: lambda: add_output(3),
            })

            dve_norm(place, "second3", xn3)
            units = gate_up_units()
            for n in range(SLOT_UNITS):
                split_low(ffn_place(0), n, units[n])
            dve_operand(place, "second3", LAYERS + 2)

            def act_low(i):
                dve.wait_ge(ffn_high, i)
                part = bass.ds((i - 1) * 1024, 1024)
                tt(flat(al[:, :, :])[:, part], st[:, 0:1024], flat(ah[:, :, :])[:, part].bitcast(F32), ALU.subtract)

            def gate_part(i):
                dve.wait_ge(ffn_exp, i + 1)
                sigmoid_from_exp(silu[:, :, :])
                tt(silu[:, :, :], silu[:, :, :], acc[0], ALU.mult)

            def up_part():
                tt(act_a[:, :, :], silu[:, :, :], acc[1], ALU.mult)

            def ffn_step(i, first):
                pl = ffn_place(i)
                for h in range(4):
                    if not (first and h == 0):
                        for n in range(h * SLOT_UNITS, (h + 1) * SLOT_UNITS):
                            split_low(pl, n, units[n])
                    if h == 0 and not first:
                        dve_mid(pl, -1, up_part)
                    elif h == 1:
                        dve_mid(pl, 0, nothing if first else lambda: act_low(i))
                    elif h == 2:
                        dve_mid(pl, 1, lambda: gate_part(i))
                    elif h == 3:
                        dve_mid(pl, 2, nothing)
            ffn_step(0, True)
            with dve.Fori(1, FFN_STEPS) as i:
                ffn_step(i, False)
            dve_mid(ffn_place(FFN_STEPS), -1, up_part)
            dve_mid(ffn_place(FFN_STEPS), 0, lambda: act_low(FFN_STEPS))

            def down_out(i, g):
                part = bass.ds(i * (2 * GN) + g * GN, GN)
                tt(x[:, :, part], acc[g], x[:, :, part], ALU.add)
            with dve.Fori(0, 2) as i:
                pl = down_place(i)
                for h in range(2 * DOWN_SLOTS):
                    for n in range(h * SLOT_UNITS, (h + 1) * SLOT_UNITS):
                        split_low(pl, n, down_units(n // 24)[n % 24])
                    if h:
                        dve_mid(pl, h - 1, (lambda: down_out(i, 0)) if h == DOWN_SLOTS else nothing)
                dve_mid(pl, 2 * DOWN_SLOTS - 1, lambda: down_out(i, 1))


def constants():
    bf16 = mybir.dt.np(BF16)
    i, j = np.arange(P)[:, None], np.arange(P)[None, :]

    def rope(pos, half):
        inv = (np.float32(10000.0) ** (-np.arange(half, dtype=np.float32) / np.float32(half))).astype(np.float32)
        ang = pos.astype(np.float32)[:, None] * inv[None, :]
        co, si = np.cos(ang).astype(np.float32), np.sin(ang).astype(np.float32)
        return co, np.stack([-si, si], axis=1)

    def by_block(a):
        return np.ascontiguousarray(a.reshape(TB, P, *a.shape[1:]).swapaxes(0, 1))
    co, si = rope(np.arange(T), 64)
    com, sim = rope(np.arange(T), 32)
    ends = np.arange(NCMP) * CMP_STRIDE + CMP_LEN - 1
    coc, sic = rope(ends, 64)
    q = np.arange(T)
    cmp_mask = np.where(ends[None, :] <= q[:, None], 0.0, NEG)
    row_ok_ = (q >= ends[0]).astype(np.float32)
    dist1, dist0 = P + i - np.arange(T)[None, :], i - j
    dist = np.concatenate([dist1, dist0], axis=1)
    count = (dist <= 128).astype(int) + (dist % 4 == 0) + (dist % 16 == 0)
    count = np.where(dist >= 0, count, 0)
    return {
        "c_ident": np.eye(P, dtype=np.float32), "c_ident_b": np.eye(P).astype(bf16),
        "c_tri_up": (i <= j).astype(np.float32), "c_neg_tri": -(i >= j).astype(np.float32),
        "c_causal_b": np.where(j > i, NEG, 0.0).astype(bf16), "c_strict_t_b": np.where(i >= j, NEG, 0.0).astype(bf16),
        "c_keep_t_b": (i < j).astype(bf16), "c_cos": by_block(co), "c_sin": by_block(si),
        "c_cos_m": by_block(com), "c_sin_m": by_block(sim), "c_row_ok": np.ascontiguousarray(row_ok_.reshape(TB, P).T),
        "c_cmp_mask_b": by_block(cmp_mask).reshape(P, TB * NCMP).astype(bf16), "c_cos_c": coc, "c_sin_c": sic,
        "c_mask_c": np.where((dist >= 0) & (dist <= 127), 0.0, NEG).astype(bf16),
        "c_log_count": np.where(count > 0, np.log(np.maximum(count, 1)), NEG).astype(np.float32),
    }


_INS = ["x", "pre_norm_g", "post_norm_g", "w_in", "b_in", "w_out", "fox_forget_bias", "nsa_cmp_pos_k", "nsa_cmp_w1_k",
        "nsa_cmp_w2_k", "nsa_cmp_pos_v", "nsa_cmp_w1_v", "nsa_cmp_w2_v", "mla_q_norm_g", "mla_w_uq", "mla_kv_norm_g",
        "mla_w_ukv", "norm1_g_2", "w_in_2", "a_q_g_2", "a_k_g_2", "conv_w_2", "conv_b_2", "conv_ln_g_2",
        "conv_ln_b_2", "c_q_g_2", "c_k_g_2", "c_sinks_2", "w_out_2", "norm2_g_2", "w_gate_2", "w_up_2", "w_down_2"]


def kernel(**inputs):
    import concourse.bacc as _bacc
    from concourse.bass_utils import run_bass_kernel_spmd as _run

    nc = _bacc.Bacc("TRN2", target_bir_lowering=False, num_devices=1)
    arrays, aps = {}, {}
    given = {name: np.ascontiguousarray(inputs[name]) for name in _INS}
    for name, a in {**given, **constants()}.items():
        arrays[f"in_{name}_dram"] = a
        aps[name] = nc.dram_tensor(f"in_{name}_dram", a.shape, mybir.dt.from_np(a.dtype), kind="ExternalInput").ap()
    out = nc.dram_tensor("out_0_dram", (1, T, DM), F32, kind="ExternalOutput").ap()
    build(nc, aps, out.rearrange("a t n -> (a t) n"))
    r = _run(nc, [arrays], core_ids=[0])
    return r.results[0]["out_0_dram"]
```

```python
from contextlib import ExitStack

import numpy as np

import concourse.bass as bass
from concourse import mybir

P = 128
F32 = mybir.dt.float32
F32R = mybir.dt.float32r
BF16 = mybir.dt.bfloat16
ALU = mybir.AluOpType
ACT = mybir.ActivationFunctionType
AX = mybir.AxisListType.X

LAYERS = 2
DM = 2048
T = 256
TB = T // P
KT = DM // P
EPS = 1e-6
NEG = -1e30
H = 4
HD = 128
SCALE = HD ** -0.5
MLA_SCALE = (128 + 64) ** -0.5
CMP_LEN, CMP_STRIDE = 32, 16
NCMP = (T - CMP_LEN) // CMP_STRIDE + 1
SCALE2 = 64 ** -0.5
TAPS = 31
PAD = TAPS - 1
DFF = 5632

GN = 512
RAW_SLOTS = 4
SPLIT_SLOTS = 4
SLOT_UNITS = 4
QUARTERS = 4

GROUPS = (
    ("mla_c", ((5904, 512),), "t"),
    ("nsa_cmp_sel", ((2560, 512),), "t"),
    ("nsa_q", ((2048, 512),), "t"),
    ("nsa_win_small", ((3072, 268), (5388, 4), (6416, 64)), "t"),
    ("sb_q", ((0, 512),), "f"),
    ("sb_k", ((512, 512),), "f"),
    ("sb_v", ((1024, 512),), "t"),
    ("fox_q", ((3852, 512),), "f"),
    ("fox_k", ((4364, 512),), "f"),
    ("fox_v", ((4876, 512),), "t"),
    ("nsa_gate", ((3340, 512),), "t"),
    ("sb_gate", ((1536, 512),), "t"),
    ("fox_gate", ((5392, 512),), "t"),
    ("mla_gate", ((6480, 512),), "t"),
)
NG = len(GROUPS)
GROUPS_2 = (
    ("c_kv", ((3584, 256),), "t"),
    ("c_q0", ((2560, 512),), "t"),
    ("b_u", ((1536, 512),), "t"),
    ("b_gate", ((2048, 512),), "t"),
    ("c_q1", ((3072, 512),), "t"),
    ("a_q", ((0, 512),), "t"),
    ("a_k", ((512, 512),), "t"),
    ("a_v", ((1024, 512),), "t"),
)
NSA_KT, SB_KT, FOX_KT, MLA_KT = 4, 0, 8, 12


class Unit:

    def __init__(self, weight, pieces, kts, layout, pair, operand, ktiles, first, last):
        self.weight, self.pieces, self.kts, self.layout = weight, pieces, kts, layout
        self.pair, self.operand, self.ktiles, self.first, self.last = pair, operand, ktiles, first, last
        self.n = sum(w for _, w in pieces)
        self.after_mid = None


def slots_of(units):
    return [units[i:i + SLOT_UNITS] for i in range(0, len(units), SLOT_UNITS)]


def input_units(weight, groups):
    return [Unit(weight, pieces, (2 * j, 2 * j + 1), layout, g % 2, "x", KT, j == 0, j == KT // 2 - 1)
            for g, (_, pieces, layout) in enumerate(groups) for j in range(KT // 2)]


def output_unit(weight, g, pair, last_pair, first_pair=0):
    return Unit(weight, ((g * GN, GN),), (2 * pair, 2 * pair + 1), "t", g % 2, "mix", KT,
                pair == first_pair, pair == last_pair)


def output_slots():
    units = [output_unit("w_out", g, pair, 7) for g in range(DM // GN) for pair in range(8)]
    units[6].after_mid = NG * 2
    return slots_of(units)


def output_slots_2():
    def unit(g, pair):
        return output_unit("w_out_2", g, pair, 1, 4)
    rest = [output_unit("w_out_2", g, pair, 7) for g in (2, 3) for pair in range(8)]
    slots = [[unit(0, 4), unit(0, 5)], [], [unit(1, 4), unit(1, 5)], [unit(0, 6)], [unit(0, 7), unit(1, 6)], [],
             [unit(1, 7), unit(0, 2), unit(0, 3)], [unit(1, 2), unit(1, 3), unit(0, 0), unit(0, 1)],
             [unit(1, 0), unit(1, 1), rest[0], rest[1]]]
    slots[6][1].after_mid = 21
    slots[7][2].after_mid = 22
    slots[8][2].after_mid = 23
    return slots + slots_of(rest[2:])


LAYER_SLOTS = slots_of(input_units("w_in", GROUPS)) + output_slots()
WIN_SLOTS = NG * 2
NSLOT = len(LAYER_SLOTS)
LAYER_UNITS = sum(len(s) for s in LAYER_SLOTS)
SLOTS_2 = slots_of(input_units("w_in_2", GROUPS_2)) + output_slots_2()
WIN_SLOTS_2 = len(GROUPS_2) * 2
NSLOT_2 = len(SLOTS_2)
UNITS_2 = sum(len(s) for s in SLOTS_2)
FFN_STEPS = DFF // GN
FFN_KT = DFF // P
DOWN_KTS = [(2 * j, 2 * j + 1) for j in range(20)] + [(40 + j,) for j in range(4)]
DOWN_UNITS = len(DOWN_KTS)


def pages(base):
    kb = 1024
    at, off = {}, base

    def page(size, *names):
        nonlocal off
        for n in names:
            at[n] = off
        off += size
    page(16 * kb, "raw")
    page(16 * kb, "wh")
    page(16 * kb, "wl")
    page(16 * kb, "x")
    page(16 * kb, "xh")
    page(16 * kb, "xl")
    page(1024, "small")
    page(512, "ident")
    page(256, "ident_b")
    page(512, "tri_up")
    page(512, "neg_tri")
    page(256, "causal_b", )
    page(256, "strict_t_b")
    page(256, "keep_t_b")
    page(64, "cmp_mask_b")
    common_end = off
    page(16 * kb, "w1k", "mh")
    page(16 * kb, "w1v", "ml")
    at["xn"] = at["y"] = off
    at["rope_in_m"] = off
    at["rope_out_m"] = off + 2560
    at["qrT"] = off + 5120
    at["pcT"] = off
    at["pT_sel"] = off + 4 * kb
    at["pT_win"] = off + 10 * kb
    off += 16 * kb
    page(9 * kb, "w_uq", "post_g")
    page(6 * kb, "rope_in", "prob")
    page(6 * kb, "w_ukv", "rope_out", "probT")
    at["w2"] = off
    page(6 * kb, "rope_tmp", "qkT", "gate_z")
    page(4 * kb, "cT", "sb_qT", "fox_qT", "o_fox")
    page(4 * kb, "c", "cmp_tok", "sb_kT", "fox_kT", "gate_silu")
    page(4 * kb, "qnT", "sb_v", "fox_v")
    page(4 * kb, "knT", "o_sb")
    page(4 * kb, "v_mla", "o_nsa")
    page(4 * kb, "cmp_blk", "o_mla")
    page(2 * kb, "bias")
    page(1 * kb, "v_sel")
    page(1 * kb, "v_win")
    page(512, "cos")
    page(1024, "sin")
    page(256, "cos_m")
    page(512, "sin_m")
    page(480, "prob_c")
    page(64, "kcT")
    page(512, "v_cmp")
    page(256, "cos_c")
    page(512, "sin_c")
    layers_end = off
    off = common_end
    page(16 * kb, "mh2")
    page(16 * kb, "ml2")
    page(16 * kb, "xn2")
    page(6 * kb, "prob2")
    page(6 * kb, "probT2")
    page(4 * kb, "tmp2")
    page(4 * kb, "cqn")
    page(4 * kb, "aqn")
    page(4 * kb, "akn")
    page(4 * kb, "cqT")
    page(2 * kb, "ckT")
    page(1 * kb, "cv")
    page(2 * kb, "ckn")
    page(4 * kb, "av")
    page(4 * kb, "u")
    page(4 * kb, "conv_y")
    page(4 * (T + PAD) * 4, "conv_h")
    page(512, "conv_wT")
    page(768, "mask_c")
    page(1536, "log_count")
    page(4 * kb, "o_c0", "o_c1", "o_a")
    block2_end = off
    at["aqT"] = at["xn2"]
    at["akT"] = at["xn2"] + 4 * kb
    at["conv_sq"] = at["xn2"] + 8 * kb
    at["conv_stat"] = at["xn2"] + 12 * kb
    at["conv_raw"] = at["xn2"] + 8 * kb
    off = common_end
    page(44 * kb, "ah")
    page(44 * kb, "al")
    at["xn3"] = at["al"]
    page(4 * kb, "silu")
    page(4 * kb, "act")
    ffn_end = off
    return at, max(layers_end, block2_end, ffn_end)


def build(nc, d, out):
    with ExitStack() as ctx:
        at, end = pages(-(-nc.sbuf_base // 64) * 64)
        assert end <= nc.sbuf_usable_end, (end, nc.sbuf_usable_end)

        def sb(name, shape, dt=F32, where=None):
            return nc.alloc_sbuf_tensor_at(name, shape, dt, offset=at[where or name])

        def sem(name):
            return ctx.enter_context(nc.semaphore(name))

        raw = sb("raw", [P, RAW_SLOTS, 2, GN])
        wh = sb("wh", [P, SPLIT_SLOTS, 2, GN], F32R)
        wl = sb("wl", [P, SPLIT_SLOTS, 2, GN], F32R)
        x = sb("x", [P, TB, DM])
        xh = sb("xh", [P, KT, T], F32R)
        xl = sb("xl", [P, KT, T], F32R)
        small = sb("small", [P, 256])
        ident = sb("ident", [P, P])
        ident_b = sb("ident_b", [P, P], BF16)
        tri_up = sb("tri_up", [P, P])
        neg_tri = sb("neg_tri", [P, P])
        causal_b = sb("causal_b", [P, P], BF16)
        strict_t_b = sb("strict_t_b", [P, P], BF16)
        keep_t_b = sb("keep_t_b", [P, P], BF16)

        cursor = [0]

        def cols(n):
            cursor[0] += n
            assert cursor[0] <= 256
            return small[:, cursor[0] - n:cursor[0]]
        one, minus_one, eps, minus_half = cols(1), cols(1), cols(1), cols(1)
        sq_sums, rstd = cols(16), cols(16)
        norm_g = cols(16)
        assert cursor[0] <= 68, cursor[0]
        cursor[0] = 68
        neg_max, den, factor = cols(8), cols(8), cols(8)
        branch = cols(24)
        row_ok = cols(2)
        fox_u, fox_sp = cols(8), cols(8)
        forget_b = cols(4)
        q_norm, kv_norm = cols(3), cols(1)
        col_bias = cols(16)
        hidT = cols(2 * NCMP)
        cmp_max, cmp_den, gate_0 = cols(8), cols(8), cols(8)
        block2_cursor = cursor[0]
        cursor[0] = 92
        gq_c, gk_c, gq_a, gk_a = cols(1), cols(1), cols(1), cols(1)
        conv_b, ln_g, ln_b = cols(4), cols(4), cols(4)
        sinks, neg_sinks, sink_e = cols(16), cols(16), cols(8)
        cursor[0] = max(cursor[0], block2_cursor)

        mh, ml = sb("mh", [P, KT, T], F32R), sb("ml", [P, KT, T], F32R)
        w1 = [sb("w1k", [P, CMP_LEN, HD]), sb("w1v", [P, CMP_LEN, HD])]
        xn, y = sb("xn", [P, TB, DM]), sb("y", [P, TB, DM])
        rope_in_m, rope_out_m = sb("rope_in_m", [P, TB, 5, 64]), sb("rope_out_m", [P, TB, 5, 64])
        qrT = sb("qrT", [P, 5, T])
        pcT = sb("pcT", [P, TB, 512])
        pT_sel, pT_win = sb("pT_sel", [P, 1536]), sb("pT_win", [P, 1536])
        w_uq, post_g = sb("w_uq", [P, 3, 768]), sb("post_g", [P, DM])
        w_ukv = sb("w_ukv", [P, 1024])
        rope_in, prob = sb("rope_in", [P, TB, 6, HD]), sb("prob", [P, 1536])
        rope_out, probT = sb("rope_out", [P, TB, 6, HD]), sb("probT", [P, 1536])
        w2 = sb("w2", [P, 2, HD])
        rope_tmp, qkT, gate_z = sb("rope_tmp", [P, 6, HD]), sb("qkT", [P, 6, T]), sb("gate_z", [P, TB, 512])
        cT, sb_qT, fox_qT = sb("cT", [P, 4, T]), sb("sb_qT", [P, H, T]), sb("fox_qT", [P, H, T])
        c = sb("c", [P, TB, 512])
        cmp_tok, sb_kT, fox_kT = sb("cmp_tok", [P, TB, 2, HD]), sb("sb_kT", [P, H, T]), sb("fox_kT", [P, H, T])
        gate_silu = sb("gate_silu", [P, TB, 512])
        qnT, sb_v, fox_v = sb("qnT", [P, H, T]), sb("sb_v", [P, TB, 512]), sb("fox_v", [P, TB, 512])
        knT, v_mla = sb("knT", [P, H, T]), sb("v_mla", [P, TB, 512])
        cmp_blk = sb("cmp_blk", [P, 2, CMP_LEN, NCMP])
        o_mix = {"sb": sb("o_sb", [P, TB, 512]), "nsa": sb("o_nsa", [P, TB, 512]),
                 "fox": sb("o_fox", [P, TB, 512]), "mla": sb("o_mla", [P, TB, 512])}
        bias = sb("bias", [P, 512])
        v_sel, v_win = sb("v_sel", [P, TB, HD]), sb("v_win", [P, TB, HD])
        cos_t, sin_t = sb("cos", [P, TB, 64]), sb("sin", [P, TB, 2, 64])
        cos_m, sin_m = sb("cos_m", [P, TB, 32]), sb("sin_m", [P, TB, 2, 32])
        prob_c = sb("prob_c", [P, TB, H, NCMP])
        kc = nc.alloc_sbuf_tensor_at("kc", [P, 3, HD], F32, offset=at["y"] + 14 * 1024 + 512)
        kcT, v_cmp = sb("kcT", [P, NCMP]), sb("v_cmp", [P, HD])
        cos_c, sin_c = sb("cos_c", [P, 64]), sb("sin_c", [P, 2, 64])
        cmp_mask_b = sb("cmp_mask_b", [P, TB * NCMP], BF16)
        pos_in = nc.alloc_sbuf_tensor_at("pos_in", [P, 2, HD], F32, offset=at["y"] + 14 * 1024 + 512)
        posT = nc.alloc_sbuf_tensor_at("posT", [P, 2, CMP_LEN], F32, offset=at["y"] + 15 * 1024 + 512)

        mh2, ml2 = sb("mh2", [P, KT, T], F32R), sb("ml2", [P, KT, T], F32R)
        xn2 = sb("xn2", [P, TB, DM])
        prob2, probT2 = sb("prob2", [P, 1536]), sb("probT2", [P, 1536])
        tmp2 = sb("tmp2", [P, TB, 512])
        cqn, aqn, akn = sb("cqn", [P, TB, 512]), sb("aqn", [P, TB, 512]), sb("akn", [P, TB, 512])
        cqT, ckT, ckn, cv = sb("cqT", [P, 4, T]), sb("ckT", [P, 2, T]), sb("ckn", [P, TB, 2, P]), sb("cv", [P, TB, 128])
        av, u = sb("av", [P, TB, 512]), sb("u", [P, TB, 512])
        conv_y, conv_h = sb("conv_y", [P, 4, T]), sb("conv_h", [P, 4, PAD + T])
        conv_wT = sb("conv_wT", [P, 4, TAPS])
        mask_c = sb("mask_c", [P, 384], BF16)
        log_count = sb("log_count", [P, 384])
        o_c = [sb("o_c0", [P, TB, 512]), sb("o_c1", [P, TB, 512])]
        o_a = sb("o_a", [P, TB, 512])
        aqT, akT = sb("aqT", [P, 4, T]), sb("akT", [P, 4, T])
        conv_sq, conv_stat = sb("conv_sq", [P, 4, T]), sb("conv_stat", [P, 3, T])
        conv_raw = sb("conv_raw", [P, 512])
        ah, al = sb("ah", [P, FFN_KT, T], F32R), sb("al", [P, FFN_KT, T], F32R)
        xn3 = sb("xn3", [P, TB, DM])
        silu, act_a = sb("silu", [P, TB, 512]), sb("act", [P, TB, 512])

        psum = ctx.enter_context(nc.psum_tensor("psum", [P, 8, 512], F32))
        acc = [psum[:, 0:2, :], psum[:, 2:4, :]]
        accf = [a.rearrange("p b c -> p (b c)") for a in acc]
        st = psum[:, 4:8, :].rearrange("p b c -> p (b c)")
        all_banks = psum[:, :, :].rearrange("p b c -> p (b c)")

        raw_loaded = [sem(f"raw_loaded{i}") for i in range(RAW_SLOTS)]
        hi_done = sem("hi_done")
        lo_done = sem("lo_done")
        unit_used = sem("unit_used")
        stage_done = sem("stage_done")
        act_mid_done = sem("act_mid_done")
        dve_mid_done = sem("dve_mid_done")
        named = {}

        def s(name):
            if name not in named:
                named[name] = sem(name)
            return named[name]

        consts_loaded = sem("consts_loaded")
        masks_loaded = sem("masks_loaded")
        x_loaded = [sem(f"x_loaded{tb}") for tb in range(TB)]
        ident_loaded = sem("ident_loaded")
        x_ready = sem("x_ready")
        layer_loads = sem("layer_loads")
        w1_loaded = sem("w1_loaded")
        bias_loaded = sem("bias_loaded")
        post_g_loaded = sem("post_g_loaded")
        block2_loads = sem("block2_loads")
        out_stored = sem("out_stored")
        norm_g_loaded = sem("norm_g_loaded")
        ffn_high = sem("ffn_high")
        CONSTS = [(ident_b[:, :], "c_ident_b"), (tri_up[:, :], "c_tri_up"), (neg_tri[:, :], "c_neg_tri"),
                  (causal_b[:, :], "c_causal_b"), (strict_t_b[:, :], "c_strict_t_b"),
                  (keep_t_b[:, :], "c_keep_t_b"), (cos_t[:, :, :], "c_cos"), (sin_t[:, :, :, :], "c_sin"),
                  (cos_m[:, :, :], "c_cos_m"), (sin_m[:, :, :, :], "c_sin_m"), (row_ok, "c_row_ok"),
                  (cmp_mask_b[:, :], "c_cmp_mask_b"), (cos_c[0:NCMP, :], "c_cos_c"),
                  (sin_c[0:NCMP, :, :], "c_sin_c")]
        POOL_CONSTS = 7
        N_CONSTS = len(CONSTS) - POOL_CONSTS
        LAYER_LOADS = 3 + 4 + 2 + 2
        BLOCK2_LOADS = 8 + 3 + 3 + 1
        BIAS_GROUPS = [g for g, (_, _, layout) in enumerate(GROUPS) if layout == "t"]
        BIAS_DMAS = [len(GROUPS[g][1]) for g in BIAS_GROUPS]
        BIAS_TOTAL = sum(BIAS_DMAS)

        def rows(weight, l):
            if weight in ("w_in", "w_out"):
                return d[weight][bass.ds(l, 1), :, :].rearrange("a k n -> (a k) n")
            return d[weight][0, :, :]

        def weight_src(unit, l, c0, w):
            m = rows(unit.weight, l)
            if unit.operand == "x":
                v = m.rearrange("(p t) n -> p t n", t=KT)
            else:
                v = m.rearrange("(t p) n -> p t n", p=P)
            return v[:, unit.kts[0]:unit.kts[-1] + 1, c0:c0 + w]

        operands = {"x": (xh, xl), "mix": (mh, ml), "mix2": (mh2, ml2), "act": (ah, al)}

        class Place:

            def __init__(self, units, slots, loads, once, single):
                self.units, self.slots, self.loads, self.once, self.single = units, slots, loads, once, single

        loads_before = [[0] * RAW_SLOTS]
        n_units = 0
        for slot in LAYER_SLOTS:
            for unit in slot:
                row = list(loads_before[-1])
                row[n_units % RAW_SLOTS] += len(unit.pieces)
                loads_before.append(row)
                n_units += 1
        LAYER_PIECES = loads_before[-1]

        def in_layer(l):
            return Place(l * LAYER_UNITS, l * NSLOT, [l * q for q in LAYER_PIECES], l + 1, False)

        def after(units, slots):
            return Place(LAYERS * LAYER_UNITS + units, LAYERS * NSLOT + slots,
                         [LAYERS * q + units // RAW_SLOTS for q in LAYER_PIECES], 1, True)

        def pieces_loaded(place, n):
            within = n // RAW_SLOTS + 1 if place.single else loads_before[n + 1][n % RAW_SLOTS]
            return 16 * (place.loads[n % RAW_SLOTS] + within)

        wait_passed = {name: sem(f"{name}_wait_passed") for name in ("sp", "pe", "act", "dve", "pool")}

        def stand_alone(eng, name):
            eng.sem_inc(wait_passed[name], 1)

        def load_unit(sp, place, n, unit, src):
            sp.wait_ge(lo_done, place.units + n + 1)
            stand_alone(sp, "sp")
            off = 0
            for piece, (c0, w) in enumerate(unit.pieces):
                sp.dma_start(raw[:, n % RAW_SLOTS, 0:len(unit.kts), off:off + w], src(unit, c0, w))\
                    .then_inc(raw_loaded[n % RAW_SLOTS], 16)
                off += w

        def split_high(place, n, unit):
            act = nc.scalar
            act.wait_ge(raw_loaded[n % RAW_SLOTS], pieces_loaded(place, n))
            act.wait_ge(unit_used, place.units + n + 1)
            k = len(unit.kts)
            act.activation(wh[:, n % SPLIT_SLOTS, 0:k, 0:unit.n], raw[:, n % RAW_SLOTS, 0:k, 0:unit.n],
                           ACT.Copy).then_inc(hi_done, 1)

        def split_low(place, n, unit):
            dve = nc.vector
            dve.wait_ge(hi_done, place.units + n + 1)
            k = len(unit.kts)
            dve.tensor_tensor(out=wl[:, n % SPLIT_SLOTS, 0:k, 0:unit.n], in0=raw[:, n % RAW_SLOTS, 0:k, 0:unit.n],
                              in1=wh[:, n % SPLIT_SLOTS, 0:k, 0:unit.n].bitcast(F32),
                              op=ALU.subtract).then_inc(lo_done, 1)

        def multiply(place, n, unit, operand=None):
            pe = nc.tensor
            if unit.after_mid is not None:
                pe.wait_ge(act_mid_done, place.slots + unit.after_mid + 2)
                pe.wait_ge(dve_mid_done, place.slots + unit.after_mid + 2)
            pe.wait_ge(lo_done, RAW_SLOTS + place.units + n + 1)
            ah_, al_ = operands[operand or unit.operand]
            slot, out_ = n % SPLIT_SLOTS, acc[unit.pair]
            for kk, kt in enumerate(unit.kts):
                first = unit.first and kk == 0
                last = unit.last and kk == len(unit.kts) - 1
                hi_w, lo_w = wh[:, slot, kk, 0:unit.n], wl[:, slot, kk, 0:unit.n]
                if unit.layout == "t":
                    for tb in range(TB):
                        tok = slice(tb * P, (tb + 1) * P)
                        o = out_[:, tb, 0:unit.n]
                        pe.matmul(o, ah_[:, kt, tok], hi_w, start=first, stop=False)
                        pe.matmul(o, ah_[:, kt, tok], lo_w, start=False, stop=False)
                        ins = pe.matmul(o, al_[:, kt, tok], hi_w, start=False, stop=last)
                else:
                    for j in range(H):
                        o = accf[unit.pair][:, j * T:(j + 1) * T]
                        f = slice(j * P, (j + 1) * P)
                        pe.matmul(o, hi_w[:, f], ah_[:, kt, :], start=first and j % 2 == 0, stop=False,
                                  skip_group_check=True)
                        pe.matmul(o, lo_w[:, f], ah_[:, kt, :], start=False, stop=False, skip_group_check=True)
                        ins = pe.matmul(o, hi_w[:, f], al_[:, kt, :], start=False, stop=last,
                                        skip_group_check=True)
            ins.then_inc(unit_used, 1)

        def pe_stage(place, h, stage):
            pe = nc.tensor
            pe.wait_ge(act_mid_done, place.slots + h + 1)
            pe.wait_ge(dve_mid_done, place.slots + h + 1)
            stand_alone(pe, "pe")
            stage()
            pe.drain().then_inc(stage_done, 1)

        def act_mid(place, h, mid):
            act = nc.scalar
            act.wait_ge(stage_done, place.slots + h + 2)
            stand_alone(act, "act")
            mid()
            act.drain().then_inc(act_mid_done, 1)

        def dve_mid(place, h, mid):
            dve = nc.vector
            dve.wait_ge(stage_done, place.slots + h + 2)
            stand_alone(dve, "dve")
            mid()
            dve.drain().then_inc(dve_mid_done, 1)

        def nothing():
            pass

        def pe_scores(q, k, extra=None):
            pe = nc.tensor
            for h in range(4):
                for blk, o, n in ((1, st[:, h * 256:(h + 1) * 256], 256),
                                  (0, st[:, 1024 + h * P:1024 + (h + 1) * P], P)):
                    parts = [(q(h, blk), k(h)[:, 0:n])] + (extra(h, blk, n) if extra else [])
                    for i, (lhsT, rhs) in enumerate(parts):
                        pe.matmul(o, lhsT, rhs, start=i == 0, stop=False, skip_group_check=True)
                    pe.matmul(o[:, n - P:n], ident_b[:, :], causal_b[:, :], start=False, stop=True,
                              skip_group_check=True)

        def pe_transpose_probs(p):
            pe = nc.tensor
            for h in range(4):
                for src, dst in ((1024 + h * P, h * 256), (h * 256, h * 256 + P), (h * 256 + P, 1024 + h * P)):
                    pe.transpose(st[:, dst:dst + P], p[:, src:src + P], ident[:, :])

        def pe_values(terms, o, width=HD):
            pe = nc.tensor
            for h in range(4):
                for blk in range(TB):
                    prods = []
                    for pT, v in terms:
                        prods.append((pT[:, h * 256 + blk * P:h * 256 + (blk + 1) * P], v(0, h)))
                        if blk == 1:
                            prods.append((pT[:, 1024 + h * P:1024 + (h + 1) * P], v(1, h)))
                    for i, (a, b) in enumerate(prods):
                        pe.matmul(o(h, blk), a, b, start=i == 0, stop=i == len(prods) - 1, skip_group_check=True)

        scores_1 = st[:, 0:1024].rearrange("p (h k) -> p h k", h=4)
        scores_0 = st[:, 1024:1536].rearrange("p (h k) -> p h k", h=4)

        def act_softmax(place, name, p):
            act = nc.scalar
            act.wait_ge(s(name + "_max"), place.once)
            for blk, base, n in ((0, 1024, P), (1, 0, 256)):
                for h in range(4):
                    ins = act.activation(p[:, base + h * n:base + (h + 1) * n], st[:, base + h * n:base + (h + 1) * n],
                                         ACT.Exp, bias=neg_max[:, blk * 4 + h:blk * 4 + h + 1],
                                         accum_out=den[:, blk * 4 + h:blk * 4 + h + 1])
            act.drain().then_inc(s(name + "_exp"), 1)

        def dve_softmax_max(place, name):
            dve = nc.vector
            dve.tensor_reduce(out=neg_max[:, 4:8], in_=scores_1, axis=AX, op=ALU.max, negate=True)
            dve.tensor_reduce(out=neg_max[:, 0:4], in_=scores_0, axis=AX, op=ALU.max, negate=True)
            dve.drain().then_inc(s(name + "_max"), 1)

        def dve_softmax_sum(place, name):
            dve = nc.vector
            dve.wait_ge(s(name + "_exp"), place.once)
            dve.reciprocal(factor, den)
            dve.drain()

        def dve_softmax(place, name):
            dve_softmax_max(place, name)
            dve_softmax_sum(place, name)

        def act_copy_half(dst):
            nc.scalar.activation(dst[:, 0:1024], st[:, 0:1024], ACT.Copy)

        def dve_copy_half(dst):
            nc.vector.tensor_copy(dst[:, 1024:1536], st[:, 1024:1536])

        def bc(ap, n):
            return ap.unsqueeze(2).to_broadcast([ap.shape[0], ap.shape[1], n])

        def over(ap, m):
            return ap.unsqueeze(1).to_broadcast([ap.shape[0], m, ap.shape[1]])

        def heads(ap, n):
            return ap.rearrange("p b (h c) -> p (b h) c", c=n)

        def dve_scaled_out(dst, src):
            nc.vector.tensor_tensor(out=heads(dst[:, :, :], HD), in0=src.rearrange("p (n c) -> p n c", c=HD),
                                    in1=bc(factor, HD), op=ALU.mult)

        def dve_evacuate_biased(pair, parts):
            for c0, w, dst in parts:
                nc.vector.tensor_tensor(out=dst, in0=acc[pair][:, :, c0:c0 + w], in1=over(bias[:, c0:c0 + w], TB),
                                        op=ALU.add)

        def dve_rope(src, dst, tmp, cos, sin, m, half, parts=P):
            dve = nc.vector
            s4 = src.rearrange("p m (a c) -> p m a c", a=2)
            t4 = tmp.rearrange("p m (a c) -> p m a c", a=2)
            dve.tensor_tensor(out=dst.rearrange("p m (a c) -> p (m a) c", a=2),
                              in0=src.rearrange("p m (a c) -> p (m a) c", a=2), in1=over(cos, 2 * m), op=ALU.mult)
            dve.tensor_tensor(out=t4[:, :, 0, :], in0=s4[:, :, 1, :], in1=over(sin[:, 0, :], m), op=ALU.mult)
            dve.tensor_tensor(out=t4[:, :, 1, :], in0=s4[:, :, 0, :], in1=over(sin[:, 1, :], m), op=ALU.mult)
            dve.drain()
            dve.tensor_tensor(out=dst, in0=dst, in1=tmp, op=ALU.add)
            dve.drain()

        def act_rstd(out_, sums, width):
            act = nc.scalar
            act.activation(out_, sums, ACT.Ln, scale=1.0 / width, bias=eps)
            act.drain()
            act.activation(out_, out_, ACT.Exp, scale=-0.5)

        def dve_refine_rstd(y, sums, scratch, width):
            dve = nc.vector
            dve.tensor_scalar(out=scratch, in0=sums, scalar1=1.0 / width, scalar2=EPS, op0=ALU.mult, op1=ALU.add)
            dve.drain()
            for _ in range(2):
                dve.tensor_tensor(out=scratch, in0=scratch, in1=y, op=ALU.mult)
                dve.drain()
            dve.tensor_scalar(out=scratch, in0=scratch, scalar1=-0.5, scalar2=1.5, op0=ALU.mult, op1=ALU.add)
            dve.drain()
            dve.tensor_tensor(out=y, in0=y, in1=scratch, op=ALU.mult)
            dve.drain()

        def pool_rstd(count, name, parts):
            pool = nc.gpsimd
            pool.wait_ge(s(name + "_sums"), count)
            stand_alone(pool, "pool")
            for part, width in parts:
                pool.tensor_scalar(out=sq_sums[:, part], in0=sq_sums[:, part], scalar1=1.0 / width, scalar2=EPS,
                                   op0=ALU.mult, op1=ALU.add).then_inc(s(name + "_ms"), 1)
            pool.wait_ge(s(name + "_ms"), count * len(parts))
            stand_alone(pool, "pool")
            lo_, hi_ = min(part.start for part, _ in parts), max(part.stop for part, _ in parts)
            pool.tensor_tensor(out=rstd[:, lo_:hi_], in0=sq_sums[:, lo_:hi_],
                               in1=minus_half.to_broadcast([P, hi_ - lo_]), op=ALU.pow).then_inc(s(name + "_rstd"), 1)

        def pool_norm(place, name):
            for tb in range(TB):
                pool_rstd(TB * (place.once - 1) + tb + 1, name, [(slice(tb, tb + 1), DM)])

        DVE_TILES, POOL_TILES = (0, 1, 2), (3,)

        def conv_taps(eng, tiles, a, b):
            for j in range(a, b):
                for ct in tiles:
                    src, w = conv_h[:, ct, j:j + T], conv_wT[:, ct, j:j + 1]
                    if j == 0:
                        eng.tensor_scalar(out=conv_y[:, ct, :], in0=src, scalar1=w, scalar2=conv_b[:, ct:ct + 1],
                                          op0=ALU.mult, op1=ALU.add)
                    elif eng is nc.vector:
                        eng.scalar_tensor_tensor(out=conv_y[:, ct, :], in0=src, scalar=w, in1=conv_y[:, ct, :],
                                                 op0=ALU.mult, op1=ALU.add)
                    else:
                        product = conv_sq[:, 2 * (j % 2) + ct % 2, :]
                        eng.tensor_scalar(out=product, in0=src, scalar1=w, scalar2=None, op0=ALU.mult)
                eng.drain()
                if eng is not nc.vector and j:
                    for ct in tiles:
                        eng.tensor_tensor(out=conv_y[:, ct, :], in0=conv_y[:, ct, :],
                                          in1=conv_sq[:, 2 * (j % 2) + ct % 2, :], op=ALU.add)

        def act_norm(place, name, buf, x_updates):
            act = nc.scalar
            for tb in range(TB):
                act.wait_ge(x_ready, x_updates + tb + 1)
                act.activation(buf[:, tb, :], x[:, tb, :], ACT.Square, accum_out=sq_sums[:, tb:tb + 1])
                act.drain().then_inc(s(name + "_sums"), 1)

        def dve_norm(place, name, buf):
            dve = nc.vector
            for tb in range(TB):
                dve.wait_ge(s(name + "_rstd"), TB * (place.once - 1) + tb + 1)
                dve.tensor_scalar(out=buf[:, tb, :], in0=x[:, tb, :], scalar1=rstd[:, tb:tb + 1],
                                  scalar2=None, op0=ALU.mult).then_inc(s(name + "_scaled"), 1)

        def pe_norm(place, name, buf):
            pe = nc.tensor
            for tb in range(TB):
                pe.wait_ge(s(name + "_scaled"), TB * (place.once - 1) + tb + 1)
                for kt in range(KT):
                    pe.transpose(all_banks[:, kt * T + tb * P:kt * T + (tb + 1) * P],
                                 buf[:, tb, :].rearrange("p (c t) -> p t c", t=KT)[:, kt, :], ident[:, :])
                    if tb == TB - 1 and kt % (KT // QUARTERS) == KT // QUARTERS - 1:
                        pe.drain().then_inc(s(name + "_turned"), 1)

        def act_operand(place, name, gains):
            act = nc.scalar
            act.wait_ge(norm_g_loaded, 16 * gains)
            for q in range(QUARTERS):
                act.wait_ge(s(name + "_turned"), QUARTERS * (place.once - 1) + q + 1)
                for kt in range(q * KT // QUARTERS, (q + 1) * KT // QUARTERS):
                    ins = act.activation(xh[:, kt, :], all_banks[:, kt * T:(kt + 1) * T], ACT.Copy,
                                         scale=norm_g[:, kt:kt + 1])
                ins.then_inc(s(name + "_high"), 1)

        def dve_operand(place, name, gains):
            dve = nc.vector
            dve.wait_ge(norm_g_loaded, 16 * gains)
            for q in range(QUARTERS):
                dve.wait_ge(s(name + "_high"), QUARTERS * (place.once - 1) + q + 1)
                for kt in range(q * KT // QUARTERS, (q + 1) * KT // QUARTERS):
                    ins = dve.scalar_tensor_tensor(out=xl[:, kt, :], in0=all_banks[:, kt * T:(kt + 1) * T],
                                                   scalar=norm_g[:, kt:kt + 1], in1=xh[:, kt, :].bitcast(F32),
                                                   op0=ALU.mult, op1=ALU.subtract)
                ins.then_inc(s(name + "_operand"), 1)

        def pe_first_operand(place, name, n):
            if n < KT // 2 and n % (KT // 2 // QUARTERS) == 0:
                q = n // (KT // 2 // QUARTERS)
                nc.tensor.wait_ge(s(name + "_operand"), QUARTERS * (place.once - 1) + q + 1)

        def pe_turn_mix(o, bank):
            pe = nc.tensor
            for j in range(4):
                for tb in range(TB):
                    pe.transpose(st[:, bank * 512 + j * T + tb * P:bank * 512 + j * T + (tb + 1) * P],
                                 o[:, tb, j * P:(j + 1) * P], ident[:, :])

        def act_mix_high(place, name, hi, kt0, bank):
            nc.scalar.activation(hi[:, kt0:kt0 + 4, :].rearrange("p k t -> p (k t)"),
                                 st[:, bank * 512:bank * 512 + 1024], ACT.Copy).then_inc(s(name + "_mix_high"), 1)

        def dve_mix_low(place, name, hi, lo, kt0, bank):
            nc.vector.wait_ge(s(name + "_mix_high"), place.once)
            nc.vector.tensor_tensor(out=lo[:, kt0:kt0 + 4, :].rearrange("p k t -> p (k t)"),
                                    in0=st[:, bank * 512:bank * 512 + 1024],
                                    in1=hi[:, kt0:kt0 + 4, :].rearrange("p k t -> p (k t)").bitcast(F32),
                                    op=ALU.subtract)

        FFN_UNITS, FFN_SLOTS = 16, 3
        FFN_SLOT_ENDS = (4, 8, 16)

        def ffn_place(i):
            a = after(UNITS_2, NSLOT_2)
            return Place(a.units + i * FFN_UNITS, a.slots + i * FFN_SLOTS,
                         [q + i * (FFN_UNITS // RAW_SLOTS) for q in a.loads], 1, True)

        def down_place(i):
            a = after(UNITS_2 + FFN_STEPS * FFN_UNITS, NSLOT_2 + FFN_STEPS * FFN_SLOTS + 1)
            return Place(a.units + i * 2 * DOWN_UNITS, a.slots + i * 2,
                         [q + i * (2 * DOWN_UNITS // RAW_SLOTS) for q in a.loads], 1, True)

        def gate_up_units():
            return [Unit(w, ((0, GN),), (2 * j, 2 * j + 1), "t", i, "x", KT, j == 0, j == KT // 2 - 1)
                    for i, w in enumerate(("w_gate_2", "w_up_2")) for j in range(KT // 2)]

        def down_units(g):
            return [Unit("w_down_2", ((0, GN),), kts, "t", g, "act", FFN_KT, j == 0, j == 23)
                    for j, kts in enumerate(DOWN_KTS)]

        block = ctx.enter_context(nc.Block())

        @block.sync
        def _(sp):
            def layer_src(l):
                return lambda unit, c0, w: weight_src(unit, l, c0, w)
            for tb in range(TB):
                sp.dma_start(x[:, tb, :], d["x"][0, tb * P:(tb + 1) * P, :]).then_inc(x_loaded[tb], 16)
            sp.dma_start(ident[:, :], d["c_ident"]).then_inc(ident_loaded, 16)
            for dst, name in CONSTS[POOL_CONSTS:]:
                sp.dma_start(dst, d[name]).then_inc(consts_loaded, 16)
            with sp.Fori(0, LAYERS) as l:
                place, n = in_layer(l), 0
                for slot in LAYER_SLOTS:
                    for unit in slot:
                        load_unit(sp, place, n, unit, layer_src(l))
                        n += 1
            place, n = after(0, 0), 0
            for slot in SLOTS_2:
                for unit in slot:
                    load_unit(sp, place, n, unit, layer_src(0))
                    n += 1
            with sp.Fori(0, FFN_STEPS) as i:
                place = ffn_place(i)
                for n, unit in enumerate(gate_up_units()):
                    load_unit(sp, place, n, unit, lambda unit, c0, w: rows(unit.weight, 0).rearrange(
                        "(p t) n -> p t n", t=KT)[:, unit.kts[0]:unit.kts[-1] + 1, bass.ds(i * GN, GN)])
            with sp.Fori(0, 2) as i:
                place = down_place(i)
                for g in range(2):
                    for j, unit in enumerate(down_units(g)):
                        load_unit(sp, place, g * DOWN_UNITS + j, unit, lambda unit, c0, w: rows(unit.weight, 0).rearrange(
                            "(t p) n -> p t n", p=P)[:, unit.kts[0]:unit.kts[-1] + 1,
                                                     bass.ds(i * (2 * GN) + g * GN, GN)])
            sp.wait_ge(out_stored, 16 * 4)

        @block.gpsimd
        def _(pool):
            def load(dst, src, signal):
                pool.dma_start(dst, src, allow_slow_non_contiguous=True).then_inc(signal, 16)
            for dst, name in CONSTS[:POOL_CONSTS]:
                load(dst, d[name], masks_loaded)
            with pool.Fori(0, LAYERS) as l:
                place = in_layer(l)

                def row(name):
                    return d[name][bass.ds(l, 1), :]

                def mat(name):
                    return d[name][bass.ds(l, 1), :, :].rearrange("a k n -> (a k) n")
                pool_norm(place, "pre")
                pool.wait_ge(act_mid_done, place.slots + 1)
                pool.wait_ge(dve_mid_done, place.slots + 1)
                pool.wait_ge(stage_done, place.slots + 1)
                load(norm_g, row("pre_norm_g").rearrange("a (p t) -> (a p) t", t=KT), norm_g_loaded)
                load(q_norm, row("mla_q_norm_g").rearrange("a (t p) -> p (a t)", p=P), layer_loads)
                load(kv_norm, row("mla_kv_norm_g").rearrange("a (t p) -> p (a t)", p=P), layer_loads)
                load(forget_b, row("fox_forget_bias").to_broadcast([P, 4]), layer_loads)
                for i, c0 in enumerate((0, 512, 3852, 4364)):
                    load(col_bias[:, 4 * i:4 * i + 4],
                         row("b_in")[:, c0:c0 + 512].rearrange("a (t p) -> p (a t)", p=P), layer_loads)
                load(w_uq[:, :, :], mat("mla_w_uq").rearrange("(t p) n -> p t n", p=P), layer_loads)
                load(w_ukv[:, :], mat("mla_w_ukv"), layer_loads)

                def load_bias(i):
                    off = 0
                    for c0, w in GROUPS[BIAS_GROUPS[i]][1]:
                        load(bias[:, off:off + w], row("b_in")[:, c0:c0 + w].to_broadcast([P, w]), bias_loaded)
                        off += w
                load_bias(0)
                load(w1[0][:, :, :], mat("nsa_cmp_w1_k").rearrange("(j p) n -> p j n", p=P), w1_loaded)
                load(w1[1][:, :, :], mat("nsa_cmp_w1_v").rearrange("(j p) n -> p j n", p=P), w1_loaded)
                load(w2[:, 0, :], mat("nsa_cmp_w2_k"), w1_loaded)
                load(w2[:, 1, :], mat("nsa_cmp_w2_v"), w1_loaded)
                pool.wait_ge(s("pre_turned"), QUARTERS * place.once)
                load(pos_in[0:CMP_LEN, 0, :], mat("nsa_cmp_pos_k"), layer_loads)
                load(pos_in[0:CMP_LEN, 1, :], mat("nsa_cmp_pos_v"), layer_loads)
                pool_rstd(place.once, "mla", [(slice(2 * tb + i, 2 * tb + i + 1), width) for tb in range(TB)
                                              for i, width in ((0, 384), (1, 128))])
                for i in range(1, len(BIAS_GROUPS)):
                    pool.wait_ge(dve_mid_done, place.slots + 2 * BIAS_GROUPS[i - 1] + 3)
                    load_bias(i)
                    if BIAS_GROUPS[i] == 6:
                        load(post_g[:, :], row("post_norm_g").to_broadcast([P, DM]), post_g_loaded)

                pool_rstd(place.once, "post", [(slice(0, TB), DM)])

            place = after(0, 0)
            def head_rstd(name, n):
                pool_rstd(1, name, [(slice(0, n), 64)])
            pool_norm(place, "first2")
            pool.wait_ge(act_mid_done, place.slots + 1)
            pool.wait_ge(dve_mid_done, place.slots + 1)
            pool.wait_ge(stage_done, place.slots + 1)
            load(norm_g, d["norm1_g_2"][0:1, :].rearrange("a (p t) -> (a p) t", t=KT), norm_g_loaded)
            for half in (0, 64):
                for dst, name in ((gq_c, "c_q_g_2"), (gk_c, "c_k_g_2"), (gq_a, "a_q_g_2"), (gk_a, "a_k_g_2")):
                    load(dst[half:half + 64, :], d[name][0:1, :].rearrange("a n -> n a"), block2_loads)
            for dst, name in ((conv_b, "conv_b_2"), (ln_g, "conv_ln_g_2"), (ln_b, "conv_ln_b_2")):
                load(dst, d[name][0:1, :].rearrange("a (t p) -> p (a t)", p=P), block2_loads)
            load(sinks, d["c_sinks_2"][0:1, :].to_broadcast([P, 16]), block2_loads)
            load(mask_c[:, :], d["c_mask_c"], block2_loads)
            load(log_count[:, :], d["c_log_count"], block2_loads)
            pool.wait_ge(s("first2_turned"), QUARTERS)
            load(conv_raw[0:TAPS, :], d["conv_w_2"][0, :, :], block2_loads)
            pool.wait_ge(s("first2_operand"), QUARTERS)
            load(norm_g, d["norm2_g_2"][0:1, :].rearrange("a (p t) -> (a p) t", t=KT), norm_g_loaded)
            head_rstd("ck2", 4)
            head_rstd("cq02", 16)
            head_rstd("cq12", 16)
            pool.wait_ge(s("conv_h2"), 1)
            conv_taps(pool, POOL_TILES, 0, 8)
            head_rstd("aq2", 16)
            conv_taps(pool, POOL_TILES, 8, 21)
            head_rstd("ak2", 16)
            conv_taps(pool, POOL_TILES, 21, TAPS)
            pool.drain().then_inc(s("conv_pool2"), 1)
            pool_norm(place, "second3")
            with pool.Fori(0, 2) as i:
                for g in range(2):
                    pool.wait_ge(dve_mid_done, down_place(i).slots + g + 2)
                    pool.dma_start(out[:, bass.ds(i * (2 * GN) + g * GN, GN)].rearrange("(b p) n -> p b n", p=P),
                                   x[:, :, bass.ds(i * (2 * GN) + g * GN, GN)]).then_inc(out_stored, 16)

        @block.tensor
        def _(pe):
            pe.sem_inc(unit_used, SPLIT_SLOTS)
            pe.sem_inc(stage_done, 1)
            pe.wait_ge(ident_loaded, 16)

            with pe.Fori(0, LAYERS) as l:
                place = in_layer(l)
                pe_norm(place, "pre", xn)

                def mla_turn_latents():
                    pe.wait_ge(consts_loaded, 16 * N_CONSTS)
                    pe.wait_ge(masks_loaded, 16 * POOL_CONSTS)
                    for j in range(4):
                        for tb in range(TB):
                            pe.transpose(st[:, j * T + tb * P:j * T + (tb + 1) * P], c[:, tb, j * P:(j + 1) * P],
                                         ident[:, :])
                    pe.wait_ge(layer_loads, 16 * LAYER_LOADS * place.once)
                    stand_alone(pe, "pe")
                    for i in range(2):
                        pe.transpose(st[:, 1024 + 32 * i:1024 + 32 * (i + 1)], pos_in[0:CMP_LEN, i, :],
                                     ident[0:CMP_LEN, 0:CMP_LEN])

                def mla_queries_and_keys():
                    for h in range(H):
                        for t in range(3):
                            pe.matmul(st[:, h * T:(h + 1) * T], w_uq[:, t, h * 192:h * 192 + 128], cT[:, t, :],
                                      start=t == 0, stop=t == 2, skip_group_check=True)
                        pe.matmul(st[:, 1024 + h * T:1024 + (h + 1) * T], w_ukv[:, h * 256:h * 256 + 128],
                                  cT[:, 3, :], start=True, stop=True, skip_group_check=True)

                def mla_values_and_ropes():
                    v_cols = w_ukv[:, :].rearrange("p (h c) -> p h c", h=H)[:, :, 128:256]
                    for tb in range(TB):
                        tok = slice(tb * P, (tb + 1) * P)
                        pe.matmul(st[:, tb * 512:(tb + 1) * 512], cT[:, 3, tok], v_cols, start=True, stop=True)
                        for t in range(3):
                            rope_cols = w_uq[:, t, :].rearrange("p (h c) -> p h c", h=H)[:, :, 128:192]
                            pe.matmul(st[:, 1024 + tb * 256:1024 + (tb + 1) * 256], cT[:, t, tok], rope_cols,
                                      start=t == 0, stop=t == 2, skip_group_check=True)
                    for i in range(2):
                        for tb in range(TB):
                            pe.transpose(st[:, 1536 + i * T + tb * P:1536 + i * T + (tb + 1) * P],
                                         cmp_tok[:, tb, i, :], ident[:, :])

                def nsa_compress_hidden():
                    pe.wait_ge(w1_loaded, 64 * place.once)
                    for i in range(2):
                        for j in range(CMP_LEN):
                            pe.matmul(st[:, 1536 + i * NCMP:1536 + (i + 1) * NCMP], w1[i][:, j, :], cmp_blk[:, i, j, :],
                                      start=j == 0, stop=j == CMP_LEN - 1, skip_group_check=True)

                def nsa_compress_out():
                    for i in range(2):
                        pe.matmul(st[0:NCMP, 1536 + i * HD:1536 + (i + 1) * HD], hidT[:, i * NCMP:(i + 1) * NCMP],
                                  w2[:, i, :], start=True, stop=True, skip_group_check=True)

                def nsa_turn_compressed_keys():
                    pe.transpose(st[:, 1536:1536 + NCMP], kc[0:NCMP, 1, :], ident[0:NCMP, 0:NCMP])

                def mla_turn_ropes():
                    for j in range(5):
                        for tb in range(TB):
                            pe.transpose(st[0:64, j * T + tb * P:j * T + (tb + 1) * P], rope_out_m[:, tb, j, :],
                                         ident[:, :])

                def nsa_turn():
                    for j in range(6):
                        for tb in range(TB):
                            pe.transpose(st[:, j * T + tb * P:j * T + (tb + 1) * P], rope_out[:, tb, j, :], ident[:, :])

                def mla_scores():
                    def rope_part(h, blk, n):
                        return [(qrT[0:64, h, blk * P:(blk + 1) * P], qrT[0:64, 4, 0:n])]
                    pe_scores(lambda h, blk: qnT[:, h, blk * P:(blk + 1) * P], lambda h: knT[:, h, :], rope_part)
                    for blk in range(TB):
                        for h in range(H):
                            o = st[:, 1536 + (blk * H + h) * NCMP:1536 + (blk * H + h + 1) * NCMP]
                            pe.matmul(o, qkT[:, h, blk * P:(blk + 1) * P], kcT[:, :],
                                      start=True, stop=False, skip_group_check=True)
                            pe.matmul(o, ident_b[:, :], cmp_mask_b[:, blk * NCMP:(blk + 1) * NCMP], start=False,
                                      stop=True, skip_group_check=True)

                def turn_probs_and_compressed(p, blk):
                    if p is not None:
                        pe_transpose_probs(p)
                    for h in range(H):
                        pe.transpose(st[0:NCMP, 1536 + h * P:1536 + (h + 1) * P], prob_c[:, blk, h, :], ident[:, :])

                def sb_scores():
                    for h in range(H):
                        pe.matmul(st[:, h * T:(h + 1) * T], sb_kT[:, h, 0:P], sb_qT[:, h, :],
                                  start=h % 2 == 0, stop=True, skip_group_check=True)
                        pe.matmul(st[:, 1024 + h * P:1024 + (h + 1) * P], sb_kT[:, h, P:T], sb_qT[:, h, P:T],
                                  start=h == 0, stop=True, skip_group_check=True)

                def sb_decays():
                    for h in range(H):
                        k0, k1 = st[:, h * T:(h + 1) * T], st[:, 1024 + h * P:1024 + (h + 1) * P]
                        sp1 = prob[:, 1024 + h * P:1024 + (h + 1) * P]
                        for o, lhsT, rhs in ((k0, neg_tri[:, :], prob[:, h * T:(h + 1) * T]),
                                             (k0[:, P:T], minus_one.to_broadcast([P, P]), sp1),
                                             (k1, neg_tri[:, :], sp1),
                                             (k0[:, 0:P], ident_b[:, :], strict_t_b[:, :]),
                                             (k1, ident_b[:, :], strict_t_b[:, :])):
                            pe.matmul(o, lhsT, rhs, start=False, stop=True, skip_group_check=True)

                def bank_pair(first):
                    return lambda h, blk: st[:, first * 512 + blk * 512 + h * HD:first * 512 + blk * 512 + (h + 1) * HD]

                def sb_and_mla_values():
                    pe_values([(prob, lambda kb, h: sb_v[:, kb, h * HD:(h + 1) * HD])], bank_pair(0))
                    pe_values([(probT, lambda kb, h: v_mla[:, kb, h * HD:(h + 1) * HD])], bank_pair(2))

                def nsa_scores(kv):
                    pe_scores(lambda h, blk: qkT[:, h, blk * P:(blk + 1) * P], lambda h: qkT[:, kv, :])

                def nsa_values():
                    for h in range(H):
                        for blk in range(TB):
                            o = bank_pair(0)(h, blk)
                            prods = [(pcT[0:NCMP, blk, h * P:(h + 1) * P], v_cmp[0:NCMP, :])]
                            for pT, v in ((pT_sel, v_sel), (pT_win, v_win)):
                                prods.append((pT[:, h * T + blk * P:h * T + (blk + 1) * P], v[:, 0, :]))
                                if blk == 1:
                                    prods.append((pT[:, 1024 + h * P:1024 + (h + 1) * P], v[:, 1, :]))
                            for i, (a, b) in enumerate(prods):
                                pe.matmul(o, a, b, start=i == 0, stop=i == len(prods) - 1, skip_group_check=True)

                def fox_all_scores():
                    for h in range(H):
                        o1, o0 = st[:, h * T:(h + 1) * T], st[:, 1024 + h * P:1024 + (h + 1) * P]
                        sp0 = fox_sp[:, h:h + 1].to_broadcast([P, P])
                        sp1 = fox_sp[:, 4 + h:5 + h].to_broadcast([P, P])
                        for o, lhsT, rhs, start in (
                                (o1, fox_qT[:, h, P:T], fox_kT[:, h, :], True),
                                (o1[:, 0:P], sp0, tri_up[:, :], False),
                                (o1[:, P:T], sp0, one.to_broadcast([P, P]), False),
                                (o1[:, P:T], sp1, tri_up[:, :], False),
                                (o1[:, P:T], ident_b[:, :], causal_b[:, :], False),
                                (o0, fox_qT[:, h, 0:P], fox_kT[:, h, 0:P], True),
                                (o0, sp0, tri_up[:, :], False),
                                (o0, ident_b[:, :], causal_b[:, :], False)):
                            pe.matmul(o, lhsT, rhs, start=start, stop=True, skip_group_check=True)
                stages = {
                    2: mla_turn_latents, 3: mla_queries_and_keys, 4: mla_values_and_ropes, 5: nsa_compress_hidden,
                    6: nsa_compress_out, 7: nsa_turn_compressed_keys, 8: mla_turn_ropes, 9: nsa_turn,
                    10: mla_scores, 11: lambda: turn_probs_and_compressed(prob, 0),
                    12: lambda: (sb_scores(), turn_probs_and_compressed(None, 1)), 13: sb_decays,
                    14: sb_and_mla_values, 15: lambda: nsa_scores(4), 16: lambda: pe_transpose_probs(prob),
                    17: lambda: nsa_scores(5), 18: lambda: pe_transpose_probs(prob), 19: nsa_values,
                    21: fox_all_scores, 22: lambda: pe_transpose_probs(prob),
                    23: lambda: pe_values([(probT, lambda kb, h: fox_v[:, kb, h * HD:(h + 1) * HD])], bank_pair(0)),
                    24: lambda: pe_turn_mix(o_mix["nsa"], 0), 25: lambda: pe_turn_mix(o_mix["sb"], 0),
                    26: lambda: pe_turn_mix(o_mix["fox"], 0), 28: lambda: pe_turn_mix(o_mix["mla"], 0),
                }
                n = 0
                for h, slot in enumerate(LAYER_SLOTS):
                    for unit in slot:
                        pe_first_operand(place, "pre", n)
                        multiply(place, n, unit)
                        n += 1
                    pe_stage(place, h, stages.get(h, nothing))

            place = after(0, 0)
            pe_norm(place, "first2", xn2)

            def turn_conv_weights():
                pe.wait_ge(block2_loads, 16 * BLOCK2_LOADS)
                for j in range(4):
                    pe.transpose(st[:, 1536 + j * TAPS:1536 + (j + 1) * TAPS], conv_raw[0:TAPS, j * P:(j + 1) * P],
                                 ident[0:TAPS, 0:TAPS])

            def turn_c_keys():
                for kv in range(2):
                    for tb in range(TB):
                        pe.transpose(st[:, kv * T + tb * P:kv * T + (tb + 1) * P], ckn[:, tb, kv, :], ident[:, :])

            def turn_pairs(src, bank):
                for j in range(4):
                    for tb in range(TB):
                        pe.transpose(st[:, bank * 512 + j * T + tb * P:bank * 512 + j * T + (tb + 1) * P],
                                     src[:, tb, j * P:(j + 1) * P], ident[:, :])

            def small_scores(qT, kT, first, mask):
                banks_begun = set()
                for parity in (0, 1):
                    for h in (parity, parity + 2):
                        j = first + h
                        half = slice(64 * parity, 64 * parity + 64)
                        for blk, c0, n in ((1, h * T, T), (0, 1024 + h * P, P)):
                            pe.matmul(st[:, c0:c0 + n], qT[half, j // 2, blk * P:(blk + 1) * P], kT(j)[half, 0:n],
                                      start=c0 // 512 not in banks_begun, stop=False, skip_group_check=True)
                            banks_begun.add(c0 // 512)
                    pe.drain()
                for h in range(4):
                    for blk, c0, n in ((1, h * T, T), (0, 1024 + h * P, P)):
                        lhsT, rhs = mask(blk)
                        pe.matmul(st[:, c0:c0 + n], lhsT, rhs, start=False, stop=True, skip_group_check=True)

            def c_mask(blk):
                return ident_b[:, :], (mask_c[:, 0:T] if blk else mask_c[:, T:T + P])

            def a_mask(blk):
                return ident[:, :], (log_count[:, 0:T] if blk else log_count[:, T:T + P])

            def small_values(first, v):
                for h in range(4):
                    j = first + h
                    for blk in range(TB):
                        o = st[:, 1536 + blk * 256 + h * 64:1536 + blk * 256 + (h + 1) * 64]
                        pe.matmul(o, probT2[:, h * T + blk * P:h * T + (blk + 1) * P], v(0, j), start=True,
                                  stop=blk == 0, skip_group_check=True)
                        if blk:
                            pe.matmul(o, probT2[:, 1024 + h * P:1024 + (h + 1) * P], v(1, j), start=False, stop=True,
                                      skip_group_check=True)

            def c_scores(group, first):
                small_scores(cqT, lambda j: ckT[:, group, :], first, c_mask)

            def c_values(group, first):
                small_values(first, lambda kb, j: cv[:, kb, 64 * group:64 * group + 64])

            def a_scores(first):
                small_scores(aqT, lambda j: akT[:, j // 2, :], first, a_mask)

            def a_values(first):
                small_values(first, lambda kb, j: av[:, kb, 64 * j:64 * j + 64])

            def sum_channels(src):
                pe.wait_ge(s("conv_pool2"), 1)
                for j in range(4):
                    pe.matmul(st[:, 1536:1536 + T], one.to_broadcast([P, P]), src[:, j, :], start=j == 0, stop=j == 3)

            def turn_probs2():
                pe_transpose_probs(prob2)
            stages2 = {
                1: turn_conv_weights, 2: turn_c_keys, 4: lambda: turn_pairs(cqn, 0), 5: lambda: c_scores(0, 0),
                6: turn_probs2, 7: lambda: (c_scores(0, 4), c_values(0, 0)), 8: turn_probs2,
                9: lambda: (turn_pairs(u, 0), c_values(0, 4)), 10: lambda: (turn_pairs(cqn, 0), turn_pairs(o_c[0], 2)),
                11: lambda: c_scores(1, 0), 12: turn_probs2, 13: lambda: (c_scores(1, 4), c_values(1, 0)),
                14: turn_probs2, 15: lambda: (turn_pairs(aqn, 0), c_values(1, 4)),
                16: lambda: (turn_pairs(akn, 0), turn_pairs(o_c[1], 2)),
                17: lambda: (a_scores(0), sum_channels(conv_y)), 18: lambda: (turn_probs2(), sum_channels(conv_sq)),
                19: lambda: (a_scores(4), a_values(0)), 20: turn_probs2, 21: lambda: a_values(4),
                22: lambda: turn_pairs(o_a, 0),
            }
            n = 0
            for h, slot in enumerate(SLOTS_2):
                for unit in slot:
                    pe_first_operand(place, "first2", n)
                    multiply(place, n, unit, "mix2" if unit.operand == "mix" else None)
                    n += 1
                pe_stage(place, h, stages2.get(h, nothing))

            pe_norm(place, "second3", xn3)

            def turn_act():
                pe_turn_mix(act_a, 0)

            def ffn_step(i, first):
                pl = ffn_place(i)
                for n, unit in enumerate(gate_up_units()):
                    if first:
                        pe_first_operand(after(0, 0), "second3", n)
                    multiply(pl, n, unit)
                    if n + 1 in FFN_SLOT_ENDS:
                        h = FFN_SLOT_ENDS.index(n + 1)
                        pe_stage(pl, h, turn_act if h == 0 and not first else nothing)
            ffn_step(0, True)
            with pe.Fori(1, FFN_STEPS) as i:
                ffn_step(i, False)
            pe_stage(ffn_place(FFN_STEPS), 0, turn_act)
            pe.wait_ge(act_mid_done, down_place(0).slots + 1)
            pe.wait_ge(dve_mid_done, down_place(0).slots + 1)
            with pe.Fori(0, 2) as i:
                pl = down_place(i)
                for g in range(2):
                    for j, unit in enumerate(down_units(g)):
                        multiply(pl, g * DOWN_UNITS + j, unit)
                    pe_stage(pl, g, nothing)


        @block.scalar
        def _(act):
            act.sem_inc(act_mid_done, 1)
            def slots_with_mids(place, slots, mids):
                n = len(slots[0])
                for h in range(1, len(slots)):
                    for unit in slots[h]:
                        split_high(place, n, unit)
                        n += 1
                    act_mid(place, h - 1, mids.get(h - 1, nothing))
                act_mid(place, len(slots) - 1, mids.get(len(slots) - 1, nothing))

            with act.Fori(0, LAYERS) as l:
                place = in_layer(l)
                act_norm(place, "pre", xn, TB * (place.once - 1))
                for n, unit in enumerate(LAYER_SLOTS[0]):
                    split_high(place, n, unit)
                act_operand(place, "pre", place.once)

                def latent_squares():
                    act.wait_ge(s("latents"), place.once)
                    for tb in range(TB):
                        for i, (a, b) in enumerate(((0, 384), (384, 512))):
                            act.activation(st[:, tb * 512 + a:tb * 512 + b], c[:, tb, a:b], ACT.Square,
                                           accum_out=sq_sums[:, 2 * tb + i:2 * tb + i + 1])
                    act.drain().then_inc(s("mla_sums"), 1)

                def latents_turned():
                    act.wait_ge(layer_loads, 16 * LAYER_LOADS * place.once)
                    for j in range(4):
                        act.activation(cT[:, j, :], st[:, j * T:(j + 1) * T], ACT.Copy,
                                       scale=q_norm[:, j:j + 1] if j < 3 else kv_norm)

                def scaled(dst, src, scale):
                    act.activation(dst, src, ACT.Copy, scale=scale)

                def hidden_silu():
                    act.activation(hidT, st[:, 1536:1536 + 2 * NCMP], ACT.Silu)

                def small_nonlinear():
                    act.wait_ge(s("small_group"), place.once)
                    act.activation(branch, branch, ACT.Sigmoid)
                    act.activation(fox_sp, fox_u, ACT.Abs)
                    act.drain()
                    act.activation(fox_sp, fox_sp, ACT.Exp, scale=-1.0)
                    act.drain()
                    act.activation(fox_sp, fox_sp, ACT.Ln, bias=1.0)
                    act.drain().then_inc(s("small_nonlinear"), 1)

                def compressed_and_mla_softmax():
                    act.wait_ge(s("cmp_shifted"), place.once)
                    p = prob_c[:, :, :, :].rearrange("p b h n -> p (b h n)")
                    act.activation(p, p, ACT.Exp).then_inc(s("cmp_exp"), 1)
                    act_softmax(place, "mla", prob)

                def sb_softplus():
                    act.activation(prob[:, :], st[:, 0:1536], ACT.Abs)
                    act.drain()
                    act.activation(prob[:, :], prob[:, :], ACT.Exp, scale=-1.0)
                    act.drain()
                    act.activation(prob[:, :], prob[:, :], ACT.Ln, bias=1.0)
                    act.drain().then_inc(s("sb_softplus"), 1)
                    scaled(pcT[0:NCMP, 1, :], st[0:NCMP, 1536:2048], 1.0)

                def biased_features(pair, dst, b0):
                    for h in range(H):
                        act.activation(dst[:, h, :], accf[pair][:, h * T:(h + 1) * T], ACT.Identity,
                                       bias=col_bias[:, b0 + h:b0 + h + 1])

                def act_gate(name):
                    act.wait_ge(s(name + "_gate"), place.once)
                    act.activation(gate_silu[:, :, :], gate_z[:, :, :], ACT.Silu)\
                        .then_inc(s(name + "_gate_silu"), 1)

                def output_squares(g):
                    for tb in range(TB):
                        act.activation(st[:, tb * GN:(tb + 1) * GN], acc[g % 2][:, tb, :], ACT.Square,
                                       accum_out=den[:, 2 * g + tb:2 * g + tb + 1])
                    act.drain().then_inc(s("y_squares"), 1)

                def high(name, kt0):
                    return lambda: act_mix_high(place, name, mh, kt0, 0)
                slots_with_mids(place, LAYER_SLOTS, {
                    1: latent_squares, 2: latents_turned,
                    3: lambda: scaled(qnT[:, :, :].rearrange("p h t -> p (h t)"), st[:, 0:1024], MLA_SCALE),
                    4: lambda: scaled(v_mla[:, :, :].rearrange("p b n -> p (b n)"), st[:, 0:1024], 1.0),
                    5: hidden_silu,
                    7: small_nonlinear,
                    8: lambda: scaled(qrT[0:64, 0:4, :].rearrange("p h t -> p (h t)"), st[0:64, 0:1024], MLA_SCALE),
                    9: lambda: scaled(qkT[:, 0:4, :].rearrange("p h t -> p (h t)"), st[:, 0:1024], SCALE),
                    10: compressed_and_mla_softmax,
                    11: lambda: (act_copy_half(probT), scaled(pcT[0:NCMP, 0, :], st[0:NCMP, 1536:2048], 1.0),
                                 biased_features(1, sb_kT, 4)),
                    12: sb_softplus,
                    13: lambda: act.activation(prob[:, :], st[:, 0:1536], ACT.Exp),
                    15: lambda: act_softmax(place, "sel", prob),
                    16: lambda: act_copy_half(pT_sel),
                    17: lambda: (act_softmax(place, "win", prob), biased_features(0, fox_kT, 12)),
                    18: lambda: act_copy_half(pT_win),
                    21: lambda: (act_softmax(place, "fox", prob), act_gate("nsa")),
                    22: lambda: act_copy_half(probT),
                    23: lambda: act_gate("sb"), 24: high("nsa", NSA_KT),
                    25: lambda: (high("sb", SB_KT)(), act_gate("fox")), 26: high("fox", FOX_KT),
                    27: lambda: act_gate("mla"), 28: high("mla", MLA_KT),
                    29: lambda: output_squares(0), 31: lambda: output_squares(1), 33: lambda: output_squares(2),
                    35: lambda: output_squares(3),
                })

            place = after(0, 0)
            act_norm(place, "first2", xn2, TB * LAYERS)
            for n, unit in enumerate(SLOTS_2[0]):
                split_high(place, n, unit)
            act_operand(place, "first2", LAYERS + 1)

            def squares(pair, n):
                act.activation(tmp2[:, :, 0:n], acc[pair][:, :, 0:n], ACT.Square)

            def head_squares(name, pair, n):
                squares(pair, n)
                act.drain().then_inc(s(name + "_squares"), 1)

            def turned_scaled(dst, gain):
                act.activation(dst, st[:, 0:dst.free_size()], ACT.Copy, scale=gain)

            def softmax(name, sink=False):
                act_softmax(place, name, prob2)
                if sink:
                    act.activation(sink_e, sink_e, ACT.Exp).then_inc(s(name + "_sink"), 1)

            def conv_gate_sigmoid():
                act.activation(tmp2[:, :, :], acc[1], ACT.Sigmoid).then_inc(s("b_gate2"), 1)

            def conv_input():
                act.activation(conv_h[:, :, PAD:PAD + T], st[:, 0:1024].rearrange("p (c t) -> p c t", c=4), ACT.Copy)\
                    .then_inc(s("conv_h2"), 1)

            def conv_square():
                act.wait_ge(s("conv_centred2"), 1)
                act.activation(conv_sq[:, :, :], conv_y[:, :, :], ACT.Square)

            def conv_rstd():
                act.wait_ge(s("conv_sumsq2"), 1)
                act_rstd(conv_stat[:, 2, :], conv_stat[:, 1, :], 512)

            def conv_silu():
                for ct in range(4):
                    act.activation(conv_sq[:, ct, :], conv_y[:, ct, :], ACT.Silu, scale=ln_g[:, ct:ct + 1],
                                   bias=ln_b[:, ct:ct + 1])

            def conv_high():
                act.activation(mh2[:, 4:8, :], conv_sq[:, :, :], ACT.Copy).then_inc(s("conv_high2"), 1)

            def flat(t):
                return t.rearrange("p a b -> p (a b)")
            slots_with_mids(place, SLOTS_2, {
                1: lambda: (head_squares("ck2", 0, 128),
                            act.activation(flat(conv_wT[:, :, :]), st[:, 1536:1536 + 4 * TAPS], ACT.Copy)),
                2: lambda: turned_scaled(flat(ckT[:, :, :]), gk_c),
                3: lambda: head_squares("cq02", 1, 512),
                4: lambda: turned_scaled(flat(cqT[:, :, :]), gq_c),
                5: lambda: softmax("c00", True), 6: lambda: act_copy_half(probT2),
                7: lambda: (conv_gate_sigmoid(), softmax("c04", True)),
                8: lambda: act_copy_half(probT2),
                9: lambda: (head_squares("cq12", 0, 512), conv_input()),
                10: lambda: (act_mix_high(place, "c0", mh2, 8, 2), turned_scaled(flat(cqT[:, :, :]), gq_c)),
                11: lambda: (head_squares("aq2", 1, 512), softmax("c10", True)),
                12: lambda: act_copy_half(probT2),
                13: lambda: (head_squares("ak2", 0, 512), softmax("c14", True)),
                14: lambda: act_copy_half(probT2),
                15: lambda: turned_scaled(flat(aqT[:, :, :]), gq_a),
                16: lambda: (act_mix_high(place, "c1", mh2, 12, 2), turned_scaled(flat(akT[:, :, :]), gk_a)),
                17: lambda: (softmax("a0"), conv_square()),
                18: lambda: (act_copy_half(probT2), conv_rstd()),
                19: lambda: softmax("a4"), 20: lambda: (act_copy_half(probT2), conv_silu()), 21: conv_high,
                22: lambda: act_mix_high(place, "a", mh2, 0, 0),
            })

            act_norm(place, "second3", xn3, TB * (LAYERS + 1))
            units = gate_up_units()
            for n in range(SLOT_UNITS):
                split_high(ffn_place(0), n, units[n])
            act_operand(place, "second3", LAYERS + 2)

            def act_turned(i):
                act.activation(flat(ah[:, :, :])[:, bass.ds((i - 1) * 1024, 1024)], st[:, 0:1024], ACT.Copy)\
                    .then_inc(ffn_high, 1)

            def gate_part():
                act.activation(flat(silu[:, :, :]), accf[0], ACT.Silu)

            def ffn_step(i, first):
                pl = ffn_place(i)
                for n, unit in enumerate(units):
                    if not (first and n < SLOT_UNITS):
                        split_high(pl, n, unit)
                    if n == 3 and not first:
                        act_mid(pl, -1, nothing)
                    elif n == 7:
                        act_mid(pl, 0, nothing if first else lambda: act_turned(i))
                    elif n == 11:
                        act_mid(pl, 1, gate_part)
            ffn_step(0, True)
            with act.Fori(1, FFN_STEPS) as i:
                ffn_step(i, False)
            act_mid(ffn_place(FFN_STEPS), -1, nothing)
            act_mid(ffn_place(FFN_STEPS), 0, lambda: act_turned(FFN_STEPS))
            with act.Fori(0, 2) as i:
                pl = down_place(i)
                for n, unit in enumerate(down_units(0) + down_units(1)):
                    split_high(pl, n, unit)
                    if n == DOWN_UNITS + SLOT_UNITS - 1:
                        act_mid(pl, 0, nothing)
                act_mid(pl, 1, nothing)

        @block.vector
        def _(dve):
            def tt(out_, in0, in1, op):
                return dve.tensor_tensor(out=out_, in0=in0, in1=in1, op=op)

            def flat(t):
                return t.rearrange("p a b -> p (a b)")

            dve.sem_inc(lo_done, RAW_SLOTS)
            dve.sem_inc(dve_mid_done, 1)
            dve.memset(one, 1.0)
            dve.memset(minus_one, -1.0)
            dve.memset(eps, EPS)
            dve.memset(minus_half, -0.5)
            dve.drain()
            for tb in range(TB):
                dve.wait_ge(x_loaded[tb], 16)
                dve.sem_inc(x_ready, 1)

            def slots_with_mids(place, slots, mids):
                n = len(slots[0])
                for h in range(1, len(slots)):
                    for unit in slots[h]:
                        split_low(place, n, unit)
                        n += 1
                    dve_mid(place, h - 1, mids.get(h - 1, nothing))
                dve_mid(place, len(slots) - 1, mids.get(len(slots) - 1, nothing))

            with dve.Fori(0, LAYERS) as l:
                place = in_layer(l)
                dve_norm(place, "pre", xn)
                for n, unit in enumerate(LAYER_SLOTS[0]):
                    split_low(place, n, unit)
                dve_operand(place, "pre", place.once)
                bias_after = {}
                total = 0
                for i, g in enumerate(BIAS_GROUPS):
                    total += BIAS_DMAS[i]
                    bias_after[g] = total

                def biased(g, parts):
                    dve.wait_ge(bias_loaded, 16 * ((place.once - 1) * BIAS_TOTAL + bias_after[g]))
                    dve_evacuate_biased(g % 2, parts)

                def latents():
                    dve.wait_ge(consts_loaded, 16 * N_CONSTS)
                    dve.wait_ge(masks_loaded, 16 * POOL_CONSTS)
                    biased(0, [(0, 512, c[:, :, :])])
                    dve.drain().then_inc(s("latents"), 1)
                    dve.wait_ge(s("mla_rstd"), place.once)
                    for tb in range(TB):
                        for i, (a, b) in enumerate(((0, 384), (384, 512))):
                            dve.tensor_scalar(out=c[:, tb, a:b], in0=c[:, tb, a:b],
                                              scalar1=rstd[:, 2 * tb + i:2 * tb + i + 1], scalar2=None, op0=ALU.mult)

                def keys_and_compressed_tokens():
                    dve.tensor_copy(flat(knT[:, :, :]), st[:, 1024:2048])
                    biased(1, [(0, 256, cmp_tok[:, :, :, :].rearrange("p b i c -> p b (i c)")),
                               (256, 128, rope_in[:, :, 4, :]), (384, 128, v_sel[:, :, :])])

                def compressed_blocks():
                    dve.tensor_copy(rope_in_m[:, :, 0:4, :].rearrange("p b h c -> p b (h c)"),
                                    st[:, 1024:1536].rearrange("p (b n) -> p b n", b=TB))
                    for i in range(2):
                        tok = st[:, 1536 + i * T:1536 + (i + 1) * T].rearrange("p (m b) -> p b m", b=CMP_STRIDE)
                        for a in range(2):
                            j = slice(a * CMP_STRIDE, (a + 1) * CMP_STRIDE)
                            tt(cmp_blk[:, i, j, :], tok[:, :, a:a + NCMP], bc(posT[:, i, j], NCMP), ALU.add)

                def nsa_queries():
                    biased(2, [(0, 512, rope_in[:, :, 0:4, :].rearrange("p b h c -> p b (h c)"))])

                def compressed_keys():
                    dve.tensor_copy(kc[0:NCMP, 0, :], st[0:NCMP, 1536:1536 + HD])
                    dve.tensor_copy(v_cmp[0:NCMP, :], st[0:NCMP, 1536 + HD:1536 + 2 * HD])
                    dve.drain()
                    dve_rope(kc[0:NCMP, 0:1, :], kc[0:NCMP, 1:2, :], kc[0:NCMP, 2:3, :], cos_c[0:NCMP, :],
                             sin_c[0:NCMP, :, :], 1, 64)

                def small_group():
                    dve.tensor_copy(kcT[:, :], st[:, 1536:1536 + NCMP])
                    b2 = branch.rearrange("p (b n) -> p b n", b=TB)
                    u2 = fox_u.rearrange("p (b n) -> p b n", b=TB)
                    biased(3, [(0, 128, rope_in[:, :, 5, :]), (128, 128, v_win[:, :, :]), (256, 12, b2),
                               (268, 4, u2), (272, 64, rope_in_m[:, :, 4, :])])
                    dve.drain()
                    tt(u2, u2, over(forget_b, TB), ALU.add)
                    dve.drain().then_inc(s("small_group"), 1)
                    for tb in range(TB):
                        tmp = qrT[:, 0:2, :].rearrange("p a t -> p (a t)")[:, 0:320].rearrange("p (h c) -> p h c", h=5)
                        dve_rope(rope_in_m[:, tb, :, :], rope_out_m[:, tb, :, :], tmp, cos_m[:, tb, :],
                                 sin_m[:, tb, :, :], 5, 32)
                    dve.wait_ge(s("small_nonlinear"), place.once)
                    dve.tensor_scalar(out=fox_u, in0=fox_u, scalar1=-1.0, scalar2=0.0, op0=ALU.mult, op1=ALU.max)
                    dve.drain()
                    tt(fox_sp, fox_sp, fox_u, ALU.add)
                    tt(gate_0.rearrange("p (b h) -> p b h", b=TB),
                       branch.rearrange("p (b h j) -> p b h j", b=TB, j=3)[:, :, :, 0], bc(row_ok, H), ALU.mult)

                def nsa_ropes():
                    dve.tensor_copy(qrT[0:64, 4, :], st[0:64, 1024:1280])
                    for tb in range(TB):
                        dve_rope(rope_in[:, tb, :, :], rope_out[:, tb, :, :], rope_tmp[:, :, :], cos_t[:, tb, :],
                                 sin_t[:, tb, :, :], 6, 64)

                def scaled_features(pair, dst, b0):
                    for h in range(H):
                        dve.tensor_scalar(out=dst[:, h, :], in0=accf[pair][:, h * T:(h + 1) * T],
                                          scalar1=col_bias[:, b0 + h:b0 + h + 1], scalar2=SCALE,
                                          op0=ALU.add, op1=ALU.mult)

                def nsa_turned():
                    dve.tensor_copy(flat(qkT[:, 4:6, :]), st[:, 1024:1536])
                    scaled_features(0, sb_qT, 0)

                def softmaxes_of_mla_and_compressed():
                    z = st[:, 1536:1536 + TB * H * NCMP].rearrange("p (a n) -> p a n", n=NCMP)
                    p = prob_c[:, :, :, :].rearrange("p b h n -> p (b h) n")
                    dve.tensor_reduce(out=cmp_max, in_=z, axis=AX, op=ALU.max)
                    dve.drain()
                    tt(p, z, bc(cmp_max, NCMP), ALU.subtract)
                    dve.drain().then_inc(s("cmp_shifted"), 1)
                    dve_softmax(place, "mla")
                    dve.wait_ge(s("cmp_exp"), place.once)
                    dve.tensor_reduce(out=cmp_den, in_=p, axis=AX, op=ALU.add)
                    dve.drain()
                    dve.reciprocal(cmp_den, cmp_den)
                    dve.drain()
                    tt(cmp_den, cmp_den, gate_0, ALU.mult)
                    dve.drain()
                    tt(p, p, bc(cmp_den, NCMP), ALU.mult)

                def sb_softplus():
                    dve.wait_ge(s("sb_softplus"), place.once)
                    dve.scalar_tensor_tensor(out=prob[:, :], in0=st[:, 0:1536], scalar=0.0, in1=prob[:, :],
                                             op0=ALU.max, op1=ALU.add)
                    dve.drain()
                    for tile in (prob[:, 0:1024].rearrange("p (h q) -> p h q", h=H)[:, :, 0:P],
                                 prob[:, 1024:1536].rearrange("p (h q) -> p h q", h=H)):
                        tt(tile, tile, over(keep_t_b[:, :], H), ALU.mult)

                def gate_probs(which):
                    f = factor.rearrange("p (b h) -> p b h", b=TB)
                    tt(f, f, branch.rearrange("p (b h j) -> p b h j", b=TB, j=3)[:, :, :, which], ALU.mult)
                    dve.drain()
                    p1 = prob[:, 0:1024].rearrange("p (h k) -> p h k", h=H)
                    p0 = prob[:, 1024:1536].rearrange("p (h k) -> p h k", h=H)
                    tt(p1, p1, bc(factor[:, 4:8], T), ALU.mult)
                    tt(p0, p0, bc(factor[:, 0:4], P), ALU.mult)

                def gate(name, g):
                    biased(g, [(0, 512, gate_z[:, :, :])])
                    dve.drain().then_inc(s(name + "_gate"), 1)
                    o = o_mix[name]
                    dve.wait_ge(s(name + "_gate_silu"), place.once)
                    tt(o[:, :, :], o[:, :, :], gate_silu[:, :, :], ALU.mult)

                def low(name, kt0):
                    dve_mix_low(place, name, mh, ml, kt0, 0)

                def output_group(g):
                    dve.wait_ge(s("y_squares"), 4 * (place.once - 1) + g + 1)
                    dve.wait_ge(post_g_loaded, 16 * place.once)
                    tt(y[:, :, g * GN:(g + 1) * GN], acc[g % 2], over(post_g[:, g * GN:(g + 1) * GN], TB), ALU.mult)

                def close_layer():
                    dve.wait_ge(s("y_squares"), 4 * place.once)
                    dve.tensor_reduce(out=sq_sums[:, 0:2], in_=den.rearrange("p (g b) -> p b g", b=TB), axis=AX,
                                      op=ALU.add)
                    dve.drain().then_inc(s("post_sums"), 1)
                    output_group(3)
                    dve.drain()
                    dve.wait_ge(s("post_rstd"), place.once)
                    for tb in range(TB):
                        dve.scalar_tensor_tensor(out=x[:, tb, :], in0=y[:, tb, :], scalar=rstd[:, tb:tb + 1],
                                                 in1=x[:, tb, :], op0=ALU.mult, op1=ALU.add).then_inc(x_ready, 1)

                slots_with_mids(place, LAYER_SLOTS, {
                    1: latents,
                    2: lambda: dve.tensor_copy(flat(posT[:, :, :]), st[:, 1024:1024 + 2 * CMP_LEN]),
                    3: keys_and_compressed_tokens, 4: compressed_blocks, 5: nsa_queries, 6: compressed_keys,
                    7: small_group, 8: nsa_ropes, 9: nsa_turned, 10: softmaxes_of_mla_and_compressed,
                    11: lambda: dve_copy_half(probT), 12: sb_softplus,
                    13: lambda: biased(6, [(0, 512, sb_v[:, :, :])]),
                    14: lambda: (dve.tensor_copy(flat(o_mix["sb"][:, :, :]), st[:, 0:1024]),
                                 dve_scaled_out(o_mix["mla"], st[:, 1024:2048])),
                    15: lambda: (dve_softmax(place, "sel"), gate_probs(1), scaled_features(1, fox_qT, 8)),
                    16: lambda: dve_copy_half(pT_sel),
                    17: lambda: (dve_softmax(place, "win"), gate_probs(2)),
                    18: lambda: dve_copy_half(pT_win),
                    19: lambda: (dve.tensor_copy(flat(o_mix["nsa"][:, :, :]), st[:, 0:1024]),
                                 biased(9, [(0, 512, fox_v[:, :, :])])),
                    21: lambda: (dve_softmax(place, "fox"), gate("nsa", 10)),
                    22: lambda: dve_copy_half(probT),
                    23: lambda: (dve_scaled_out(o_mix["fox"], st[:, 0:1024]), gate("sb", 11)),
                    24: lambda: low("nsa", NSA_KT), 25: lambda: (low("sb", SB_KT), gate("fox", 12)),
                    26: lambda: low("fox", FOX_KT), 27: lambda: gate("mla", 13), 28: lambda: low("mla", MLA_KT),
                    29: lambda: output_group(0), 31: lambda: output_group(1), 33: lambda: output_group(2),
                    35: close_layer,
                })

            place = after(0, 0)
            dve_norm(place, "first2", xn2)
            for n, unit in enumerate(SLOTS_2[0]):
                split_low(place, n, unit)
            dve_operand(place, "first2", LAYERS + 1)
            dve.memset(conv_h[:, :, 0:PAD], 0.0)
            taps_at = {9: 2, 10: 6, 11: 5, 12: 6, 13: 5, 14: 5, 15: 2}
            assert sum(taps_at.values()) == TAPS
            done = [0]

            def head_sums(name, n):
                m = TB * n // 64
                dve.wait_ge(s(name + "_squares"), 1)
                dve.tensor_reduce(out=sq_sums[:, 0:m].rearrange("p (b h) -> p b h", b=TB),
                                  in_=tmp2[:, :, 0:n].rearrange("p b (h c) -> p b h c", c=64), axis=AX, op=ALU.add)
                dve.drain().then_inc(s(name + "_sums"), 1)

            def head_scale(name, pair, n, dst):
                m = TB * n // 64
                dve.wait_ge(s(name + "_rstd"), 1)
                for tb in range(TB):
                    tt(dst(tb), acc[pair][:, tb, 0:n].rearrange("p (h c) -> p h c", c=64),
                       bc(rstd[:, tb * m // 2:(tb + 1) * m // 2], 64), ALU.mult)

            def kv_group():
                dve.wait_ge(block2_loads, 16 * BLOCK2_LOADS)
                dve.tensor_scalar(out=neg_sinks, in0=sinks, scalar1=-1.0, scalar2=None, op0=ALU.mult)
                for g in (gq_c, gq_a):
                    dve.tensor_scalar(out=g, in0=g, scalar1=SCALE2, scalar2=None, op0=ALU.mult)
                head_sums("ck2", 128)
                dve.tensor_copy(cv[:, :, :], acc[0][:, :, 128:256])
                head_scale("ck2", 0, 128, lambda tb: ckn[:, tb, :, 0:64])
                dve.drain()
                dve.tensor_copy(ckn[:, :, :, 64:128], ckn[:, :, :, 0:64])

            def split_heads(t):
                return lambda tb: t[:, tb, :].rearrange("p (h c) -> p h c", c=64)

            def sinks_max(name, first):
                dve.tensor_reduce(out=neg_max[:, 4:8], in_=scores_1, axis=AX, op=ALU.max, negate=True)
                dve.tensor_reduce(out=neg_max[:, 0:4], in_=scores_0, axis=AX, op=ALU.max, negate=True)
                dve.drain()
                m = neg_max.rearrange("p (b h) -> p b h", b=TB)
                tt(m, m, over(neg_sinks[:, first:first + 4], TB), ALU.min)
                dve.drain()
                tt(sink_e.rearrange("p (b h) -> p b h", b=TB), m, over(sinks[:, first:first + 4], TB), ALU.add)
                dve.drain().then_inc(s(name + "_max"), 1)

            def sinks_sum(name):
                dve.wait_ge(s(name + "_exp"), 1)
                dve.wait_ge(s(name + "_sink"), 1)
                tt(den, den, sink_e, ALU.add)
                dve.drain()
                dve.reciprocal(factor, den)

            def small_out(o, first):
                for tb in range(TB):
                    tt(o[:, tb, first * 64:(first + 4) * 64].rearrange("p (h c) -> p h c", c=64),
                       st[:, 1536 + tb * 256:1536 + (tb + 1) * 256].rearrange("p (h c) -> p h c", c=64),
                       bc(factor[:, 4 * tb:4 * tb + 4], 64), ALU.mult)
                dve.drain()

            def dve_taps(h):
                dve.wait_ge(s("conv_h2"), 1)
                conv_taps(dve, DVE_TILES, done[0], done[0] + taps_at[h])
                done[0] += taps_at[h]

            def conv_gate():
                dve.wait_ge(s("b_gate2"), 1)
                tt(u[:, :, :], u[:, :, :], tmp2[:, :, :], ALU.mult)
                dve.drain()

            def conv_centre():
                tt(conv_y[:, :, :], conv_y[:, :, :], over(conv_stat[:, 0, :], 4), ALU.subtract)
                dve.drain().then_inc(s("conv_centred2"), 1)

            def conv_mean_and_scores():
                softmax_max("a0")
                dve.tensor_scalar(out=conv_stat[:, 0, :], in0=st[:, 1536:1536 + T], scalar1=1.0 / 512,
                                  scalar2=None, op0=ALU.mult)
                dve.drain()
                conv_centre()
                softmax_sum("a0")

            def conv_sumsq():
                dve.tensor_copy(conv_stat[:, 1, :], st[:, 1536:1536 + T])
                dve.drain().then_inc(s("conv_sumsq2"), 1)

            def conv_normalise():
                dve_refine_rstd(conv_stat[:, 2, :], conv_stat[:, 1, :], conv_stat[:, 0, :], 512)
                tt(conv_y[:, :, :], conv_y[:, :, :], over(conv_stat[:, 2, :], 4), ALU.mult)

            def conv_low():
                dve.wait_ge(s("conv_high2"), 1)
                tt(ml2[:, 4:8, :], conv_sq[:, :, :], mh2[:, 4:8, :].bitcast(F32), ALU.subtract)

            def softmax_max(name):
                dve_softmax_max(place, name)

            def softmax_sum(name):
                dve_softmax_sum(place, name)

            def add_output(*groups):
                for g in groups:
                    cols_ = slice(g * GN, (g + 1) * GN)
                    tt(x[:, :, cols_], acc[g % 2], x[:, :, cols_], ALU.add)

            def last_output():
                for tb in range(TB):
                    tt(x[:, tb, 3 * GN:], acc[1][:, tb, :], x[:, tb, 3 * GN:], ALU.add).then_inc(x_ready, 1)

            slots_with_mids(place, SLOTS_2, {
                1: kv_group,
                3: lambda: (head_sums("cq02", 512), head_scale("cq02", 1, 512, split_heads(cqn))),
                5: lambda: (sinks_max("c00", 0), dve.tensor_copy(u[:, :, :], acc[0]), sinks_sum("c00")),
                6: lambda: dve_copy_half(probT2),
                7: lambda: (sinks_max("c04", 4), small_out(o_c[0], 0), conv_gate(), sinks_sum("c04")),
                8: lambda: dve_copy_half(probT2),
                9: lambda: (head_sums("cq12", 512), small_out(o_c[0], 4), dve_taps(9),
                            head_scale("cq12", 0, 512, split_heads(cqn))),
                10: lambda: (dve_mix_low(place, "c0", mh2, ml2, 8, 2), dve_taps(10)),
                11: lambda: (head_sums("aq2", 512), sinks_max("c10", 8), dve_taps(11),
                             head_scale("aq2", 1, 512, split_heads(aqn)), sinks_sum("c10")),
                12: lambda: (dve_copy_half(probT2), dve_taps(12)),
                13: lambda: (head_sums("ak2", 512), sinks_max("c14", 12), small_out(o_c[1], 0), dve_taps(13),
                             head_scale("ak2", 0, 512, split_heads(akn)), sinks_sum("c14")),
                14: lambda: (dve_copy_half(probT2), dve_taps(14)),
                15: lambda: (small_out(o_c[1], 4), dve.tensor_copy(av[:, :, :], acc[1]), dve_taps(15)),
                16: lambda: dve_mix_low(place, "c1", mh2, ml2, 12, 2),
                17: conv_mean_and_scores,
                18: lambda: (conv_sumsq(), dve_copy_half(probT2)),
                19: lambda: (softmax_max("a4"), small_out(o_a, 0), conv_normalise(), softmax_sum("a4")),
                20: lambda: dve_copy_half(probT2), 21: lambda: (small_out(o_a, 4), conv_low()),
                22: lambda: dve_mix_low(place, "a", mh2, ml2, 0, 0),
                23: lambda: add_output(0), 24: lambda: add_output(1), 26: lambda: add_output(2), 28: last_output,
            })

            dve_norm(place, "second3", xn3)
            units = gate_up_units()
            for n in range(SLOT_UNITS):
                split_low(ffn_place(0), n, units[n])
            dve_operand(place, "second3", LAYERS + 2)

            def act_low(i):
                dve.wait_ge(ffn_high, i)
                part = bass.ds((i - 1) * 1024, 1024)
                tt(flat(al[:, :, :])[:, part], st[:, 0:1024], flat(ah[:, :, :])[:, part].bitcast(F32), ALU.subtract)

            def up_part():
                tt(act_a[:, :, :], silu[:, :, :], acc[1], ALU.mult)

            def ffn_step(i, first):
                pl = ffn_place(i)
                for n, unit in enumerate(units):
                    if not (first and n < SLOT_UNITS):
                        split_low(pl, n, unit)
                    if n == 3 and not first:
                        dve_mid(pl, -1, up_part)
                    elif n == 7:
                        dve_mid(pl, 0, nothing if first else lambda: act_low(i))
                    elif n == 11:
                        dve_mid(pl, 1, nothing)
            ffn_step(0, True)
            with dve.Fori(1, FFN_STEPS) as i:
                ffn_step(i, False)
            dve_mid(ffn_place(FFN_STEPS), -1, up_part)
            dve_mid(ffn_place(FFN_STEPS), 0, lambda: act_low(FFN_STEPS))

            def down_out(i, g):
                part = bass.ds(i * (2 * GN) + g * GN, GN)
                tt(x[:, :, part], acc[g], x[:, :, part], ALU.add)
            with dve.Fori(0, 2) as i:
                pl = down_place(i)
                for n, unit in enumerate(down_units(0) + down_units(1)):
                    split_low(pl, n, unit)
                    if n == DOWN_UNITS + SLOT_UNITS - 1:
                        dve_mid(pl, 0, lambda: down_out(i, 0))
                dve_mid(pl, 1, lambda: down_out(i, 1))


def constants():
    bf16 = mybir.dt.np(BF16)
    i, j = np.arange(P)[:, None], np.arange(P)[None, :]

    def rope(pos, half):
        inv = (np.float32(10000.0) ** (-np.arange(half, dtype=np.float32) / np.float32(half))).astype(np.float32)
        ang = pos.astype(np.float32)[:, None] * inv[None, :]
        co, si = np.cos(ang).astype(np.float32), np.sin(ang).astype(np.float32)
        return co, np.stack([-si, si], axis=1)

    def by_block(a):
        return np.ascontiguousarray(a.reshape(TB, P, *a.shape[1:]).swapaxes(0, 1))
    co, si = rope(np.arange(T), 64)
    com, sim = rope(np.arange(T), 32)
    ends = np.arange(NCMP) * CMP_STRIDE + CMP_LEN - 1
    coc, sic = rope(ends, 64)
    q = np.arange(T)
    cmp_mask = np.where(ends[None, :] <= q[:, None], 0.0, NEG)
    row_ok_ = (q >= ends[0]).astype(np.float32)
    dist1, dist0 = P + i - np.arange(T)[None, :], i - j
    dist = np.concatenate([dist1, dist0], axis=1)
    count = (dist <= 128).astype(int) + (dist % 4 == 0) + (dist % 16 == 0)
    count = np.where(dist >= 0, count, 0)
    return {
        "c_ident": np.eye(P, dtype=np.float32), "c_ident_b": np.eye(P).astype(bf16),
        "c_tri_up": (i <= j).astype(np.float32), "c_neg_tri": -(i >= j).astype(np.float32),
        "c_causal_b": np.where(j > i, NEG, 0.0).astype(bf16), "c_strict_t_b": np.where(i >= j, NEG, 0.0).astype(bf16),
        "c_keep_t_b": (i < j).astype(bf16), "c_cos": by_block(co), "c_sin": by_block(si),
        "c_cos_m": by_block(com), "c_sin_m": by_block(sim), "c_row_ok": np.ascontiguousarray(row_ok_.reshape(TB, P).T),
        "c_cmp_mask_b": by_block(cmp_mask).reshape(P, TB * NCMP).astype(bf16), "c_cos_c": coc, "c_sin_c": sic,
        "c_mask_c": np.where((dist >= 0) & (dist <= 127), 0.0, NEG).astype(bf16),
        "c_log_count": np.where(count > 0, np.log(np.maximum(count, 1)), NEG).astype(np.float32),
    }


_INS = ["x", "pre_norm_g", "post_norm_g", "w_in", "b_in", "w_out", "fox_forget_bias", "nsa_cmp_pos_k", "nsa_cmp_w1_k",
        "nsa_cmp_w2_k", "nsa_cmp_pos_v", "nsa_cmp_w1_v", "nsa_cmp_w2_v", "mla_q_norm_g", "mla_w_uq", "mla_kv_norm_g",
        "mla_w_ukv", "norm1_g_2", "w_in_2", "a_q_g_2", "a_k_g_2", "conv_w_2", "conv_b_2", "conv_ln_g_2",
        "conv_ln_b_2", "c_q_g_2", "c_k_g_2", "c_sinks_2", "w_out_2", "norm2_g_2", "w_gate_2", "w_up_2", "w_down_2"]


def kernel(**inputs):
    import concourse.bacc as _bacc
    from concourse.bass_utils import run_bass_kernel_spmd as _run

    nc = _bacc.Bacc("TRN2", target_bir_lowering=False, num_devices=1)
    arrays, aps = {}, {}
    given = {name: np.ascontiguousarray(inputs[name]) for name in _INS}
    for name, a in {**given, **constants()}.items():
        arrays[f"in_{name}_dram"] = a
        aps[name] = nc.dram_tensor(f"in_{name}_dram", a.shape, mybir.dt.from_np(a.dtype), kind="ExternalInput").ap()
    out = nc.dram_tensor("out_0_dram", (1, T, DM), F32, kind="ExternalOutput").ap()
    build(nc, aps, out.rearrange("a t n -> (a t) n"))
    r = _run(nc, [arrays], core_ids=[0])
    return r.results[0]["out_0_dram"]
```
